# Optimizing a Trainium2 kernel written in Bass

```python
import jax, jax.numpy as jnp
from jax import lax
import numpy as np

D_MODEL = 1024
BATCH = 1
SEQ = 1024
DEPTH = 2

POOL_WIDTH = 512
POOL_WINDOWS = (2, 4, 8, 16)
POOL_GROUP = POOL_WIDTH // len(POOL_WINDOWS)
CONV_WIDTH = 512
CONV_K = 3
AB_IN = 2 * POOL_WIDTH + 4 * CONV_WIDTH
AB_MIX = POOL_WIDTH + CONV_WIDTH

MLA_HEADS = 16
QK_NOPE = 64
QK_ROPE = 32
V_HEAD = 64
Q_LORA = 768
KV_LORA = 256
QK_HEAD = QK_NOPE + QK_ROPE
MLA_WIDTH = MLA_HEADS * V_HEAD
C_IN = Q_LORA + KV_LORA + QK_ROPE + MLA_WIDTH
ROPE_THETA = 10000.0
Q_BLOCK = 128
EPS = 1e-6

N_EVEN = (DEPTH + 1) // 2
N_ODD = DEPTH // 2

kernel_name = "hybrid_pool_shortconv_mla_trunk"

def rms_norm(x, g):
    xf = x.astype(jnp.float32)
    y = xf * lax.rsqrt(jnp.mean(xf * xf, axis=-1, keepdims=True) + EPS)
    return (y * g.astype(jnp.float32)).astype(x.dtype)

def pool_mixer(u, w, scale):
    B, S, _ = u.shape
    uf = u.astype(jnp.float32)
    cs = jnp.cumsum(uf, axis=1)
    t = jnp.arange(1, S + 1, dtype=jnp.float32)[None, :, None]
    diffs = []
    for g, win in enumerate(POOL_WINDOWS):
        sl = slice(g * POOL_GROUP, (g + 1) * POOL_GROUP)
        csg = cs[..., sl]
        lag = jnp.pad(csg, ((0, 0), (win, 0), (0, 0)))[:, :S]
        mean = (csg - lag) / jnp.minimum(t, float(win))
        diffs.append(mean - uf[..., sl])
    d = jnp.stack(diffs, axis=2).astype(u.dtype)
    y = jnp.einsum('bsgc,gcd->bsgd', d, w).reshape(B, S, POOL_WIDTH)
    return y * scale

def short_conv_mixer(h, b_gate, c_gate, w):
    S = h.shape[1]
    u = c_gate * h
    up = jnp.pad(u, ((0, 0), (CONV_K - 1, 0), (0, 0)))
    conv = w[0] * up[:, 0:S]
    for k in range(1, CONV_K):
        conv = conv + w[k] * up[:, k:k + S]
    return b_gate * conv

def even_layer(x, norm_g, w_in, pool_w, pool_scale, conv_w, w_out):
    h = rms_norm(x, norm_g)
    proj = h @ w_in
    u_a, z_a, h_b, b_b, c_b, z_b = jnp.split(
        proj, [POOL_WIDTH, 2 * POOL_WIDTH, 2 * POOL_WIDTH + CONV_WIDTH,
               2 * POOL_WIDTH + 2 * CONV_WIDTH, 2 * POOL_WIDTH + 3 * CONV_WIDTH], axis=-1)
    y_a = pool_mixer(u_a, pool_w, pool_scale) * jax.nn.silu(z_a)
    y_b = short_conv_mixer(h_b, b_b, c_b, conv_w) * jax.nn.silu(z_b)
    return x + jnp.concatenate([y_a, y_b], axis=-1) @ w_out

def rope_tail(q, cos, sin):
    q_n, q_r = q[..., :QK_NOPE], q[..., QK_NOPE:]
    half = QK_ROPE // 2
    x1, x2 = q_r[..., :half], q_r[..., half:]
    c, s = cos[:, :, None, :], sin[:, :, None, :]
    rot = jnp.concatenate([x1 * c - x2 * s, x1 * s + x2 * c], axis=-1)
    return jnp.concatenate([q_n, rot.astype(q.dtype)], axis=-1)

def causal_attention(q, k, v):
    B, S, H, _ = q.shape
    n_blocks = S // Q_BLOCK
    k_idx = jnp.arange(S)
    scale = QK_HEAD ** -0.5

    def block(i):
        start = i * Q_BLOCK
        qb = lax.dynamic_slice_in_dim(q, start, Q_BLOCK, axis=1)
        s = jnp.einsum('bqhd,bkhd->bhqk', qb, k,
                       preferred_element_type=jnp.float32) * scale
        q_idx = start + jnp.arange(Q_BLOCK)
        s = jnp.where(k_idx[None, :] <= q_idx[:, None], s, -jnp.inf)
        p = jax.nn.softmax(s, axis=-1)
        return jnp.einsum('bhqk,bkhd->bqhd', p.astype(v.dtype), v)

    o = lax.map(block, jnp.arange(n_blocks))
    return o.transpose(1, 0, 2, 3, 4).reshape(B, S, H * V_HEAD)

def odd_layer(x, cos, sin, norm_g, w_in, q_lat_g, w_uq, kv_lat_g, w_ukv,
              q_head_g, k_head_g, w_out):
    B, S, _ = x.shape
    h = rms_norm(x, norm_g)
    c_q, c_kv, k_rope, z = jnp.split(
        h @ w_in, [Q_LORA, Q_LORA + KV_LORA, Q_LORA + KV_LORA + QK_ROPE], axis=-1)
    q = (rms_norm(c_q, q_lat_g) @ w_uq).reshape(B, S, MLA_HEADS, QK_HEAD)
    kv = (rms_norm(c_kv, kv_lat_g) @ w_ukv).reshape(B, S, MLA_HEADS, QK_NOPE + V_HEAD)
    k_nope, v = kv[..., :QK_NOPE], kv[..., QK_NOPE:]
    k = jnp.concatenate(
        [k_nope, jnp.broadcast_to(k_rope[:, :, None, :], (B, S, MLA_HEADS, QK_ROPE))], axis=-1)
    q = rope_tail(rms_norm(q, q_head_g), cos, sin)
    k = rope_tail(rms_norm(k, k_head_g), cos, sin)
    o = causal_attention(q, k, v)
    return x + (o * jax.nn.silu(z)) @ w_out

def setup_inputs(seed: int = 0) -> dict:
    key = jax.random.key(seed)
    ks = jax.random.split(key, 17)
    nrm = jax.random.normal
    f32 = jnp.float32
    x = nrm(ks[0], (BATCH, SEQ, D_MODEL), f32)
    offset = jax.random.randint(ks[1], (BATCH, 1), 0, 1024, dtype=jnp.int32)
    positions = (offset + jnp.arange(SEQ, dtype=jnp.int32)[None, :]).astype(jnp.int32)
    return {
        "x": x,
        "positions": positions,
        "norm_ab": 1.0 + 0.02 * nrm(ks[2], (N_EVEN, D_MODEL), f32),
        "w_in_ab": nrm(ks[3], (N_EVEN, D_MODEL, AB_IN), f32) * D_MODEL ** -0.5,
        "pool_w": nrm(ks[4], (N_EVEN, len(POOL_WINDOWS), POOL_GROUP, POOL_GROUP), f32) * POOL_GROUP ** -0.5,
        "pool_scale": 1.0 + 0.1 * nrm(ks[5], (N_EVEN, POOL_WIDTH), f32),
        "conv_w": nrm(ks[6], (N_EVEN, CONV_K, CONV_WIDTH), f32) * CONV_K ** -0.5,
        "w_out_ab": nrm(ks[7], (N_EVEN, AB_MIX, D_MODEL), f32) * AB_MIX ** -0.5,
        "norm_c": 1.0 + 0.02 * nrm(ks[8], (N_ODD, D_MODEL), f32),
        "w_in_c": nrm(ks[9], (N_ODD, D_MODEL, C_IN), f32) * D_MODEL ** -0.5,
        "q_lat_norm": 1.0 + 0.02 * nrm(ks[10], (N_ODD, Q_LORA), f32),
        "w_uq": nrm(ks[11], (N_ODD, Q_LORA, MLA_HEADS * QK_HEAD), f32) * Q_LORA ** -0.5,
        "kv_lat_norm": 1.0 + 0.02 * nrm(ks[12], (N_ODD, KV_LORA), f32),
        "w_ukv": nrm(ks[13], (N_ODD, KV_LORA, MLA_HEADS * (QK_NOPE + V_HEAD)), f32) * KV_LORA ** -0.5,
        "q_head_norm": 1.0 + 0.02 * nrm(ks[14], (N_ODD, QK_HEAD), f32),
        "k_head_norm": 1.0 + 0.02 * nrm(ks[15], (N_ODD, QK_HEAD), f32),
        "w_out_c": nrm(ks[16], (N_ODD, MLA_WIDTH, D_MODEL), f32) * MLA_WIDTH ** -0.5,
    }

def reference(x, positions, norm_ab, w_in_ab, pool_w, pool_scale, conv_w, w_out_ab,
              norm_c, w_in_c, q_lat_norm, w_uq, kv_lat_norm, w_ukv, q_head_norm,
              k_head_norm, w_out_c):
    inv_freq = ROPE_THETA ** (-jnp.arange(0, QK_ROPE, 2, dtype=jnp.float32) / QK_ROPE)
    ang = positions.astype(jnp.float32)[..., None] * inv_freq
    cos, sin = jnp.cos(ang), jnp.sin(ang)
    for layer in range(DEPTH):
        i = layer // 2
        if layer % 2 == 0:
            x = even_layer(x, norm_ab[i], w_in_ab[i], pool_w[i], pool_scale[i],
                           conv_w[i], w_out_ab[i])
        else:
            x = odd_layer(x, cos, sin, norm_c[i], w_in_c[i], q_lat_norm[i], w_uq[i],
                          kv_lat_norm[i], w_ukv[i], q_head_norm[i], k_head_norm[i],
                          w_out_c[i])
    return x


_drawn_inputs = setup_inputs


def setup_inputs(seed=0):
    import zlib

    import numpy as np

    out = dict(_drawn_inputs(seed))
    spreads = {}
    factors = {'norm_ab': 3.122,
     'norm_c': 8.0,
     'q_lat_norm': 8.0,
     'kv_lat_norm': 8.0,
     'q_head_norm': 8.0,
     'k_head_norm': 8.0}
    for name, (base, spread) in spreads.items():
        noise = np.random.default_rng([zlib.crc32(name.encode()), seed]).standard_normal(out[name].shape)
        drawn = base * np.exp(spread * noise) if base else spread * noise
        out[name] = __import__('jax').numpy.asarray(drawn.astype(out[name].dtype))
    for name, factor in factors.items():
        out[name] = (out[name] * factor).astype(out[name].dtype)
    return out
```

```python
from contextlib import ExitStack

import concourse.bass as bass
import numpy as np
from concourse import mybir

F32 = mybir.dt.float32
F32R = mybir.dt.float32r
I32 = mybir.dt.int32
ACT = mybir.ActivationFunctionType
ALU = mybir.AluOpType
AX_X = mybir.AxisListType.X

P = 128
BANK = 512
S = 1024
D = 1024
NT = S // P
NK = D // P
WINDOWS = (2, 4, 8, 16)
GROUPS = len(WINDOWS)
MIX = 512
AB_IN = 6 * MIX
CONV_K = 3
HEADS, NOPE, ROPE, VH = 16, 64, 32, 64
QKH = NOPE + ROPE
HALF = ROPE // 2
Q_LORA, KV_LORA = 768, 256
KQ, KKV = Q_LORA // P, KV_LORA // P
Q_COLS = HEADS * QKH
KV_COLS = HEADS * (NOPE + VH)
Z_COL = Q_LORA + KV_LORA + ROPE
C_IN = Z_COL + HEADS * VH
THETA = 10000.0
EPS = 1e-6
SCALE = float(QKH) ** -0.5
MASKED = -1e30
PAIRS = HEADS // 2


def f32(ap):
    return ap.bitcast(F32)


class Chain:

    def __init__(self, eng, sem, base=0):
        self.eng, self.sem, self.base, self.n = eng, sem, base, 0

    def __call__(self, ins):
        self.n += 1
        ins.then_inc(self.sem, 1)
        self.eng.wait_ge(self.sem, self.base + self.n)


RSQRT_STEPS = 10


def rsqrt(nc, link, y, t, x):
    link(nc.vector.tensor_scalar(y.bitcast(I32), x.bitcast(I32), -0.5, float(0x5F3759DF), ALU.mult, ALU.add))
    for _ in range(3):
        link(nc.vector.tensor_tensor(t, y, y, ALU.mult))
        link(nc.vector.scalar_tensor_tensor(t, t, -0.5, x, ALU.mult, ALU.mult))
        link(nc.vector.scalar_tensor_tensor(y, t, 1.5, y, ALU.add, ALU.mult))


def three_passes(nc, out, w_hi, w_lo, a_hi, a_lo, first, last):
    nc.tensor.matmul(out, w_hi, a_hi, start=first, stop=False)
    nc.tensor.matmul(out, w_hi, a_lo, start=False, stop=False)
    return nc.tensor.matmul(out, w_lo, a_hi, start=False, stop=last)


def phase(nc, name):
    ctx = ExitStack()

    def sb(n, shape, dt=F32):
        return ctx.enter_context(nc.sbuf_tensor(f"{name}_{n}", shape, dt))

    def ps(n, shape):
        return ctx.enter_context(nc.psum_tensor(f"{name}_{n}", shape, F32))

    def sem(n):
        return ctx.enter_context(nc.semaphore(f"{name}_{n}"))

    return ctx, sb, ps, sem


def constants(nc, ident, mask):
    ctx, sb, ps, sem = phase(nc, "const")
    with ctx:
        filled, shaped = sem("filled"), sem("shaped")
        with nc.Block() as block:

            @block.vector
            def _(dve):
                nc.vector.memset(ident[:], 0.0).then_inc(filled, 1)
                nc.vector.memset(mask[:], 0.0).then_inc(filled, 1)

            @block.gpsimd
            def _(pool):
                pool.wait_ge(filled, 2)
                nc.gpsimd.affine_select(out=ident[:], in_=ident[:], compare_op=ALU.not_equal, fill=1.0,
                                        base=0, pattern=[[-1, P]], channel_multiplier=1).then_inc(shaped, 1)
                tri = mask[:, S - P:S]
                nc.gpsimd.affine_select(out=tri, in_=tri, compare_op=ALU.is_ge, fill=MASKED,
                                        base=0, pattern=[[-1, P]], channel_multiplier=1).then_inc(shaped, 1)
                pool.wait_ge(shaped, 2)


def normalise_and_transpose(nc, name, x_sb, x_dram, gamma, ident, act_hi, act_lo):
    ctx, sb, ps, sem = phase(nc, name)
    with ctx:
        gam = sb("gamma", [P, D])
        junk = sb("squares", [P, D])
        ss = sb("ss", [P, NT])
        ms = sb("ms", [P, NT])
        rstd = sb("rstd", [P, NT])
        tmp = sb("tmp", [P, NT])
        xn = sb("xn", [P, 2, D])
        tp = ps("tp", [P, 2, NK, P])
        gamma_in = sem("gamma_in")
        x_in = [sem(f"x_in{t}") for t in range(NT)]
        squared, scalars, normed = sem("squared"), sem("scalars"), sem("normed")
        turned, hi_done, lo_done = sem("turned"), sem("hi_done"), sem("lo_done")
        with nc.Block() as block:

            @block.sync
            def _(sp):
                if x_dram is not None:
                    for t in range(NT):
                        sp.dma_start(x_sb[:, t, :], x_dram[t * P:(t + 1) * P, :]).then_inc(x_in[t], 16)

            @block.scalar
            def _(act):
                act.dma_start(gam[:], gamma.to_broadcast([P, D])).then_inc(gamma_in, 16)
                for t in range(NT):
                    if x_dram is not None:
                        act.wait_ge(x_in[t], 16)
                    if t:
                        act.wait_ge(squared, t)
                    nc.scalar.activation(junk[:], x_sb[:, t, :], ACT.Square,
                                         accum_out=ss[:, t:t + 1]).then_inc(squared, 1)
                with act.Fori(0, NT // 2) as i:
                    for e in range(2):
                        t = 2 * i + e
                        act.wait_ge(turned, t + 1)
                        nc.scalar.activation(act_hi[:, :, bass.ds(t * P, P)], tp[:, e],
                                             ACT.Copy).then_inc(hi_done, 1)

            @block.vector
            def _(dve):
                link = Chain(dve, scalars)
                dve.wait_ge(squared, NT)
                link(nc.vector.tensor_scalar(ms[:], ss[:], 1.0 / D, EPS, ALU.mult, ALU.add))
                rsqrt(nc, link, rstd[:], tmp[:], ms[:])
                dve.wait_ge(gamma_in, 16)

                def norm(t, e):
                    nc.vector.scalar_tensor_tensor(xn[:, e], x_sb[:, t, :], rstd[:, t:t + 1], gam[:],
                                                   ALU.mult, ALU.mult).then_inc(normed, 1)

                def low(t, e):
                    dve.wait_ge(hi_done, t + 1)
                    cols = slice(t * P, (t + 1) * P)
                    nc.vector.tensor_tensor(act_lo[:, :, cols], tp[:, e], f32(act_hi[:, :, cols]),
                                            ALU.subtract).then_inc(lo_done, 1)

                dve.sem_inc(lo_done, 2)
                norm(0, 0)
                norm(1, 1)
                for t in range(NT):
                    low(t, t % 2)
                    if t + 2 < NT:
                        norm(t + 2, t % 2)

            @block.tensor
            def _(pe):
                with pe.Fori(0, NT // 2) as i:
                    for e in range(2):
                        t = 2 * i + e
                        pe.wait_ge(normed, t + 1)
                        pe.wait_ge(lo_done, t + 1)
                        for k in range(NK):
                            last = nc.tensor.transpose(tp[:, e, k], xn[:, e, k * P:(k + 1) * P], ident[:])
                        last.then_inc(turned, 1)


def mixers(nc, w_in, pool_w, pool_scale, conv_w, act_hi, act_lo, y):
    ctx, sb, ps, sem = phase(nc, "mix")
    with ctx:
        w = sb("w", [P, 2, NK, P])
        w_hi = sb("w_hi", [P, 2, NK, P], F32R)
        w_lo = sb("w_lo", [P, 2, NK, P], F32R)
        pw = sb("pw", [P, GROUPS, P])
        pw_hi = sb("pw_hi", [P, P], F32R)
        pw_lo = sb("pw_lo", [P, P], F32R)
        scl = sb("scl", [P, GROUPS])
        cw = sb("cw", [P, CONV_K, GROUPS])
        u = sb("u", [P, S])
        za = sb("za", [P, S])
        hb = sb("hb", [P, S])
        bb = sb("bb", [P, S])
        cb = sb("cb", [P, S])
        zb = sb("zb", [P, S])
        sums = sb("sums", [P, 2, S])
        d_hi = sb("d_hi", [P, S], F32R)
        d_lo = sb("d_lo", [P, S], F32R)
        count = sb("count", [P, max(WINDOWS)])
        inv = sb("inv", [P, max(WINDOWS)])
        head = sb("head", [P, max(WINDOWS)])
        proj = ps("proj", [P, 2, S])
        pooled = ps("pooled", [P, S])
        w_loaded = [sem("w_loaded0"), sem("w_loaded1")]
        small = [sem(f"small{n}") for n in range(3)]
        hi_done, lo_done, proj_ready, evacuated = sem("hi_done"), sem("lo_done"), sem("proj_ready"), sem("evacuated")
        counted, d_ready, pool_ready, mixed = sem("counted"), sem("d_ready"), sem("pool_ready"), sem("mixed")
        chain, pw_high, pw_done = sem("chain"), sem("pw_high"), sem("pw_done")
        N = 6 * GROUPS
        dest = [u, za, hb, bb, cb, zb]
        w_rows = w_in.rearrange("(k p) n -> p k n", p=P)
        with nc.Block() as block:

            @block.sync
            def _(sp):
                with sp.Fori(0, GROUPS) as g:
                    for j in range(6):
                        m = 6 * g + j
                        col = sp.snap(g * P + j * MIX)
                        sp.wait_ge(lo_done, m + 1)
                        sp.dma_start(w[:, j % 2], w_rows[:, :, bass.ds(col, P)]).then_inc(
                            w_loaded[j % 2], 16)

            @block.gpsimd
            def _(pool):
                nc.gpsimd.iota(count[:], pattern=[[1, max(WINDOWS)]], base=1, channel_multiplier=0,
                               allow_small_or_imprecise_dtypes=True).then_inc(counted, 1)

            @block.scalar
            def _(act):
                act.dma_start(pw[:], pool_w.rearrange("g c d -> c g d")).then_inc(small[0], 16)
                with nc.allow_non_contiguous_dma(reason="a few scalars per channel"):
                    act.dma_start(scl[:], pool_scale.rearrange("(g p) -> p g", p=P)).then_inc(small[1], 16)
                    act.dma_start(cw[:], conv_w.rearrange("k (g p) -> p k g", p=P)).then_inc(small[2], 16)

                def high(m):
                    act.wait_ge(w_loaded[m % 2], 16 * (m // 2 + 1))
                    act.wait_ge(proj_ready, m + 1)
                    nc.scalar.activation(w_hi[:, m % 2], w[:, m % 2], ACT.Copy).then_inc(hi_done, 1)

                act.sem_inc(evacuated, 2)
                high(0)
                act.wait_ge(small[0], 16)
                for m in range(N):
                    if m + 1 < N:
                        high(m + 1)
                    act.wait_ge(proj_ready, m + 3)
                    if m % 6 == 0:
                        act.wait_ge(mixed, m // 6 + 1)
                    nc.scalar.activation(dest[m % 6][:], proj[:, m % 2], ACT.Silu if m % 6 in (1, 5) else ACT.Copy
                                         ).then_inc(evacuated, 1)
                    if m % 6 == 0:
                        nc.scalar.activation(pw_hi[:], pw[:, m // 6], ACT.Copy).then_inc(pw_high, 1)

            @block.vector
            def _(dve):
                link = Chain(dve, chain)

                def low(m):
                    dve.wait_ge(hi_done, m + 1)
                    nc.vector.tensor_tensor(w_lo[:, m % 2], w[:, m % 2], f32(w_hi[:, m % 2]),
                                            ALU.subtract).then_inc(lo_done, 1)

                dve.sem_inc(lo_done, 2)
                dve.sem_inc(mixed, 1)
                low(0)
                dve.wait_ge(counted, 1)
                dve.wait_ge(small[1], 16)
                dve.wait_ge(small[2], 16)

                def pool_sums(g):
                    win = WINDOWS[g]
                    src, n = u, 0
                    step = 1
                    while step < win:
                        dst = sums[:, n % 2]
                        link(nc.vector.tensor_tensor(dst[:, step:], src[:, step:], src[:, :S - step], ALU.add))
                        link(nc.vector.tensor_copy(dst[:, :step], src[:, :step]))
                        src, n, step = dst, n + 1, 2 * step
                    link(nc.vector.tensor_scalar(head[:, :win], count[:, :win], float(win), None, ALU.min))
                    link(nc.vector.reciprocal(inv[:, :win], head[:, :win]))
                    link(nc.vector.tensor_tensor(head[:, :win], src[:, :win], inv[:, :win], ALU.mult))
                    other = sums[:, n % 2]
                    link(nc.vector.scalar_tensor_tensor(other[:, win:], src[:, win:], 1.0 / win, u[:, win:],
                                                        ALU.mult, ALU.subtract))
                    link(nc.vector.tensor_tensor(other[:, :win], head[:, :win], u[:, :win], ALU.subtract))
                    link(nc.vector.tensor_copy(d_hi[:], other))
                    nc.vector.tensor_tensor(d_lo[:], other, f32(d_hi[:]), ALU.subtract).then_inc(d_ready, 1)

                def conv(g):
                    ch, acc = sums[:, 0], sums[:, 1]
                    dve.wait_ge(d_ready, g + 1)
                    link(nc.vector.tensor_tensor(ch, cb[:], hb[:], ALU.mult))
                    link(nc.vector.tensor_scalar(acc, ch, cw[:, 2, g:g + 1], None, ALU.mult))
                    for k in (1, 0):
                        lag = CONV_K - 1 - k
                        link(nc.vector.scalar_tensor_tensor(acc[:, lag:], ch[:, :S - lag], cw[:, k, g:g + 1],
                                                            acc[:, lag:], ALU.mult, ALU.add))
                    link(nc.vector.tensor_tensor(acc, acc, bb[:], ALU.mult))
                    link(nc.vector.tensor_tensor(y[:, GROUPS + g, :], acc, zb[:], ALU.mult))

                for m in range(N):
                    if m + 1 < N:
                        low(m + 1)
                    g = m // 6
                    dve.wait_ge(evacuated, m + 3)
                    if m % 6 == 1:
                        dve.wait_ge(pw_high, g + 1)
                        nc.vector.tensor_tensor(pw_lo[:], pw[:, g], f32(pw_hi[:]), ALU.subtract).then_inc(pw_done, 1)
                        pool_sums(g)
                    if m % 6 == 5:
                        conv(g)
                        dve.wait_ge(pool_ready, g + 1)
                        nc.vector.scalar_tensor_tensor(y[:, g, :], pooled[:], scl[:, g:g + 1], za[:],
                                                       ALU.mult, ALU.mult).then_inc(mixed, 1)

            @block.tensor
            def _(pe):
                pe.sem_inc(proj_ready, 2)
                with pe.Fori(0, GROUPS) as g:
                    for j in range(6):
                        m = 6 * g + j
                        pe.wait_ge(lo_done, m + 3)
                        pe.wait_ge(evacuated, m + 1)
                        for c in range(2):
                            for k in range(NK):
                                cols = slice(c * BANK, (c + 1) * BANK)
                                last = three_passes(nc, proj[:, j % 2, cols], w_hi[:, j % 2, k], w_lo[:, j % 2, k],
                                                    act_hi[:, k, cols], act_lo[:, k, cols], k == 0, k == NK - 1)
                        last.then_inc(proj_ready, 1)
                    pe.wait_ge(pw_done, g + 1)
                    pe.wait_ge(d_ready, g + 1)
                    pe.wait_ge(mixed, g + 1)
                    for c in range(2):
                        cols = slice(c * BANK, (c + 1) * BANK)
                        last = three_passes(nc, pooled[:, cols], pw_hi[:], pw_lo[:],
                                            d_hi[:, cols], d_lo[:, cols], True, True)
                    last.then_inc(pool_ready, 1)


def output_projection(nc, name, w_out, features, res_dram, res, dest):
    ctx, sb, ps, sem = phase(nc, name)
    with ctx:
        w = sb("w", [P, 2, D])
        w_hi = sb("w_hi", [P, NK, D], F32R)
        w_lo = sb("w_lo", [P, NK, D], F32R)
        a_hi = sb("a_hi", [P, 2, NK, P], F32R)
        a_lo = sb("a_lo", [P, 2, NK, P], F32R)
        out = ps("out", [P, 2, D])
        w_in = [sem("w_in0"), sem("w_in1")]
        res_in = [sem(f"res_in{t}") for t in range(NT)]
        w_high, w_done, a_high, a_done = sem("w_high"), sem("w_done"), sem("a_high"), sem("a_done")
        projected, added = sem("projected"), sem("added")
        stored = [sem("stored0"), sem("stored1")]
        with nc.Block() as block:

            @block.sync
            def _(sp):
                for k in range(NK):
                    sp.wait_ge(w_done, k + 1)
                    sp.dma_start(w[:, k % 2, :], w_out[k * P:(k + 1) * P, :]).then_inc(w_in[k % 2], 16)
                with sp.Fori(0, NT // 2) as i:
                    for e in range(2):
                        t = 2 * i + e
                        row, tile = sp.snap(t * P), sp.snap(t)
                        sp.wait_ge(added, t + 3)
                        sp.dma_start(dest[bass.ds(row, P), :], res[:, bass.ds(tile, 1), :]).then_inc(stored[e], 16)
                for e in range(2):
                    sp.wait_ge(stored[e], 16 * (NT // 2))

            @block.scalar
            def _(act):
                for t in range(NT):
                    act.dma_start(res[:, t, :], res_dram[t * P:(t + 1) * P, :]).then_inc(res_in[t], 16)

                def split_rows(k):
                    act.wait_ge(w_in[k % 2], 16 * (k // 2 + 1))
                    nc.scalar.activation(w_hi[:, k, :], w[:, k % 2, :], ACT.Copy).then_inc(w_high, 1)

                def split_features(t):
                    act.wait_ge(projected, t + 1)
                    nc.scalar.activation(a_hi[:, t % 2], features[:, :, t * P:(t + 1) * P],
                                         ACT.Copy).then_inc(a_high, 1)

                split_features(0)
                for k in range(NK):
                    split_rows(k)
                for t in range(1, NT):
                    split_features(t)

            @block.vector
            def _(dve):
                dve.sem_inc(w_done, 2)
                dve.sem_inc(added, 2)

                def low_features(t):
                    dve.wait_ge(a_high, t + 1)
                    nc.vector.tensor_tensor(a_lo[:, t % 2], features[:, :, t * P:(t + 1) * P],
                                            f32(a_hi[:, t % 2]), ALU.subtract).then_inc(a_done, 1)

                low_features(0)
                for k in range(NK):
                    dve.wait_ge(w_high, k + 1)
                    nc.vector.tensor_tensor(w_lo[:, k, :], w[:, k % 2, :], f32(w_hi[:, k, :]),
                                            ALU.subtract).then_inc(w_done, 1)
                for t in range(NT):
                    if t + 1 < NT:
                        low_features(t + 1)
                    dve.wait_ge(res_in[t], 16)
                    dve.wait_ge(projected, t + 3)
                    nc.vector.tensor_tensor(res[:, t, :], out[:, t % 2, :], res[:, t, :],
                                            ALU.add).then_inc(added, 1)

            @block.tensor
            def _(pe):
                pe.sem_inc(projected, 2)
                with pe.Fori(0, NT // 2) as i:
                    for e in range(2):
                        t = 2 * i + e
                        pe.wait_ge(a_done, t + 1)
                        pe.wait_ge(added, t + 1)
                        for k in range(NK):
                            pe.wait_ge(w_done, k + 3)
                            for c in range(2):
                                cols = slice(c * BANK, (c + 1) * BANK)
                                last = three_passes(nc, out[:, e, cols], a_hi[:, e, k], a_lo[:, e, k],
                                                    w_hi[:, k, cols], w_lo[:, k, cols], k == 0, k == NK - 1)
                        last.then_inc(projected, 1)


def latent_projection(nc, w_in, positions, q_lat_g, kv_lat_g, q_head_g, k_head_g, ident, act_hi, act_lo,
                      latent, gate, rms_qkv, q_tab, k_rope, k_rope_ss):
    ctx, sb, ps, sem = phase(nc, "lat")
    with ctx:
        w = sb("w", [P, 2, NK, P])
        w_hi = sb("w_hi", [P, 2, NK, P], F32R)
        w_lo = sb("w_lo", [P, 2, NK, P], F32R)
        gam = sb("gam", [P, KQ + KKV])
        squares = sb("squares", [P, S])
        sq = sb("sq", [P, 2, S])
        krt = sb("krt", [P, S])
        ones = sb("ones", [P, 2])
        ms = sb("ms", [P, 2, NT])
        tmp = sb("tmp", [P, 2, NT])
        pos_i = sb("pos_i", [P, NT], I32)
        pos = sb("pos", [P, NT])
        freq = sb("freq", [P, HALF])
        head_g = sb("head_g", [P, 2, ROPE])
        ang = sb("ang", [P, NT, HALF])
        turns = sb("turns", [P, NT, HALF])
        red = sb("red", [P, 2, NT, HALF])
        trig = sb("trig", [P, 2, NT, HALF])
        kr = sb("kr", [P, NT, ROPE])
        ktab = sb("ktab", [P, 4, NT, HALF])
        prod = sb("prod", [P, 4, NT, HALF])
        kr2 = sb("kr2", [P, NT, ROPE])
        proj = ps("proj", [P, 2, S])
        small_ps = ps("small", [P, BANK])
        turned_ps = ps("turned", [P, NT, ROPE])
        w_loaded = [sem("w_loaded0"), sem("w_loaded1")]
        gam_in = [sem("gam_in0"), sem("gam_in1")]
        small_in = [sem(f"small_in{n}") for n in range(3)]
        hi_done, lo_done, proj_ready, evacuated = sem("hi_done"), sem("lo_done"), sem("proj_ready"), sem("evacuated")
        chain, freq_set, reduced, trig_done = sem("chain"), sem("freq_set"), sem("reduced"), sem("trig_done")
        squared, summed, ones_set, small_ready, kr_out = (
            sem("squared"), sem("summed"), sem("ones_set"), sem("small_ready"), sem("kr_out"))
        LAT = KQ + KKV
        N = LAT + 1 + NK
        w_rows = w_in.rearrange("(k p) n -> p k n", p=P)

        def load(sp, m, slot, col):
            sp.wait_ge(lo_done, m + 1)
            sp.dma_start(w[:, slot], w_rows[:, :, col]).then_inc(w_loaded[slot], 16)

        with nc.Block() as block:

            @block.sync
            def _(sp):
                with sp.Fori(0, LAT // 2) as i:
                    for e in range(2):
                        load(sp, 2 * i + e, e, bass.ds(sp.snap(i * 2 * P + e * P), P))
                load(sp, LAT, 0, slice(LAT * P, LAT * P + P))
                with sp.Fori(0, NK // 2) as i:
                    for e in range(2):
                        load(sp, 2 * i + LAT + 1 + e, 1 - e, bass.ds(sp.snap(i * 2 * P + Z_COL + e * P), P))

            @block.gpsimd
            def _(pool):
                for j in range(HALF):
                    f = float(np.float32(THETA ** (-2.0 * j / ROPE)))
                    nc.gpsimd.memset(freq[:, j:j + 1], f).then_inc(freq_set, 1)
                nc.gpsimd.memset(ones[:], 1.0).then_inc(ones_set, 1)
                for n, m in enumerate([1, 2, 3, 4, 5, 7]):
                    if n:
                        pool.wait_ge(summed, n)
                    pool.wait_ge(squared, m + 1)
                    total = sq[:, 0 if m < KQ else 1, :]
                    nc.gpsimd.tensor_tensor(total, total, squares[:], ALU.add).then_inc(summed, 1)

            @block.scalar
            def _(act):
                with nc.allow_non_contiguous_dma(reason="a few scalars per channel or token"):
                    act.dma_start(gam[:, :KQ], q_lat_g.rearrange("(k p) -> p k", p=P)).then_inc(gam_in[0], 16)
                    act.dma_start(gam[:, KQ:], kv_lat_g.rearrange("(k p) -> p k", p=P)).then_inc(gam_in[1], 16)
                    act.dma_start(pos_i[:], positions.rearrange("(t p) -> p t", p=P)).then_inc(small_in[0], 16)
                act.dma_start(head_g[:, 0], q_head_g[:, NOPE:].to_broadcast([P, ROPE])).then_inc(small_in[1], 16)
                act.dma_start(head_g[:, 1], k_head_g[:, NOPE:].to_broadcast([P, ROPE])).then_inc(small_in[2], 16)
                act.sem_inc(evacuated, 2)

                def high(m):
                    act.wait_ge(w_loaded[m % 2], 16 * (m // 2 + 1))
                    act.wait_ge(proj_ready, m + 1)
                    nc.scalar.activation(w_hi[:, m % 2], w[:, m % 2], ACT.Copy).then_inc(hi_done, 1)

                high(0)
                high(1)
                act.wait_ge(reduced, 2)
                nc.scalar.activation(trig[:], red[:], ACT.Sin).then_inc(trig_done, 1)
                act.wait_ge(gam_in[0], 16)
                act.wait_ge(gam_in[1], 16)
                for m in range(N):
                    if 1 <= m < N - 1:
                        high(m + 1)
                    act.wait_ge(proj_ready, m + 3)
                    src = proj[:, m % 2]
                    if m < LAT:
                        nc.scalar.activation(latent[:, m, :], src, ACT.Copy, scale=gam[:, m:m + 1])
                        if m in (0, KQ):
                            sq_dst = sq[:, 0 if m == 0 else 1, :]
                        else:
                            sq_dst = squares[:]
                            before = m - 1 if m < KQ else m - 2
                            if before:
                                act.wait_ge(summed, before)
                        nc.scalar.activation(sq_dst, src, ACT.Square).then_inc(squared, 1)
                        act.wait_ge(squared, m + 1)
                        act.sem_inc(evacuated, 1)
                    elif m == LAT:
                        nc.scalar.activation(krt[0:ROPE, :], src[0:ROPE, :], ACT.Copy).then_inc(evacuated, 1)
                    else:
                        nc.scalar.activation(gate[:, m - LAT - 1, :], src, ACT.Silu).then_inc(evacuated, 1)

            @block.vector
            def _(dve):
                link = Chain(dve, chain)

                def low(m):
                    dve.wait_ge(hi_done, m + 1)
                    nc.vector.tensor_tensor(w_lo[:, m % 2], w[:, m % 2], f32(w_hi[:, m % 2]),
                                            ALU.subtract).then_inc(lo_done, 1)

                def by_token(ap):
                    return ap.unsqueeze(1).to_broadcast([P, NT, HALF])

                dve.sem_inc(lo_done, 2)
                low(0)
                low(1)
                dve.wait_ge(small_in[0], 16)
                dve.wait_ge(freq_set, HALF)
                link(nc.vector.tensor_copy(pos[:], pos_i[:]))
                link(nc.vector.tensor_tensor(ang[:], pos[:].unsqueeze(2).to_broadcast([P, NT, HALF]),
                                             by_token(freq[:]), ALU.mult))
                for which, quarter in ((0, 0.0), (1, 0.25)):
                    r = red[:, which]
                    link(nc.vector.tensor_scalar(turns[:], ang[:], TURN, quarter, ALU.mult, ALU.add))
                    link(nc.vector.tensor_scalar(turns[:], turns[:], ROUND, ROUND, ALU.add, ALU.subtract))
                    link(nc.vector.scalar_tensor_tensor(r, turns[:], -TWO_PI[0], ang[:], ALU.mult, ALU.add))
                    for part in TWO_PI[1:]:
                        link(nc.vector.scalar_tensor_tensor(r, turns[:], -part, r, ALU.mult, ALU.add))
                    if which:
                        link(nc.vector.tensor_scalar(r, r, float(np.float32(np.pi / 2)), None, ALU.add))
                    link(nc.vector.tensor_scalar(r, r, PI, -PI, ALU.min, ALU.max))
                    dve.sem_inc(reduced, 1)
                dve.wait_ge(trig_done, 1)
                dve.wait_ge(small_in[1], 16)
                dve.wait_ge(small_in[2], 16)
                sin, cos = trig[:, 0], trig[:, 1]
                for which, tab in ((0, q_tab), (1, ktab)):
                    g1, g2 = head_g[:, which, :HALF], head_g[:, which, HALF:]
                    for n, (g, f) in enumerate(((g1, cos), (g2, sin), (g1, sin), (g2, cos))):
                        link(nc.vector.tensor_tensor(tab[:, n], f, by_token(g), ALU.mult))
                for m in range(2, N):
                    low(m)
                dve.wait_ge(small_ready, 1)
                for n, width in ((0, Q_LORA), (1, KV_LORA)):
                    link(nc.vector.tensor_scalar(ms[:, n], small_ps[:, n * NT:(n + 1) * NT], 1.0 / width, EPS,
                                                 ALU.mult, ALU.add))
                rsqrt(nc, link, rms_qkv[:], tmp[:], ms[:])
                link(nc.vector.tensor_copy(kr[:], turned_ps[:]))
                link(nc.vector.tensor_tensor(kr2[:], kr[:], kr[:], ALU.mult))
                link(nc.vector.tensor_reduce(k_rope_ss[:], kr2[:], AX_X, ALU.add))
                x1, x2 = kr[:, :, :HALF], kr[:, :, HALF:]
                for n, x in enumerate((x1, x2, x1, x2)):
                    link(nc.vector.tensor_tensor(prod[:, n], x, ktab[:, n], ALU.mult))
                link(nc.vector.tensor_tensor(k_rope[:, :, :HALF], prod[:, 0], prod[:, 1], ALU.subtract))
                link(nc.vector.tensor_tensor(k_rope[:, :, HALF:], prod[:, 2], prod[:, 3], ALU.add))

            @block.tensor
            def _(pe):
                def tile(m, slot):
                    pe.wait_ge(lo_done, m + 3)
                    pe.wait_ge(evacuated, m + 1)
                    for c in range(2):
                        for k in range(NK):
                            cols = slice(c * BANK, (c + 1) * BANK)
                            last = three_passes(nc, proj[:, slot, cols], w_hi[:, slot, k], w_lo[:, slot, k],
                                                act_hi[:, k, cols], act_lo[:, k, cols], k == 0, k == NK - 1)
                    last.then_inc(proj_ready, 1)

                pe.sem_inc(proj_ready, 2)
                with pe.Fori(0, LAT // 2) as i:
                    for e in range(2):
                        tile(2 * i + e, e)
                tile(LAT, 0)
                with pe.Fori(0, NK // 2) as i:
                    for e in range(2):
                        tile(2 * i + LAT + 1 + e, 1 - e)
                pe.wait_ge(ones_set, 1)
                pe.wait_ge(summed, LAT - 2)
                for n in range(2):
                    for t in range(NT):
                        col = n * NT + t
                        nc.tensor.matmul(small_ps[:, col:col + 1], sq[:, n, t * P:(t + 1) * P], ones[:, 0:1],
                                         start=True, stop=True)
                for t in range(NT):
                    last = nc.tensor.transpose(turned_ps[:, t], krt[0:ROPE, t * P:(t + 1) * P],
                                               ident[0:ROPE, 0:ROPE])
                last.then_inc(small_ready, 1)


TURN = float(np.float32(1.0 / (2.0 * np.pi)))
ROUND = float(1.5 * 2 ** 23)
PI = float(np.nextafter(np.float32(np.pi), np.float32(0)))


def _two_pi_parts():
    parts, rest = [], 2.0 * np.pi
    for bits in (8, 11):
        unit = 2.0 ** (np.floor(np.log2(rest)) - bits + 1)
        parts.append(float(np.floor(rest / unit) * unit))
        rest -= parts[-1]
    return parts + [float(np.float32(rest))]


TWO_PI = _two_pi_parts()


def head_projection(nc, name, w_up, latent, k0, nk, cols, rms, split_kv, eps_extra, tab, k_rope, dests):
    ctx, sb, ps, sem = phase(nc, name)
    with ctx:
        banks = cols // BANK
        w = sb("w", [P, 2, cols])
        w_hi = sb("w_hi", [P, nk, cols], F32R)
        w_lo = sb("w_lo", [P, nk, cols], F32R)
        a_hi = sb("a_hi", [P, 2, nk, P], F32R)
        a_lo = sb("a_lo", [P, 2, nk, P], F32R)
        norm_w = NOPE if split_kv else QKH
        x = sb("x", [P, 2, HEADS, QKH])
        v = sb("v", [P, 2, HEADS, VH]) if split_kv else None
        sq = sb("sq", [P, HEADS, norm_w])
        ss = sb("ss", [P, HEADS])
        rs = sb("rs", [P, HEADS])
        tmp = sb("tmp", [P, HEADS])
        prod = sb("prod", [P, 4, HEADS, HALF]) if not split_kv else None
        out = ps("out", [P, 2, banks, BANK])
        w_in = [sem("w_in0"), sem("w_in1")]
        w_high, w_done, a_high, a_done = sem("w_high"), sem("w_done"), sem("a_high"), sem("a_done")
        projected, evacuated, squared = sem("projected"), sem("evacuated"), sem("squared")
        chain, scaled, turned, pool_chain = sem("chain"), sem("scaled"), sem("turned"), sem("pool_chain")
        stored = [[sem(f"stored{n}{e}") for e in range(2)] for n in range(len(dests))]
        LINKS = RSQRT_STEPS + 2
        with nc.Block() as block:

            @block.sync
            def _(sp):
                for k in range(nk):
                    sp.wait_ge(w_done, k + 1)
                    sp.dma_start(w[:, k % 2, :], w_up[k * P:(k + 1) * P, :]).then_inc(w_in[k % 2], 16)
                with sp.Fori(0, NT // 2) as i:
                    for e in range(2):
                        t = 2 * i + e
                        row = sp.snap(t * P)
                        sp.wait_ge(turned, t + 3)
                        sp.dma_start(dests[0][bass.ds(row, P), :], x[:, e].rearrange("p h d -> p (h d)")
                                     ).then_inc(stored[0][e], 16)
                        if split_kv:
                            sp.dma_start(dests[1][bass.ds(row, P), :], v[:, e].rearrange("p h d -> p (h d)")
                                         ).then_inc(stored[1][e], 16)
                for n in range(len(dests)):
                    for e in range(2):
                        sp.wait_ge(stored[n][e], 16 * (NT // 2))

            @block.scalar
            def _(act):
                def split_rows(k):
                    act.wait_ge(w_in[k % 2], 16 * (k // 2 + 1))
                    nc.scalar.activation(w_hi[:, k, :], w[:, k % 2, :], ACT.Copy).then_inc(w_high, 1)

                def split_features(t):
                    act.wait_ge(projected, t + 1)
                    nc.scalar.activation(a_hi[:, t % 2], latent[:, k0:k0 + nk, t * P:(t + 1) * P],
                                         ACT.Copy).then_inc(a_high, 1)

                act.sem_inc(evacuated, 2)
                split_features(0)
                for k in range(nk):
                    split_rows(k)
                for t in range(NT):
                    if t + 1 < NT:
                        split_features(t + 1)
                    act.wait_ge(projected, t + 3)
                    if t >= 2:
                        for n in range(len(dests)):
                            act.wait_ge(stored[n][t % 2], 16 * (t // 2))
                    r = rms[:, t:t + 1]
                    flat = out[:, t % 2].rearrange("p b c -> p (b c)")
                    if split_kv:
                        kv = flat.rearrange("p (h d) -> p h d", h=HEADS)
                        nc.scalar.activation(v[:, t % 2], kv[:, :, NOPE:], ACT.Copy, scale=r)
                        nc.scalar.activation(x[:, t % 2, :, :NOPE], kv[:, :, :NOPE], ACT.Copy,
                                             scale=r).then_inc(evacuated, 1)
                    else:
                        nc.scalar.activation(x[:, t % 2].rearrange("p h d -> p (h d)"), flat, ACT.Copy,
                                             scale=r).then_inc(evacuated, 1)

            @block.vector
            def _(dve):
                link = Chain(dve, chain)
                dve.sem_inc(w_done, 2)

                def low_features(t):
                    dve.wait_ge(a_high, t + 1)
                    nc.vector.tensor_tensor(a_lo[:, t % 2], latent[:, k0:k0 + nk, t * P:(t + 1) * P],
                                            f32(a_hi[:, t % 2]), ALU.subtract).then_inc(a_done, 1)

                low_features(0)
                for k in range(nk):
                    dve.wait_ge(w_high, k + 1)
                    nc.vector.tensor_tensor(w_lo[:, k, :], w[:, k % 2, :], f32(w_hi[:, k, :]),
                                            ALU.subtract).then_inc(w_done, 1)
                for t in range(NT):
                    if t + 1 < NT:
                        low_features(t + 1)
                    dve.wait_ge(squared, t + 1)
                    link(nc.vector.tensor_reduce(ss[:], sq[:], AX_X, ALU.add))
                    if split_kv:
                        link(nc.vector.tensor_scalar(ss[:], ss[:], eps_extra[:, t:t + 1], None, ALU.add))
                    link(nc.vector.tensor_scalar(ss[:], ss[:], 1.0 / QKH, EPS, ALU.mult, ALU.add))
                    if t:
                        dve.wait_ge(turned, t + 2)
                    rsqrt(nc, link, rs[:], tmp[:], ss[:])
                    head = x[:, t % 2, :, :norm_w]
                    nc.vector.tensor_tensor(head, head, rs[:].unsqueeze(2).to_broadcast([P, HEADS, norm_w]),
                                            ALU.mult).then_inc(scaled, 1)

            @block.gpsimd
            def _(pool):
                link = Chain(pool, pool_chain)
                pool.sem_inc(turned, 2)

                def square(t):
                    pool.wait_ge(evacuated, t + 3)
                    head = x[:, t % 2, :, :norm_w]
                    nc.gpsimd.tensor_tensor(sq[:], head, head, ALU.mult).then_inc(squared, 1)

                square(0)
                for t in range(NT):
                    pool.wait_ge(scaled, t + 1)
                    if t + 1 < NT:
                        square(t + 1)
                    x1, x2 = x[:, t % 2, :, NOPE:NOPE + HALF], x[:, t % 2, :, NOPE + HALF:]
                    if split_kv:
                        nc.gpsimd.tensor_tensor(
                            x[:, t % 2, :, NOPE:], k_rope[:, t, :].unsqueeze(1).to_broadcast([P, HEADS, ROPE]),
                            rs[:].unsqueeze(2).to_broadcast([P, HEADS, ROPE]), ALU.mult).then_inc(turned, 1)
                        continue
                    for n, a in enumerate((x1, x2, x1, x2)):
                        ins = nc.gpsimd.tensor_tensor(
                            prod[:, n], a, tab[:, n, t, :].unsqueeze(1).to_broadcast([P, HEADS, HALF]), ALU.mult)
                        if n == 3:
                            link(ins)
                    nc.gpsimd.tensor_tensor(x1, prod[:, 0], prod[:, 1], ALU.subtract)
                    link(nc.gpsimd.tensor_tensor(x2, prod[:, 2], prod[:, 3], ALU.add))
                    pool.sem_inc(turned, 1)

            @block.tensor
            def _(pe):
                pe.sem_inc(projected, 2)
                with pe.Fori(0, NT // 2) as i:
                    for e in range(2):
                        t = 2 * i + e
                        pe.wait_ge(a_done, t + 1)
                        pe.wait_ge(evacuated, t + 1)
                        for k in range(nk):
                            pe.wait_ge(w_done, k + 3)
                            for c in range(banks):
                                cc = slice(c * BANK, (c + 1) * BANK)
                                last = three_passes(nc, out[:, e, c], a_hi[:, e, k], a_lo[:, e, k],
                                                    w_hi[:, k, cc], w_lo[:, k, cc], k == 0, k == nk - 1)
                        last.then_inc(projected, 1)


def attention(nc, q_d, k_d, v_d, q_head_g, k_head_g, ident, mask, gate):
    ctx, sb, ps, sem = phase(nc, "att")
    with ctx:
        q_st = sb("q_st", [P, NT, 2 * QKH])
        k_st = sb("k_st", [P, NT, 2 * QKH])
        v_st = sb("v_st", [P, NT, 2 * VH])
        gqk = sb("gqk", [P, 2])
        t_hi = [[sb(f"{n}t_hi{e}", [P, S], F32R) for n in "qk"] for e in range(2)]
        t_lo = [[sb(f"{n}t_lo{e}", [P, S], F32R) for n in "qk"] for e in range(2)]
        v2 = [sb(f"v2{e}", [P, NT, 2 * VH], F32R) for e in range(2)]
        neg_max = sb("neg_max", [P, 2, NT])
        total = sb("total", [P, 2, NT])
        inv = sb("inv", [P, 2, NT])
        probs = [sb("probs0", [P, 4, BANK]), sb("probs1", [P, 4, S])]
        pt_hi = sb("pt_hi", [P, 3, BANK], F32R)
        pt_lo = sb("pt_lo", [P, 3, BANK], F32R)
        o_part = sb("o_part", [P, BANK])
        carrier = sb("carrier", [P, 8])
        o_sum = sb("o_sum", [P, 2, BANK])
        s_ps = ps("s_ps", [P, 2, S])
        pt_ps = ps("pt_ps", [P, 3, BANK])
        o_ps = ps("o_ps", [P, BANK])
        g_in = [sem("g_in0"), sem("g_in1")]
        g_made = sem("g_made")
        loaded = [sem(f"loaded_{n}") for n in "qkv"]
        stage_free = sem("stage_free")
        s_ready = sem("s_ready")
        s_free = sem("s_free")
        t_high = sem("t_high")
        v_high = sem("v_high")
        exp_done, inv_done, p_ready = sem("exp_done"), sem("inv_done"), sem("p_ready")
        pt_ready, pt_high, pt_low = sem("pt_ready"), sem("pt_high"), sem("pt_low")
        pv_done = sem("pv_done")
        o_copied, o_summed, gated = sem("o_copied"), sem("o_summed"), sem("gated")

        def rows(e):
            return slice(e * VH, (e + 1) * VH)

        def walk(a, qk, pv, Fori):
            a(0, 0)
            qk(0, 0, 0)
            qk(0, 0, 1)
            a(1, 1)
            pv(0, 0, 0, 0)
            with Fori(0, PAIRS - 1) as i:
                for e, pair in ((1, i), (0, i + 1)):
                    h = 2 * i + 2 - e
                    qk(h, e, 0)
                    pv(h - 1, 1 - e, 1, i)
                    qk(h, e, 1)
                    a(h + 1, 1 - e)
                    pv(h, e, 0, pair)
            h = HEADS - 1
            qk(h, 1, 0)
            pv(h - 1, 0, 1, PAIRS - 1)
            qk(h, 1, 1)
            pv(h, 1, 0, PAIRS - 1)
            pv(h, 1, 1, PAIRS - 1)

        with nc.Block() as block:

            @block.sync
            def _(sp):
                def load(first):
                    for n, (dst, src, width) in enumerate(((q_st, q_d, QKH), (k_st, k_d, QKH), (v_st, v_d, VH))):
                        view = src.rearrange("(t p) c -> p t c", p=P)
                        cols = bass.ds(first[n], 2 * width)
                        sp.dma_start(dst[:], view[:, :, cols]).then_inc(loaded[n], 16)

                load([0, 0, 0])
                with sp.Fori(1, PAIRS) as pair:
                    first = [sp.snap(pair * 2 * width) for width in (QKH, QKH, VH)]
                    sp.wait_ge(stage_free, 2 * pair)
                    load(first)

            @block.gpsimd
            def _(pool):
                def a(h, e):
                    pass

                def qk(h, e, c):
                    pool.wait_ge(gated, 2 * h + c + 1)
                    for r in range(4):
                        i = 4 * c + r
                        pool.wait_ge(inv_done, 8 * h + i + 1)
                        row = probs[c][:, r, :(i + 1) * P]
                        nc.gpsimd.tensor_tensor(row, row, inv[:, e, i:i + 1].to_broadcast([P, (i + 1) * P]),
                                                ALU.mult).then_inc(p_ready, 1)

                def pv(h, e, c, pair):
                    rows_done = 8 * HEADS if isinstance(h, int) and h == HEADS - 1 else 8 * h + 8 + 4 * c
                    pool.wait_ge(p_ready, rows_done)
                    pool.wait_ge(o_summed, 2 * h + c + 2)
                    g = gate[rows(e), pair if isinstance(pair, int) else bass.ds(pair, 1), c * BANK:(c + 1) * BANK]
                    o = o_sum[rows(e), c, :] if isinstance(pair, int) else o_sum[rows(e), c:c + 1, :]
                    nc.gpsimd.tensor_tensor(g, g, o, ALU.mult).then_inc(gated, 1)

                pool.sem_inc(gated, 2)
                walk(a, qk, pv, pool.Fori)

            @block.scalar
            def _(act):
                def a(h, e):
                    act.wait_ge(s_ready, 10 * h + 1)
                    nc.scalar.activation(t_hi[e][0][0:QKH, :], s_ps[0:QKH, 0, :], ACT.Copy,
                                         scale=gqk[0:QKH, 1:2]).then_inc(t_high, 1)
                    act.wait_ge(s_ready, 10 * h + 2)
                    nc.scalar.activation(t_hi[e][1][0:QKH, :], s_ps[0:QKH, 1, :], ACT.Copy).then_inc(t_high, 1)
                    if isinstance(h, int) and h == 0:
                        act.wait_ge(loaded[2], 16)
                    else:
                        act.wait_ge(loaded[2], a_pair(h, e) * 16)
                    off = e * VH
                    nc.scalar.activation(v2[e][:, :, off:off + VH], v_st[:, :, rows(e)],
                                         ACT.Copy).then_inc(v_high, 1)

                def qk(h, e, c):
                    for r in range(4):
                        i = 4 * c + r
                        act.wait_ge(s_free, 10 * h + 2 + i + 1 + 2)
                        row = probs[c][:, r, :(i + 1) * P]
                        nc.scalar.activation(row, row, ACT.Exp, bias=neg_max[:, e, i:i + 1], scale=-1.0,
                                             accum_out=total[:, e, i:i + 1]).then_inc(exp_done, 1)

                def pv(h, e, c, pair):
                    for j in range(4 * (c + 1)):
                        n = 4 * c + j
                        off = max(0, j - 4 * c) * P
                        act.wait_ge(pt_ready, 12 * h + n + 1)
                        nc.scalar.activation(pt_hi[:, n % 3, off:], pt_ps[:, n % 3, off:],
                                             ACT.Copy).then_inc(pt_high, 1)
                    act.wait_ge(pv_done, 12 * h + 4 + 8 * c)
                    nc.scalar.activation(o_part[rows(e), :], o_ps[rows(1 - e), :], ACT.Copy).then_inc(o_copied, 1)

                with nc.allow_non_contiguous_dma(reason="a few scalars per channel"):
                    act.dma_start(gqk[0:QKH, 0:1], q_head_g.rearrange("a d -> d a")).then_inc(g_in[0], 16)
                    act.dma_start(gqk[0:QKH, 1:2], k_head_g.rearrange("a d -> d a")).then_inc(g_in[1], 16)
                act.wait_ge(g_made, 2)
                walk(a, qk, pv, act.Fori)

            @block.vector
            def _(dve):
                def inverse(h, e, i):
                    dve.wait_ge(exp_done, 8 * h + i + 1)
                    nc.vector.reciprocal(inv[:, e, i:i + 1], total[:, e, i:i + 1]).then_inc(inv_done, 1)

                def a(h, e):
                    dve.wait_ge(t_high, 2 * h + 1)
                    nc.vector.scalar_tensor_tensor(t_lo[e][0][0:QKH, :], s_ps[0:QKH, 0, :], gqk[0:QKH, 1:2],
                                                   f32(t_hi[e][0][0:QKH, :]), ALU.mult,
                                                   ALU.subtract).then_inc(s_free, 1)
                    dve.wait_ge(t_high, 2 * h + 2)
                    nc.vector.tensor_tensor(t_lo[e][1][0:QKH, :], s_ps[0:QKH, 1, :],
                                            f32(t_hi[e][1][0:QKH, :]), ALU.subtract).then_inc(s_free, 1)
                    dve.wait_ge(v_high, h + 1)
                    hi, lo = e * VH, (1 - e) * VH
                    nc.vector.tensor_tensor(v2[e][:, :, lo:lo + VH], v_st[:, :, rows(e)],
                                            f32(v2[e][:, :, hi:hi + VH]), ALU.subtract).then_inc(stage_free, 1)

                def qk(h, e, c):
                    for r in range(4):
                        i = 4 * c + r
                        n = (i + 1) * P
                        if r >= 2:
                            dve.wait_ge(exp_done, 8 * h + i - 1)
                        dve.wait_ge(s_ready, 10 * h + 2 + i + 1)
                        if r >= 2:
                            nc.vector.reciprocal(inv[:, e, i - 2:i - 1],
                                                 total[:, e, i - 2:i - 1]).then_inc(inv_done, 1)
                        else:
                            col = 4 * e + 2 * c + r
                            nc.vector.memset(carrier[:, col:col + 1], 0.0)
                        nc.vector.tensor_tensor_reduce(probs[c][:, r, :n], s_ps[:, i % 2, :n], mask[:, S - n:],
                                                       -SCALE, 3e38, ALU.add, ALU.min,
                                                       neg_max[:, e, i:i + 1]).then_inc(s_free, 1)
                    inverse(h, e, 4 * c + 2)
                    inverse(h, e, 4 * c + 3)

                def pv(h, e, c, pair):
                    for j in range(4 * (c + 1)):
                        n = 4 * c + j
                        off = max(0, j - 4 * c) * P
                        dve.wait_ge(pt_high, 12 * h + n + 1)
                        nc.vector.tensor_tensor(pt_lo[:, n % 3, off:], pt_ps[:, n % 3, off:],
                                                f32(pt_hi[:, n % 3, off:]), ALU.subtract).then_inc(pt_low, 1)
                    dve.wait_ge(o_copied, 2 * h + c + 1)
                    dve.wait_ge(gated, 2 * h + c + 1)
                    nc.vector.tensor_tensor(o_sum[rows(e), c, :], o_ps[rows(e), :], o_part[rows(e), :],
                                            ALU.add).then_inc(o_summed, 1)

                dve.wait_ge(g_in[0], 16)
                dve.wait_ge(g_in[1], 16)
                nc.vector.tensor_tensor(gqk[0:NOPE, 1:2], gqk[0:NOPE, 0:1], gqk[0:NOPE, 1:2],
                                        ALU.mult).then_inc(g_made, 1)
                nc.vector.memset(gqk[NOPE:QKH, 1:2], 1.0).then_inc(g_made, 1)
                dve.wait_ge(g_made, 2)
                dve.sem_inc(s_free, 2)
                dve.sem_inc(pt_low, 3)
                dve.sem_inc(o_summed, 1)
                walk(a, qk, pv, dve.Fori)

            @block.tensor
            def _(pe):
                def a(h, e):
                    for n, st in enumerate((q_st, k_st)):
                        pe.wait_ge(loaded[n], a_pair(h, e) * 16)
                        pe.wait_ge(s_free, 10 * h + n + 1)
                        for t in range(NT):
                            last = nc.tensor.transpose(s_ps[0:QKH, n, t * P:(t + 1) * P],
                                                       st[:, t, e * QKH:(e + 1) * QKH], ident[:])
                        last.then_inc(s_ready, 1)

                def qk(h, e, c):
                    q_hi, q_lo = t_hi[e][0], t_lo[e][0]
                    k_hi, k_lo = t_hi[e][1], t_lo[e][1]
                    for r in range(4):
                        i = 4 * c + r
                        if r == 0:
                            pe.wait_ge(s_free, 10 * h + 4)
                        pe.wait_ge(s_free, 10 * h + 2 + i + 1)
                        qs = slice(i * P, (i + 1) * P)
                        for kc in range(c + 1):
                            ks = slice(kc * BANK, min((kc + 1) * BANK, (i + 1) * P))
                            last = three_passes(nc, s_ps[:, i % 2, ks], q_hi[0:QKH, qs], q_lo[0:QKH, qs],
                                                k_hi[0:QKH, ks], k_lo[0:QKH, ks], True, True)
                        last.then_inc(s_ready, 1)

                def pv(h, e, c, pair):
                    blocks = 4 * (c + 1)

                    def turn(j):
                        n = 4 * c + j
                        pe.wait_ge(pt_low, 12 * h + n + 1)
                        for r in range(max(0, j - 4 * c), 4):
                            if j == 0:
                                pe.wait_ge(p_ready, 8 * h + 4 * c + r + 1)
                            last = nc.tensor.transpose(pt_ps[:, n % 3, r * P:(r + 1) * P],
                                                       probs[c][:, r, j * P:(j + 1) * P], ident[:])
                        last.then_inc(pt_ready, 1)

                    def product(j):
                        n = 4 * c + j
                        pe.wait_ge(pt_low, 12 * h + n + 4)
                        if j == 0:
                            pe.wait_ge(v_low_seen, h + 1)
                            pe.wait_ge(o_summed, 2 * h + c + 1)
                        off = max(0, j - 4 * c) * P
                        vs = v2[e][:, j, :]
                        nc.tensor.matmul(o_ps[:, off:], vs, pt_hi[:, n % 3, off:], start=(j == 0), stop=False)
                        nc.tensor.matmul(o_ps[:, off:], vs, pt_lo[:, n % 3, off:], start=False,
                                         stop=(j == blocks - 1)).then_inc(pv_done, 1)

                    turn(0)
                    turn(1)
                    for j in range(blocks):
                        if j + 2 < blocks:
                            turn(j + 2)
                        product(j)

                v_low_seen = stage_free
                walk(a, qk, pv, pe.Fori)


def a_pair(h, e):
    return (h - e + 2) // 2


def hybrid_trunk(nc, x, positions, norm_ab, w_in_ab, pool_w, pool_scale, conv_w, w_out_ab, norm_c, w_in_c,
                 q_lat_norm, w_uq, kv_lat_norm, w_ukv, q_head_norm, k_head_norm, w_out_c, out):
    x1_d = nc.dram_tensor("x1_scratch", [S, D], F32, kind="Internal").ap()
    q_d = nc.dram_tensor("q_scratch", [S, Q_COLS], F32, kind="Internal").ap()
    k_d = nc.dram_tensor("k_scratch", [S, Q_COLS], F32, kind="Internal").ap()
    v_d = nc.dram_tensor("v_scratch", [S, HEADS * VH], F32, kind="Internal").ap()
    with ExitStack() as keep:
        def sb(n, shape, dt=F32, ctx=keep):
            return ctx.enter_context(nc.sbuf_tensor(n, shape, dt))

        ident = sb("ident", [P, P])
        mask = sb("mask", [P, S])
        wide = sb("wide", [P, NK, S])
        rms_qkv = sb("rms_qkv", [P, 2, NT])
        k_rope_ss = sb("k_rope_ss", [P, NT])
        k_rope = sb("k_rope", [P, NT, ROPE])
        q_tab = sb("q_tab", [P, 4, NT, HALF])
        constants(nc, ident, mask)
        with ExitStack() as layer0:
            act_hi = sb("act0_hi", [P, NK, S], F32R, layer0)
            act_lo = sb("act0_lo", [P, NK, S], F32R, layer0)
            with nc.sbuf_tensor("x_in", [P, NT, D], F32) as x_sb:
                normalise_and_transpose(nc, "norm0", x_sb, x[0], norm_ab, ident, act_hi, act_lo)
            mixers(nc, w_in_ab[0], pool_w[0], pool_scale[0], conv_w[0], act_hi, act_lo, wide)
        with ExitStack() as latents:
            tokens = sb("tokens", [P, NT, D], F32, latents)
            output_projection(nc, "out0", w_out_ab[0], wide, x[0], tokens, x1_d)
            with ExitStack() as layer1:
                act_hi = sb("act1_hi", [P, NK, S], F32R, layer1)
                act_lo = sb("act1_lo", [P, NK, S], F32R, layer1)
                normalise_and_transpose(nc, "norm1", tokens, None, norm_c, ident, act_hi, act_lo)
                latent_projection(nc, w_in_c[0], positions[0], q_lat_norm[0], kv_lat_norm[0], q_head_norm,
                                  k_head_norm, ident, act_hi, act_lo, tokens, wide, rms_qkv, q_tab, k_rope,
                                  k_rope_ss)
            head_projection(nc, "q", w_uq[0], tokens, 0, KQ, Q_COLS, rms_qkv[:, 0], False, None, q_tab, None,
                            [q_d])
            head_projection(nc, "kv", w_ukv[0], tokens, KQ, KKV, KV_COLS, rms_qkv[:, 1], True, k_rope_ss, None,
                            k_rope, [k_d, v_d])
        attention(nc, q_d, k_d, v_d, q_head_norm, k_head_norm, ident, mask, wide)
        with nc.sbuf_tensor("final", [P, NT, D], F32) as final:
            output_projection(nc, "out1", w_out_c[0], wide, x1_d, final, out[0])


INPUTS = ["x", "positions", "norm_ab", "w_in_ab", "pool_w", "pool_scale", "conv_w", "w_out_ab", "norm_c",
          "w_in_c", "q_lat_norm", "w_uq", "kv_lat_norm", "w_ukv", "q_head_norm", "k_head_norm", "w_out_c"]


def kernel(**inputs):
    import concourse.bacc as bacc
    from concourse.bass_utils import run_bass_kernel_spmd

    nc = bacc.Bacc("TRN2", target_bir_lowering=False, num_devices=1)
    arrays, args = {}, []
    for name in INPUTS:
        a = np.ascontiguousarray(inputs[name])
        arrays[f"in_{name}"] = a
        args.append(nc.dram_tensor(f"in_{name}", a.shape, mybir.dt.from_np(a.dtype), kind="ExternalInput").ap())
    out = nc.dram_tensor("out_x", (1, S, D), F32, kind="ExternalOutput").ap()
    hybrid_trunk(nc, *args, out)
    result = run_bass_kernel_spmd(nc, [arrays], core_ids=[0])
    return result.results[0]["out_x"]
```

```python
from contextlib import ExitStack

import concourse.bass as bass
import numpy as np
from concourse import mybir

F32 = mybir.dt.float32
F32R = mybir.dt.float32r
I32 = mybir.dt.int32
ACT = mybir.ActivationFunctionType
ALU = mybir.AluOpType
AX_X = mybir.AxisListType.X

P = 128
BANK = 512
S = 1024
D = 1024
NT = S // P
NK = D // P
WINDOWS = (2, 4, 8, 16)
GROUPS = len(WINDOWS)
MIX = 512
AB_IN = 6 * MIX
CONV_K = 3
HEADS, NOPE, ROPE, VH = 16, 64, 32, 64
QKH = NOPE + ROPE
HALF = ROPE // 2
Q_LORA, KV_LORA = 768, 256
KQ, KKV = Q_LORA // P, KV_LORA // P
Q_COLS = HEADS * QKH
KV_COLS = HEADS * (NOPE + VH)
Z_COL = Q_LORA + KV_LORA + ROPE
C_IN = Z_COL + HEADS * VH
THETA = 10000.0
EPS = 1e-6
SCALE = float(QKH) ** -0.5
MASKED = -1e30
PAIRS = HEADS // 2
TILES = (0, 1, 2, 3, 7, 6, 5, 4)


def f32(ap):
    return ap.bitcast(F32)


class Chain:

    def __init__(self, eng, sem, base=0):
        self.eng, self.sem, self.base, self.n = eng, sem, base, 0

    def __call__(self, ins):
        self.n += 1
        ins.then_inc(self.sem, 1)
        self.eng.wait_ge(self.sem, self.base + self.n)


RSQRT_STEPS = 10


def rsqrt(nc, link, y, t, x):
    link(nc.vector.tensor_scalar(y.bitcast(I32), x.bitcast(I32), -0.5, float(0x5F3759DF), ALU.mult, ALU.add))
    for _ in range(3):
        link(nc.vector.tensor_tensor(t, y, y, ALU.mult))
        link(nc.vector.scalar_tensor_tensor(t, t, -0.5, x, ALU.mult, ALU.mult))
        link(nc.vector.scalar_tensor_tensor(y, t, 1.5, y, ALU.add, ALU.mult))


def three_passes(nc, out, w_hi, w_lo, a_hi, a_lo, first, last):
    nc.tensor.matmul(out, w_hi, a_hi, start=first, stop=False)
    nc.tensor.matmul(out, w_hi, a_lo, start=False, stop=False)
    return nc.tensor.matmul(out, w_lo, a_hi, start=False, stop=last)


def phase(nc, name):
    ctx = ExitStack()

    def sb(n, shape, dt=F32):
        return ctx.enter_context(nc.sbuf_tensor(f"{name}_{n}", shape, dt))

    def ps(n, shape):
        return ctx.enter_context(nc.psum_tensor(f"{name}_{n}", shape, F32))

    def sem(n):
        return ctx.enter_context(nc.semaphore(f"{name}_{n}"))

    return ctx, sb, ps, sem


def constants(nc, ident, mask):
    ctx, sb, ps, sem = phase(nc, "const")
    with ctx:
        filled, shaped = sem("filled"), sem("shaped")
        with nc.Block() as block:

            @block.vector
            def _(dve):
                nc.vector.memset(ident[:], 0.0).then_inc(filled, 1)
                nc.vector.memset(mask[:], 0.0).then_inc(filled, 1)

            @block.gpsimd
            def _(pool):
                pool.wait_ge(filled, 2)
                nc.gpsimd.affine_select(out=ident[:], in_=ident[:], compare_op=ALU.not_equal, fill=1.0,
                                        base=0, pattern=[[-1, P]], channel_multiplier=1).then_inc(shaped, 1)
                tri = mask[:, S - P:S]
                nc.gpsimd.affine_select(out=tri, in_=tri, compare_op=ALU.is_ge, fill=MASKED,
                                        base=0, pattern=[[-1, P]], channel_multiplier=1).then_inc(shaped, 1)
                pool.wait_ge(shaped, 2)


def mixers(nc, x, gamma, w_in, pool_w, pool_scale, conv_w, ident, act_hi, act_lo, y, w_out, w_next, w_next_in):
    ctx, sb, ps, sem = phase(nc, "mix")
    with ctx:
        w = sb("w", [P, 2, NK, P])
        w_hi = sb("w_hi", [P, 2, NK, P], F32R)
        w_lo = sb("w_lo", [P, 2, NK, P], F32R)
        pw = sb("pw", [P, GROUPS, P])
        pw_hi = sb("pw_hi", [P, P], F32R)
        pw_lo = sb("pw_lo", [P, P], F32R)
        scl = sb("scl", [P, GROUPS])
        cw = sb("cw", [P, CONV_K, GROUPS])
        u = sb("u", [P, S])
        za = sb("za", [P, S])
        hb = sb("hb", [P, S])
        bb = sb("bb", [P, S])
        cb = sb("cb", [P, S])
        zb = sb("zb", [P, S])
        sums = sb("sums", [P, 2, S])
        d_hi = sb("d_hi", [P, S], F32R)
        d_lo = sb("d_lo", [P, S], F32R)
        count = sb("count", [P, max(WINDOWS)])
        inv = sb("inv", [P, max(WINDOWS)])
        head = sb("head", [P, max(WINDOWS)])
        ss = sb("ss", [P, NT])
        ms = sb("ms", [P, NT])
        rstd = sb("rstd", [P, NT])
        tmp = sb("tmp", [P, NT])
        x_sb, squares, gam, xn = y, hb, cb, sums
        proj = ps("proj", [P, 2, S])
        tp = ps("tp", [P, 2, NK, P])
        pooled = tp[:, 0].rearrange("p k t -> p (k t)")
        w_loaded = [sem("w_loaded0"), sem("w_loaded1")]
        gamma_in = sem("gamma_in")
        x_in = [sem(f"x_in{t}") for t in range(NT)]
        squared, scalars, normed = sem("squared"), sem("scalars"), sem("normed")
        turned, act_high, act_done = sem("turned"), sem("act_high"), sem("act_done")
        small = [sem(f"small{n}") for n in range(3)]
        hi_done, lo_done, proj_ready, evacuated = sem("hi_done"), sem("lo_done"), sem("proj_ready"), sem("evacuated")
        counted, d_ready, pool_ready, mixed = sem("counted"), sem("d_ready"), sem("pool_ready"), sem("mixed")
        chain, pw_high, pw_done = sem("chain"), sem("pw_high"), sem("pw_done")
        N = 6 * GROUPS
        dest = [u, za, hb, bb, cb, zb]
        w_rows = w_in.rearrange("(k p) n -> p k n", p=P)
        with nc.Block() as block:

            @block.sync
            def _(sp):
                for t in range(NT):
                    sp.dma_start(x_sb[:, t, :], x[t * P:(t + 1) * P, :]).then_inc(x_in[t], 16)
                    if t == NT // 2 - 1:
                        for j in range(2):
                            sp.dma_start(w[:, j], w_rows[:, :, j * MIX:j * MIX + P]).then_inc(w_loaded[j], 16)

                def load(m, j, col):
                    sp.wait_ge(lo_done, m + 1)
                    sp.dma_start(w[:, j % 2], w_rows[:, :, col]).then_inc(w_loaded[j % 2], 16)

                for j in range(2, 6):
                    load(j, j, slice(j * MIX, j * MIX + P))
                for k in range(NK):
                    sp.dma_start(w_next[:, k, :], w_out[k * P:(k + 1) * P, :]).then_inc(w_next_in[k], 16)
                with sp.Fori(1, GROUPS) as g:
                    for j in range(6):
                        load(6 * g + j, j, bass.ds(sp.snap(g * P + j * MIX), P))

            @block.gpsimd
            def _(pool):
                nc.gpsimd.iota(count[:], pattern=[[1, max(WINDOWS)]], base=1, channel_multiplier=0,
                               allow_small_or_imprecise_dtypes=True).then_inc(counted, 1)

            @block.scalar
            def _(act):
                act.dma_start(gam[:], gamma.to_broadcast([P, D])).then_inc(gamma_in, 16)

                def square(t):
                    act.wait_ge(x_in[t], 16)
                    if t:
                        act.wait_ge(squared, t)
                    nc.scalar.activation(squares[:], x_sb[:, t, :], ACT.Square,
                                         accum_out=ss[:, t:t + 1]).then_inc(squared, 1)

                def act_tile(t):
                    act.wait_ge(turned, t + 1)
                    nc.scalar.activation(act_hi[:, :, t * P:(t + 1) * P], tp[:, t % 2], ACT.Copy).then_inc(act_high, 1)

                for t in range(NT // 2):
                    square(t)
                act.dma_start(pw[:], pool_w.rearrange("g c d -> c g d")).then_inc(small[0], 16)
                with nc.allow_non_contiguous_dma(reason="a few scalars per channel"):
                    act.dma_start(scl[:], pool_scale.rearrange("(g p) -> p g", p=P)).then_inc(small[1], 16)
                    act.dma_start(cw[:], conv_w.rearrange("k (g p) -> p k g", p=P)).then_inc(small[2], 16)

                def high(m):
                    act.wait_ge(w_loaded[m % 2], 16 * (m // 2 + 1))
                    act.wait_ge(proj_ready, m + 1)
                    nc.scalar.activation(w_hi[:, m % 2], w[:, m % 2], ACT.Copy).then_inc(hi_done, 1)

                act.sem_inc(evacuated, 2)
                high(0)
                high(1)
                square(4)
                act_tile(0)
                square(5)
                act_tile(1)
                square(6)
                act_tile(2)
                square(7)
                for t in range(3, NT):
                    act_tile(t)
                act.wait_ge(small[0], 16)
                for m in range(N):
                    if 1 <= m < N - 1:
                        high(m + 1)
                    act.wait_ge(proj_ready, m + 3)
                    if m % 6 == 0:
                        act.wait_ge(mixed, m // 6 + 1)
                    nc.scalar.activation(dest[m % 6][:], proj[:, m % 2], ACT.Silu if m % 6 in (1, 5) else ACT.Copy
                                         ).then_inc(evacuated, 1)
                    if m % 6 == 0:
                        nc.scalar.activation(pw_hi[:], pw[:, m // 6], ACT.Copy).then_inc(pw_high, 1)

            @block.vector
            def _(dve):
                link = Chain(dve, chain)

                def low(m):
                    dve.wait_ge(hi_done, m + 1)
                    nc.vector.tensor_tensor(w_lo[:, m % 2], w[:, m % 2], f32(w_hi[:, m % 2]),
                                            ALU.subtract).then_inc(lo_done, 1)

                dve.sem_inc(lo_done, 2)
                dve.sem_inc(mixed, 1)
                dve.sem_inc(act_done, 2)

                def statistics(half):
                    ts = slice(half * NT // 2, (half + 1) * NT // 2)
                    dve.wait_ge(squared, ts.stop)
                    link(nc.vector.tensor_scalar(ms[:, ts], ss[:, ts], 1.0 / D, EPS, ALU.mult, ALU.add))
                    rsqrt(nc, link, rstd[:, ts], tmp[:, ts], ms[:, ts])

                def norm(t):
                    nc.vector.scalar_tensor_tensor(xn[:, t % 2], x_sb[:, t, :], rstd[:, t:t + 1], gam[:],
                                                   ALU.mult, ALU.mult).then_inc(normed, 1)

                def act_low(t):
                    dve.wait_ge(act_high, t + 1)
                    cols = slice(t * P, (t + 1) * P)
                    nc.vector.tensor_tensor(act_lo[:, :, cols], tp[:, t % 2], f32(act_hi[:, :, cols]),
                                            ALU.subtract).then_inc(act_done, 1)

                statistics(0)
                dve.wait_ge(gamma_in, 16)
                norm(0)
                norm(1)
                low(0)
                for t in range(NT):
                    if t == 1:
                        low(1)
                    act_low(t)
                    if t == 2:
                        statistics(1)
                    if t + 2 < NT:
                        norm(t + 2)
                dve.wait_ge(counted, 1)
                dve.wait_ge(small[1], 16)
                dve.wait_ge(small[2], 16)

                def pool_sums(g):
                    win = WINDOWS[g]
                    src, n = u, 0
                    step = 1
                    while step < win:
                        dst = sums[:, n % 2]
                        link(nc.vector.tensor_tensor(dst[:, step:], src[:, step:], src[:, :S - step], ALU.add))
                        link(nc.vector.tensor_copy(dst[:, :step], src[:, :step]))
                        src, n, step = dst, n + 1, 2 * step
                    link(nc.vector.tensor_scalar(head[:, :win], count[:, :win], float(win), None, ALU.min))
                    link(nc.vector.reciprocal(inv[:, :win], head[:, :win]))
                    link(nc.vector.tensor_tensor(head[:, :win], src[:, :win], inv[:, :win], ALU.mult))
                    other = sums[:, n % 2]
                    link(nc.vector.scalar_tensor_tensor(other[:, win:], src[:, win:], 1.0 / win, u[:, win:],
                                                        ALU.mult, ALU.subtract))
                    link(nc.vector.tensor_tensor(other[:, :win], head[:, :win], u[:, :win], ALU.subtract))
                    link(nc.vector.tensor_copy(d_hi[:], other))
                    nc.vector.tensor_tensor(d_lo[:], other, f32(d_hi[:]), ALU.subtract).then_inc(d_ready, 1)

                def conv(g):
                    ch, acc = sums[:, 0], sums[:, 1]
                    dve.wait_ge(d_ready, g + 1)
                    link(nc.vector.tensor_tensor(ch, cb[:], hb[:], ALU.mult))
                    link(nc.vector.tensor_scalar(acc, ch, cw[:, 2, g:g + 1], None, ALU.mult))
                    for k in (1, 0):
                        lag = CONV_K - 1 - k
                        link(nc.vector.scalar_tensor_tensor(acc[:, lag:], ch[:, :S - lag], cw[:, k, g:g + 1],
                                                            acc[:, lag:], ALU.mult, ALU.add))
                    link(nc.vector.tensor_tensor(acc, acc, bb[:], ALU.mult))

                for m in range(N):
                    if 1 <= m < N - 1:
                        low(m + 1)
                    g = m // 6
                    dve.wait_ge(evacuated, m + 3)
                    if m % 6 == 1:
                        dve.wait_ge(pw_high, g + 1)
                        nc.vector.tensor_tensor(pw_lo[:], pw[:, g], f32(pw_hi[:]), ALU.subtract).then_inc(pw_done, 1)
                        pool_sums(g)
                    if m % 6 == 4:
                        conv(g)
                        dve.wait_ge(pool_ready, g + 1)
                        nc.vector.scalar_tensor_tensor(y[:, g, :], pooled, scl[:, g:g + 1], za[:],
                                                       ALU.mult, ALU.mult)
                    if m % 6 == 5:
                        nc.vector.tensor_tensor(y[:, GROUPS + g, :], sums[:, 1], zb[:], ALU.mult).then_inc(mixed, 1)

            @block.tensor
            def _(pe):
                pe.sem_inc(proj_ready, 2)

                def transpose(t):
                    pe.wait_ge(normed, t + 1)
                    pe.wait_ge(act_done, t + 1)
                    for k in range(NK):
                        last = nc.tensor.transpose(tp[:, t % 2, k], xn[:, t % 2, k * P:(k + 1) * P], ident[:])
                    last.then_inc(turned, 1)

                def project(j, c, ks):
                    for k in ks:
                        cols = slice(c * BANK, (c + 1) * BANK)
                        last = three_passes(nc, proj[:, j % 2, cols], w_hi[:, j % 2, k], w_lo[:, j % 2, k],
                                            act_hi[:, k, cols], act_lo[:, k, cols], k == 0, k == NK - 1)
                    return last

                def project_group(g, j0):
                    for j in range(j0, 6):
                        m = 6 * g + j
                        pe.wait_ge(lo_done, m + 3)
                        pe.wait_ge(evacuated, m + 1)
                        for c in range(2):
                            last = project(j, c, range(NK))
                        last.then_inc(proj_ready, 1)
                        if j == 3:
                            pool_map(g)

                def pool_map(g):
                    pe.wait_ge(pw_done, g + 1)
                    pe.wait_ge(d_ready, g + 1)
                    pe.wait_ge(mixed, g + 1)
                    for c in range(2):
                        cols = slice(c * BANK, (c + 1) * BANK)
                        last = three_passes(nc, pooled[:, cols], pw_hi[:], pw_lo[:],
                                            d_hi[:, cols], d_lo[:, cols], True, True)
                    last.then_inc(pool_ready, 1)

                for t in range(NT // 2):
                    transpose(t)
                pe.wait_ge(act_done, NT // 2 + 2)
                for j in range(2):
                    pe.wait_ge(lo_done, j + 3)
                    for half in range(2):
                        project(j, 0, range(half * NK // 2, (half + 1) * NK // 2))
                        transpose(NT // 2 + 2 * j + half)
                pe.wait_ge(act_done, NT + 2)
                for j in range(2):
                    project(j, 1, range(NK)).then_inc(proj_ready, 1)
                project_group(0, 2)
                with pe.Fori(1, GROUPS) as g:
                    project_group(g, 0)


class Weights:

    def __init__(self, nc, keep, name):
        self.nc = nc
        self.w = keep.enter_context(nc.sbuf_tensor(f"{name}_w", [P, 2, NK, P], F32))
        self.w_hi = keep.enter_context(nc.sbuf_tensor(f"{name}_w_hi", [P, 2, NK, P], F32R))
        self.w_lo = keep.enter_context(nc.sbuf_tensor(f"{name}_w_lo", [P, 2, NK, P], F32R))
        self.w_loaded = [keep.enter_context(nc.semaphore(f"{name}_w_loaded{n}")) for n in range(2)]
        self.hi_done = keep.enter_context(nc.semaphore(f"{name}_hi_done"))
        self.lo_done = keep.enter_context(nc.semaphore(f"{name}_lo_done"))

    def load(self, sp, w_in, m, slot, col):
        sp.wait_ge(self.lo_done, m + 1)
        sp.dma_start(self.w[:, slot], w_in.rearrange("(k p) n -> p k n", p=P)[:, :, col]).then_inc(
            self.w_loaded[slot], 16)

    def high(self, act, m, proj_ready=None):
        act.wait_ge(self.w_loaded[m % 2], 16 * (m // 2 + 1))
        if proj_ready is not None:
            act.wait_ge(proj_ready, m + 1)
        self.nc.scalar.activation(self.w_hi[:, m % 2], self.w[:, m % 2], ACT.Copy).then_inc(self.hi_done, 1)

    def low(self, dve, m):
        dve.wait_ge(self.hi_done, m + 1)
        self.nc.vector.tensor_tensor(self.w_lo[:, m % 2], self.w[:, m % 2], f32(self.w_hi[:, m % 2]),
                                     ALU.subtract).then_inc(self.lo_done, 1)


def output_projection(nc, name, features, res_dram, dest, w, w_hi, w_lo, w_in, norm=None, following=None):
    ctx, sb, ps, sem = phase(nc, name)
    with ctx:
        a_hi = sb("a_hi", [P, 2, NK, P], F32R)
        a_lo = sb("a_lo", [P, 2, NK, P], F32R)
        SLOTS = 3
        res = sb("res", [P, SLOTS, D])
        out = ps("out", [P, 2, D])
        res_in = [sem(f"res_in{n}") for n in range(SLOTS)]
        w_high, w_done, a_high, a_done = sem("w_high"), sem("w_done"), sem("a_high"), sem("a_done")
        projected, added = sem("projected"), sem("added")
        stored = [sem(f"stored{n}") for n in range(SLOTS)]
        if norm:
            gamma, ident, act_hi, act_lo = norm
            gam = sb("gamma", [P, D])
            squares = sb("squares", [P, D])
            xn = sb("xn", [P, D])
            ss = sb("ss", [P, NT])
            ms = sb("ms", [P, NT])
            rstd = sb("rstd", [P, NT])
            tmp = sb("tmp", [P, NT])
            tp = ps("tp", [P, NK, P])
            gamma_in = sem("gamma_in")
            squared, scalars, normed = sem("squared"), sem("scalars"), sem("normed")
            turned, act_high, act_done = sem("turned"), sem("act_high"), sem("act_done")
        with nc.Block() as block:

            @block.sync
            def _(sp):
                def load(t):
                    n = t % SLOTS
                    sp.dma_start(res[:, n, :], res_dram[t * P:(t + 1) * P, :]).then_inc(res_in[n], 16)

                for t in range(SLOTS):
                    load(t)
                if following:
                    for m in range(2):
                        following[1].load(sp, following[0], m, m, slice(m * P, (m + 1) * P))
                for t in range(NT):
                    n = t % SLOTS
                    sp.wait_ge(added, t + 3)
                    sp.dma_start(dest[t * P:(t + 1) * P, :], res[:, n, :]).then_inc(stored[n], 16)
                    if t and t - 1 + SLOTS < NT:
                        before = t - 1
                        sp.wait_ge(stored[before % SLOTS], 16 * (before // SLOTS + 1))
                        if norm:
                            sp.wait_ge(normed, before + 1)
                        load(before + SLOTS)
                for n in range(SLOTS):
                    sp.wait_ge(stored[n], 16 * len(range(n, NT, SLOTS)))

            @block.scalar
            def _(act):
                if norm:
                    act.dma_start(gam[:], gamma.to_broadcast([P, D])).then_inc(gamma_in, 16)

                def split_features(t):
                    act.wait_ge(projected, t + 1)
                    nc.scalar.activation(a_hi[:, t % 2], features[:, :, t * P:(t + 1) * P],
                                         ACT.Copy).then_inc(a_high, 1)

                split_features(0)
                for k in range(NK):
                    act.wait_ge(w_in[k], 16)
                    nc.scalar.activation(w_hi[:, k, :], w[:, k, :], ACT.Copy).then_inc(w_high, 1)
                for t in range(NT):
                    if t + 1 < NT:
                        split_features(t + 1)
                    if norm:
                        act.wait_ge(added, t + 3)
                        if t:
                            act.wait_ge(squared, t)
                        nc.scalar.activation(squares[:], res[:, t % SLOTS, :], ACT.Square,
                                             accum_out=ss[:, t:t + 1]).then_inc(squared, 1)
                        act.wait_ge(turned, t + 1)
                        nc.scalar.activation(act_hi[:, :, t * P:(t + 1) * P], tp[:], ACT.Copy).then_inc(act_high, 1)
                    if following and t in (2, 3):
                        following[1].high(act, t - 2)

            @block.vector
            def _(dve):
                dve.sem_inc(added, 2)
                if following:
                    dve.sem_inc(following[1].lo_done, 2)

                def low_features(t):
                    dve.wait_ge(a_high, t + 1)
                    nc.vector.tensor_tensor(a_lo[:, t % 2], features[:, :, t * P:(t + 1) * P],
                                            f32(a_hi[:, t % 2]), ALU.subtract).then_inc(a_done, 1)

                low_features(0)
                for k in range(NK):
                    dve.wait_ge(w_high, k + 1)
                    nc.vector.tensor_tensor(w_lo[:, k, :], w[:, k, :], f32(w_hi[:, k, :]),
                                            ALU.subtract).then_inc(w_done, 1)
                if norm:
                    link = Chain(dve, scalars)
                    dve.wait_ge(gamma_in, 16)
                for t in range(NT):
                    n = t % SLOTS
                    if t + 1 < NT:
                        low_features(t + 1)
                    dve.wait_ge(res_in[n], 16 * (t // SLOTS + 1))
                    dve.wait_ge(projected, t + 3)
                    nc.vector.tensor_tensor(res[:, n, :], out[:, t % 2, :], res[:, n, :], ALU.add).then_inc(added, 1)
                    if norm:
                        one = slice(t, t + 1)
                        dve.wait_ge(squared, t + 1)
                        link(nc.vector.tensor_scalar(ms[:, one], ss[:, one], 1.0 / D, EPS, ALU.mult, ALU.add))
                        rsqrt(nc, link, rstd[:, one], tmp[:, one], ms[:, one])
                        nc.vector.scalar_tensor_tensor(xn[:], res[:, n, :], rstd[:, one], gam[:],
                                                       ALU.mult, ALU.mult).then_inc(normed, 1)
                        dve.wait_ge(act_high, t + 1)
                        cols = slice(t * P, (t + 1) * P)
                        nc.vector.tensor_tensor(act_lo[:, :, cols], tp[:], f32(act_hi[:, :, cols]),
                                                ALU.subtract).then_inc(act_done, 1)
                    if following and t in (2, 3):
                        following[1].low(dve, t - 2)

            @block.tensor
            def _(pe):
                def transpose(t):
                    pe.wait_ge(normed, t + 1)
                    if t:
                        pe.wait_ge(act_done, t)
                    for k in range(NK):
                        last = nc.tensor.transpose(tp[:, k], xn[:, k * P:(k + 1) * P], ident[:])
                    last.then_inc(turned, 1)

                pe.sem_inc(projected, 2)
                for t in range(NT):
                    pe.wait_ge(a_done, t + 1)
                    pe.wait_ge(added, t + 1)
                    for k in range(NK):
                        if t == 0:
                            pe.wait_ge(w_done, k + 1)
                        if norm and t and k == NK - 2:
                            transpose(t - 1)
                        for c in range(2):
                            cols = slice(c * BANK, (c + 1) * BANK)
                            last = three_passes(nc, out[:, t % 2, cols], a_hi[:, t % 2, k], a_lo[:, t % 2, k],
                                                w_hi[:, k, cols], w_lo[:, k, cols], k == 0, k == NK - 1)
                    last.then_inc(projected, 1)
                if norm:
                    transpose(NT - 1)


def latent_projection(nc, w_in, positions, q_lat_g, kv_lat_g, q_head_g, k_head_g, ident, act_hi, act_lo,
                      latent, gate, rms_qkv, q_tab, k_rope, k_rope_ss, weights, w_ukv, w_next, w_next_in):
    ctx, sb, ps, sem = phase(nc, "lat")
    with ctx:
        w_hi, w_lo, lo_done = weights.w_hi, weights.w_lo, weights.lo_done
        gam = sb("gam", [P, KQ + KKV])
        squares = sb("squares", [P, S])
        sq = sb("sq", [P, 2, S])
        krt = sb("krt", [P, S])
        ones = sb("ones", [P, 2])
        ms = sb("ms", [P, 2, NT])
        tmp = sb("tmp", [P, 2, NT])
        pos_i = sb("pos_i", [P, NT], I32)
        pos = sb("pos", [P, NT])
        freq = sb("freq", [P, HALF])
        head_g = sb("head_g", [P, 2, ROPE])
        ang = sb("ang", [P, NT, HALF])
        turns = sb("turns", [P, NT, HALF])
        red = sb("red", [P, 2, NT, HALF])
        trig = sb("trig", [P, 2, NT, HALF])
        kr = sb("kr", [P, NT, ROPE])
        ktab = sb("ktab", [P, 4, NT, HALF])
        prod = sb("prod", [P, 4, NT, HALF])
        kr2 = sb("kr2", [P, NT, ROPE])
        proj = ps("proj", [P, 2, S])
        small_ps = ps("small", [P, BANK])
        turned_ps = ps("turned", [P, NT, ROPE])
        gam_in = [sem("gam_in0"), sem("gam_in1")]
        small_in = [sem(f"small_in{n}") for n in range(3)]
        proj_ready, evacuated = sem("proj_ready"), sem("evacuated")
        chain, freq_set, reduced, trig_done = sem("chain"), sem("freq_set"), sem("reduced"), sem("trig_done")
        squared, summed, ones_set, small_ready, kr_out = (
            sem("squared"), sem("summed"), sem("ones_set"), sem("small_ready"), sem("kr_out"))
        LAT = KQ + KKV
        N = LAT + 1 + NK

        with nc.Block() as block:

            @block.sync
            def _(sp):
                with sp.Fori(1, LAT // 2) as i:
                    for e in range(2):
                        weights.load(sp, w_in, 2 * i + e, e, bass.ds(sp.snap(i * 2 * P + e * P), P))
                for k in range(KKV):
                    sp.dma_start(w_next[:, k, :], w_ukv[k * P:(k + 1) * P, :]).then_inc(w_next_in[k], 16)
                weights.load(sp, w_in, LAT, 0, slice(LAT * P, LAT * P + P))
                with sp.Fori(0, NK // 2) as i:
                    for e in range(2):
                        weights.load(sp, w_in, 2 * i + LAT + 1 + e, 1 - e, bass.ds(sp.snap(i * 2 * P + Z_COL + e * P), P))

            @block.gpsimd
            def _(pool):
                for j in range(HALF):
                    f = float(np.float32(THETA ** (-2.0 * j / ROPE)))
                    nc.gpsimd.memset(freq[:, j:j + 1], f).then_inc(freq_set, 1)
                nc.gpsimd.memset(ones[:], 1.0).then_inc(ones_set, 1)
                for n, m in enumerate([1, 2, 3, 4, 5, 7]):
                    if n:
                        pool.wait_ge(summed, n)
                    pool.wait_ge(squared, m + 1)
                    total = sq[:, 0 if m < KQ else 1, :]
                    nc.gpsimd.tensor_tensor(total, total, squares[:], ALU.add).then_inc(summed, 1)

            @block.scalar
            def _(act):
                with nc.allow_non_contiguous_dma(reason="a few scalars per channel or token"):
                    act.dma_start(gam[:, :KQ], q_lat_g.rearrange("(k p) -> p k", p=P)).then_inc(gam_in[0], 16)
                    act.dma_start(gam[:, KQ:], kv_lat_g.rearrange("(k p) -> p k", p=P)).then_inc(gam_in[1], 16)
                    act.dma_start(pos_i[:], positions.rearrange("(t p) -> p t", p=P)).then_inc(small_in[0], 16)
                act.dma_start(head_g[:, 0], q_head_g[:, NOPE:].to_broadcast([P, ROPE])).then_inc(small_in[1], 16)
                act.dma_start(head_g[:, 1], k_head_g[:, NOPE:].to_broadcast([P, ROPE])).then_inc(small_in[2], 16)
                act.sem_inc(evacuated, 2)

                act.wait_ge(reduced, 2)
                nc.scalar.activation(trig[:], red[:], ACT.Sin).then_inc(trig_done, 1)
                act.wait_ge(gam_in[0], 16)
                act.wait_ge(gam_in[1], 16)
                for m in range(N):
                    if 1 <= m < N - 1:
                        weights.high(act, m + 1, proj_ready)
                    act.wait_ge(proj_ready, m + 3)
                    src = proj[:, m % 2]
                    if m < LAT:
                        nc.scalar.activation(latent[:, m, :], src, ACT.Copy, scale=gam[:, m:m + 1])
                        if m in (0, KQ):
                            sq_dst = sq[:, 0 if m == 0 else 1, :]
                        else:
                            sq_dst = squares[:]
                            before = m - 1 if m < KQ else m - 2
                            if before:
                                act.wait_ge(summed, before)
                        nc.scalar.activation(sq_dst, src, ACT.Square).then_inc(squared, 1)
                        act.wait_ge(squared, m + 1)
                        act.sem_inc(evacuated, 1)
                    elif m == LAT:
                        nc.scalar.activation(krt[0:ROPE, :], src[0:ROPE, :], ACT.Copy).then_inc(evacuated, 1)
                    else:
                        nc.scalar.activation(gate[:, m - LAT - 1, :], src, ACT.Silu).then_inc(evacuated, 1)

            @block.vector
            def _(dve):
                link = Chain(dve, chain)

                def by_token(ap):
                    return ap.unsqueeze(1).to_broadcast([P, NT, HALF])

                dve.wait_ge(small_in[0], 16)
                dve.wait_ge(freq_set, HALF)
                link(nc.vector.tensor_copy(pos[:], pos_i[:]))
                link(nc.vector.tensor_tensor(ang[:], pos[:].unsqueeze(2).to_broadcast([P, NT, HALF]),
                                             by_token(freq[:]), ALU.mult))
                for which, quarter in ((0, 0.0), (1, 0.25)):
                    r = red[:, which]
                    link(nc.vector.tensor_scalar(turns[:], ang[:], TURN, quarter, ALU.mult, ALU.add))
                    link(nc.vector.tensor_scalar(turns[:], turns[:], ROUND, ROUND, ALU.add, ALU.subtract))
                    link(nc.vector.scalar_tensor_tensor(r, turns[:], -TWO_PI[0], ang[:], ALU.mult, ALU.add))
                    for part in TWO_PI[1:]:
                        link(nc.vector.scalar_tensor_tensor(r, turns[:], -part, r, ALU.mult, ALU.add))
                    if which:
                        link(nc.vector.tensor_scalar(r, r, float(np.float32(np.pi / 2)), None, ALU.add))
                    link(nc.vector.tensor_scalar(r, r, PI, -PI, ALU.min, ALU.max))
                    dve.sem_inc(reduced, 1)
                dve.wait_ge(trig_done, 1)
                dve.wait_ge(small_in[1], 16)
                dve.wait_ge(small_in[2], 16)
                sin, cos = trig[:, 0], trig[:, 1]
                for which, tab in ((0, q_tab), (1, ktab)):
                    g1, g2 = head_g[:, which, :HALF], head_g[:, which, HALF:]
                    for n, (g, f) in enumerate(((g1, cos), (g2, sin), (g1, sin), (g2, cos))):
                        link(nc.vector.tensor_tensor(tab[:, n], f, by_token(g), ALU.mult))
                for m in range(2, LAT + 6):
                    weights.low(dve, m)
                dve.wait_ge(small_ready, 1)
                for n, width in ((0, Q_LORA), (1, KV_LORA)):
                    link(nc.vector.tensor_scalar(ms[:, n], small_ps[:, n * NT:(n + 1) * NT], 1.0 / width, EPS,
                                                 ALU.mult, ALU.add))
                rsqrt(nc, link, rms_qkv[:], tmp[:], ms[:])
                link(nc.vector.tensor_copy(kr[:], turned_ps[:]))
                link(nc.vector.tensor_tensor(kr2[:], kr[:], kr[:], ALU.mult))
                link(nc.vector.tensor_reduce(k_rope_ss[:], kr2[:], AX_X, ALU.add))
                link(nc.vector.tensor_scalar(k_rope_ss[:], k_rope_ss[:], QKH * EPS, None, ALU.add))
                x1, x2 = kr[:, :, :HALF], kr[:, :, HALF:]
                for n, x in enumerate((x1, x2, x1, x2)):
                    link(nc.vector.tensor_tensor(prod[:, n], x, ktab[:, n], ALU.mult))
                link(nc.vector.tensor_tensor(k_rope[:, :, :HALF], prod[:, 0], prod[:, 1], ALU.subtract))
                link(nc.vector.tensor_tensor(k_rope[:, :, HALF:], prod[:, 2], prod[:, 3], ALU.add))
                for m in range(LAT + 6, N):
                    weights.low(dve, m)

            @block.tensor
            def _(pe):
                def tile(m, slot):
                    pe.wait_ge(lo_done, m + 3)
                    pe.wait_ge(evacuated, m + 1)
                    for c in range(2):
                        for k in range(NK):
                            cols = slice(c * BANK, (c + 1) * BANK)
                            last = three_passes(nc, proj[:, slot, cols], w_hi[:, slot, k], w_lo[:, slot, k],
                                                act_hi[:, k, cols], act_lo[:, k, cols], k == 0, k == NK - 1)
                    last.then_inc(proj_ready, 1)

                pe.sem_inc(proj_ready, 2)
                with pe.Fori(0, LAT // 2) as i:
                    for e in range(2):
                        tile(2 * i + e, e)
                for j in range(3):
                    tile(LAT + j, j % 2)
                pe.wait_ge(ones_set, 1)
                pe.wait_ge(summed, LAT - 2)
                for n in range(2):
                    for t in range(NT):
                        col = n * NT + t
                        nc.tensor.matmul(small_ps[:, col:col + 1], sq[:, n, t * P:(t + 1) * P], ones[:, 0:1],
                                         start=True, stop=True)
                for t in range(NT):
                    last = nc.tensor.transpose(turned_ps[:, t], krt[0:ROPE, t * P:(t + 1) * P],
                                               ident[0:ROPE, 0:ROPE])
                last.then_inc(small_ready, 1)
                with pe.Fori(1, NK // 2) as i:
                    for e in range(2):
                        tile(2 * i + LAT + 1 + e, 1 - e)


TURN = float(np.float32(1.0 / (2.0 * np.pi)))
ROUND = float(1.5 * 2 ** 23)
PI = float(np.nextafter(np.float32(np.pi), np.float32(0)))


def _two_pi_parts():
    parts, rest = [], 2.0 * np.pi
    for bits in (8, 11):
        unit = 2.0 ** (np.floor(np.log2(rest)) - bits + 1)
        parts.append(float(np.floor(rest / unit) * unit))
        rest -= parts[-1]
    return parts + [float(np.float32(rest))]


TWO_PI = _two_pi_parts()


def head_projections(nc, w_kv, w_kv_lo, w_kv_at, w_kv_in, w_uq, latent, rms_qkv, q_tab, k_rope, k_rope_ss,
                     q_head_g, k_head_g, gqk, q_d, k_d, v_d, q_stored):
    ctx, sb, ps, sem = phase(nc, "heads")
    with ctx:
        EARLY = KQ - 2
        STEPS = 2 * NT

        def shared(name, like, blocks, dt):
            return nc.alloc_sbuf_tensor_at(name, [P, blocks, Q_COLS], dt, offset=like)

        at = -(-nc.sbuf_base // 32) * 32
        sb("uq_place", [P, EARLY, Q_COLS])
        uq = nc.alloc_sbuf_tensor_at("uq", [P, EARLY, Q_COLS], F32, offset=at)
        uq_lo = nc.alloc_sbuf_tensor_at("uq_lo", [P, EARLY, Q_COLS], F32R, offset=at)
        uq_hi = sb("uq_hi", [P, EARLY, Q_COLS], F32R)
        a_hi = sb("a_hi", [P, 2, KQ, P], F32R)
        a_lo = sb("a_lo", [P, 2, KQ, P], F32R)
        RING = 4
        x = sb("x", [P, RING, HEADS, QKH])
        assert nc.sbuf_base <= w_kv_at, (nc.sbuf_base, w_kv_at)
        if w_kv_at > nc.sbuf_base:
            sb("gap", [P, (w_kv_at - nc.sbuf_base) // 4])
        sb("kv_place", [P, KKV, KV_COLS])
        kv_hi_at = -(-nc.sbuf_base // 32) * 32
        sb("kv_hi_place", [P, KKV, KV_COLS])
        w_kv_hi = nc.alloc_sbuf_tensor_at("w_kv_hi", [P, KKV, KV_COLS], F32R, offset=kv_hi_at)
        late = shared("uq_late", w_kv_at, KQ - EARLY, F32)
        late_lo = shared("uq_late_lo", w_kv_at, KQ - EARLY, F32R)
        late_hi = shared("uq_late_hi", kv_hi_at, KQ - EARLY, F32R)
        v = sb("v", [P, 2, HEADS, VH])
        sq = sb("sq", [P, HEADS * QKH])
        ss = sb("ss", [P, HEADS])
        rs = sb("rs", [P, 2, HEADS])
        tmp = sb("tmp", [P, HEADS])
        prod = v[:, 0].rearrange("p h d -> p (h d)").rearrange("p (n h d) -> p n h d", n=4, h=HEADS)
        out = ps("out", [P, 2, 4, BANK])
        uq_in = [sem(f"uq_in{k}") for k in range(KQ)]
        kv_high, kv_done = sem("kv_high"), sem("kv_done")
        uq_high, uq_done, late_done = sem("uq_high"), sem("uq_done"), sem("late_done")
        a_high, a_done = sem("a_high"), sem("a_done")
        projected, squared, v_done = sem("projected"), sem("squared"), sem("v_done")
        k_done = sem("k_done")
        chain, reduced, scaled = sem("chain"), sem("reduced"), sem("scaled")
        turned, multiplied, half_read = sem("turned"), sem("multiplied"), sem("half_read")
        x_stored = [sem(f"x_stored{e}") for e in range(RING)]
        g_in, g_made = [sem("g_in0"), sem("g_in1")], sem("g_made")
        v_stored = [sem(f"v_stored{e}") for e in range(2)]
        half = KV_COLS // 2

        def features(n):
            t = n % NT
            lo, hi = (KQ, KQ + KKV) if n < NT else (0, KQ)
            return latent[:, lo:hi, t * P:(t + 1) * P], slice(0, hi - lo)

        def head_part(n):
            if n < NT:
                return out[:, n % 2].rearrange("p b c -> p (b c)").rearrange("p (h d) -> p h d", h=HEADS)[:, :, :NOPE]
            return out[:, n % 2, :3].rearrange("p b c -> p (b c)").rearrange("p (h d) -> p h d", h=HEADS)

        def squares(n):
            w = NOPE if n < NT else QKH
            return sq[:, :HEADS * w].rearrange("p (h d) -> p h d", h=HEADS)

        def products(eng, link, n, js):
            for j in js:
                ins = eng.tensor_tensor(prod[:, j], x[:, n % RING, :, NOPE + j % 2 * HALF:NOPE + (j % 2 + 1) * HALF],
                                        q_tab[:, j, n - NT, :].unsqueeze(1).to_broadcast([P, HEADS, HALF]), ALU.mult)
            link(ins)

        def sums(eng, link, n, halves):
            for j in halves:
                ins = eng.tensor_tensor(x[:, n % RING, :, NOPE + j * HALF:NOPE + (j + 1) * HALF], prod[:, 2 * j],
                                        prod[:, 2 * j + 1], ALU.add if j else ALU.subtract)
            link(ins)

        def rms(n):
            return rms_qkv[:, 1 if n < NT else 0, n % NT:n % NT + 1]

        with nc.Block() as block:

            @block.sync
            def _(sp):
                for k in range(EARLY):
                    sp.dma_start(uq[:, k, :], w_uq[k * P:(k + 1) * P, :]).then_inc(uq_in[k], 16)
                for n in range(STEPS):
                    t, e = n % NT, n % 2
                    sp.wait_ge(turned, n + 1 + (n == STEPS - 1))
                    dest, flat = k_d if n < NT else q_d, x[:, n % RING].rearrange("p h d -> p (h d)")
                    if n == STEPS - 1:
                        for part, done in ((slice(0, 2 * QKH), q_stored[0]), (slice(2 * QKH, Q_COLS), q_stored[1])):
                            sp.dma_start(dest[t * P:(t + 1) * P, part], flat[:, part]).then_inc(done, 16)
                        continue
                    sp.dma_start(dest[t * P:(t + 1) * P, :], flat).then_inc(x_stored[n % RING], 16)
                    if n < NT:
                        sp.dma_start(v_d[t * P:(t + 1) * P, :],
                                     v[:, e].rearrange("p h d -> p (h d)")).then_inc(v_stored[e], 16)
                for e in range(RING):
                    sp.wait_ge(x_stored[e], 16 * len(range(e, STEPS - 1, RING)))
                for e in range(2):
                    sp.wait_ge(v_stored[e], 16 * (NT // 2))

            @block.scalar
            def _(act):
                def split_features(n):
                    if n >= 2:
                        act.wait_ge(projected, n + 1)
                    src, ks = features(n)
                    nc.scalar.activation(a_hi[:, n % 2, ks], src, ACT.Copy).then_inc(a_high, 1)

                with nc.allow_non_contiguous_dma(reason="a few scalars per channel"):
                    act.dma_start(gqk[0:QKH, 0:1], q_head_g.rearrange("a d -> d a")).then_inc(g_in[0], 16)
                    act.dma_start(gqk[0:QKH, 1:2], k_head_g.rearrange("a d -> d a")).then_inc(g_in[1], 16)
                act.sem_inc(k_done, 2)
                split_features(0)
                for k in range(KKV):
                    act.wait_ge(w_kv_in[k], 16)
                    for c in range(2):
                        cols = slice(c * half, (c + 1) * half)
                        nc.scalar.activation(w_kv_hi[:, k, cols], w_kv[:, k, cols], ACT.Copy).then_inc(kv_high, 1)
                for n in range(STEPS):
                    if n + 1 < STEPS:
                        split_features(n + 1)
                    if n == NT:
                        for k in range(EARLY, KQ):
                            act.wait_ge(uq_in[k], 16)
                            nc.scalar.activation(late_hi[:, k - EARLY, :], late[:, k - EARLY, :],
                                                 ACT.Copy).then_inc(uq_high, 1)
                    act.wait_ge(projected, n + 3)
                    if n == NT - 1:
                        for k in range(EARLY, KQ):
                            act.dma_start(late[:, k - EARLY, :], w_uq[k * P:(k + 1) * P, :]).then_inc(uq_in[k], 16)
                    if n:
                        act.wait_ge(reduced, n)
                    nc.scalar.activation(squares(n), head_part(n), ACT.Square, scale=rms(n)).then_inc(squared, 1)
                    if n < NT:
                        if n >= 2:
                            act.wait_ge(v_stored[n % 2], 16 * (n // 2))
                        kv = out[:, n % 2].rearrange("p b c -> p (b c)").rearrange("p (h d) -> p h d", h=HEADS)
                        nc.scalar.activation(v[:, n % 2], kv[:, :, NOPE:], ACT.Copy, scale=rms(n)).then_inc(v_done, 1)
                        if n >= RING:
                            act.wait_ge(x_stored[n % RING], 16 * (n // RING))
                        nc.scalar.activation(x[:, n % RING, :, :NOPE], kv[:, :, :NOPE], ACT.Copy,
                                             scale=rms(n)).then_inc(k_done, 1)
                    if 1 <= n <= EARLY:
                        act.wait_ge(uq_in[n - 1], 16)
                        nc.scalar.activation(uq_hi[:, n - 1, :], uq[:, n - 1, :], ACT.Copy).then_inc(uq_high, 1)

            @block.vector
            def _(dve):
                link = Chain(dve, chain)

                def low_features(n):
                    dve.wait_ge(a_high, n + 1)
                    src, ks = features(n)
                    nc.vector.tensor_tensor(a_lo[:, n % 2, ks], src, f32(a_hi[:, n % 2, ks]),
                                            ALU.subtract).then_inc(a_done, 1)

                low_features(0)
                for k in range(KKV):
                    for c in range(2):
                        cols = slice(c * half, (c + 1) * half)
                        dve.wait_ge(kv_high, 2 * k + c + 1)
                        nc.vector.tensor_tensor(w_kv_lo[:, k, cols], w_kv[:, k, cols], f32(w_kv_hi[:, k, cols]),
                                                ALU.subtract).then_inc(kv_done, 1)
                for n in range(STEPS):
                    if n + 1 < STEPS:
                        low_features(n + 1)
                    if n == NT:
                        for k in range(EARLY, KQ):
                            dve.wait_ge(uq_high, k + 1)
                            nc.vector.tensor_tensor(late_lo[:, k - EARLY, :], late[:, k - EARLY, :],
                                                    f32(late_hi[:, k - EARLY, :]), ALU.subtract).then_inc(late_done, 1)
                    dve.wait_ge(squared, n + 1)
                    ins = nc.vector.tensor_reduce(ss[:], squares(n), AX_X, ALU.add)
                    ins.then_inc(reduced, 1)
                    dve.wait_ge(reduced, n + 1)
                    if n < NT:
                        link(nc.vector.tensor_scalar(ss[:], ss[:], k_rope_ss[:, n:n + 1], 1.0 / QKH,
                                                     ALU.add, ALU.mult))
                    else:
                        link(nc.vector.tensor_scalar(ss[:], ss[:], 1.0 / QKH, EPS, ALU.mult, ALU.add))
                    e = n % 2
                    if n >= 2:
                        dve.wait_ge(turned, n - 1)
                    rsqrt(nc, link, rs[:, e], tmp[:], ss[:])
                    at = rs[:, e].unsqueeze(2)
                    if n < NT:
                        dve.wait_ge(k_done, n + 3)
                        k = x[:, n % RING, :, :NOPE]
                        nc.vector.tensor_tensor(k, k, at.to_broadcast([P, HEADS, NOPE]), ALU.mult).then_inc(scaled, 1)
                    else:
                        dve.wait_ge(x_stored[n % RING], 16 * (n // RING))
                        nc.vector.scalar_tensor_tensor(x[:, n % RING], head_part(n), rms(n),
                                                       at.to_broadcast([P, HEADS, QKH]),
                                                       ALU.mult, ALU.mult).then_inc(scaled, 1)
                    if n == 2:
                        dve.wait_ge(g_in[0], 16)
                        dve.wait_ge(g_in[1], 16)
                        nc.vector.tensor_tensor(gqk[0:NOPE, 1:2], gqk[0:NOPE, 0:1], gqk[0:NOPE, 1:2], ALU.mult)
                        nc.vector.memset(gqk[NOPE:QKH, 1:2], 1.0)
                dve.wait_ge(scaled, STEPS)
                dve.wait_ge(turned, STEPS - 1)
                products(nc.vector, link, STEPS - 1, (2, 3))
                dve.sem_inc(half_read, 1)
                dve.wait_ge(half_read, 2)
                sums(nc.vector, link, STEPS - 1, (1,))
                dve.sem_inc(turned, 1)

            @block.gpsimd
            def _(pool):
                link = Chain(pool, multiplied)
                for n in range(NT):
                    pool.wait_ge(scaled, n + 1)
                    e = n % 2
                    nc.gpsimd.tensor_tensor(
                        x[:, n % RING, :, NOPE:], k_rope[:, n, :].unsqueeze(1).to_broadcast([P, HEADS, ROPE]),
                        rs[:, e].unsqueeze(2).to_broadcast([P, HEADS, ROPE]), ALU.mult).then_inc(turned, 1)
                    if 1 <= n <= EARLY:
                        pool.wait_ge(uq_high, n)
                        nc.gpsimd.tensor_tensor(uq_lo[:, n - 1, :], uq[:, n - 1, :], f32(uq_hi[:, n - 1, :]),
                                                ALU.subtract).then_inc(uq_done, 1)
                pool.wait_ge(v_stored[0], 16 * (NT // 2))
                for n in range(NT, STEPS):
                    pool.wait_ge(scaled, n + 1)
                    if n == STEPS - 1:
                        products(nc.gpsimd, link, n, (0, 1))
                        pool.sem_inc(half_read, 1)
                        pool.wait_ge(half_read, 2)
                        sums(nc.gpsimd, link, n, (0,))
                        pool.sem_inc(turned, 1)
                        continue
                    products(nc.gpsimd, link, n, range(4))
                    sums(nc.gpsimd, link, n, range(2))
                    pool.sem_inc(turned, 1)

            @block.tensor
            def _(pe):
                pe.sem_inc(projected, 2)

                def step(n, e, nk, banks, ready, w_hi, w_lo):
                    pe.wait_ge(a_done, n + 1)
                    for k in range(nk):
                        for c in range(banks):
                            cc = slice(c * BANK, (c + 1) * BANK)
                            ready(k, c)
                            last = three_passes(nc, out[:, e, c], a_hi[:, e, k], a_lo[:, e, k],
                                                w_hi(k, cc), w_lo(k, cc), k == 0, k == nk - 1)
                    last.then_inc(projected, 1)

                def kv_ready(k, c):
                    if c % 2 == 0:
                        pe.wait_ge(kv_done, 2 * k + c // 2 + 1)

                def uq_ready(k, c):
                    if c == 0 and k < EARLY:
                        pe.wait_ge(uq_done, k + 1)
                    elif c == 0:
                        pe.wait_ge(late_done, k - EARLY + 1)

                with pe.Fori(0, NT // 2) as i:
                    for e in range(2):
                        pe.wait_ge(k_done, 2 * i + e + 1)
                        step(2 * i + e, e, KKV, 4, kv_ready,
                             lambda k, cc: w_kv_hi[:, k, cc], lambda k, cc: w_kv_lo[:, k, cc])
                with pe.Fori(NT // 2, NT) as i:
                    for e in range(2):
                        pe.wait_ge(k_done, NT + 1 + e)
                        pe.wait_ge(scaled, 2 * i + e - 1)
                        step(2 * i + e, e, KQ, 3, uq_ready,
                             lambda k, cc: uq_hi[:, k, cc] if k < EARLY else late_hi[:, k - EARLY, cc],
                             lambda k, cc: uq_lo[:, k, cc] if k < EARLY else late_lo[:, k - EARLY, cc])


def attention(nc, q_d, k_d, v_d, q_stored, gqk, ident, mask, gate, w_out, w_next, w_next_in):
    ctx, sb, ps, sem = phase(nc, "att")
    with ctx:
        q_st = sb("q_st", [P, NT, 2 * QKH])
        k_st = sb("k_st", [P, NT, 2 * QKH])
        v_st = sb("v_st", [P, NT, 2 * VH])
        t_hi = [[sb(f"{n}t_hi{e}", [P, S], F32R) for n in "qk"] for e in range(2)]
        t_lo = [[sb(f"{n}t_lo{e}", [P, S], F32R) for n in "qk"] for e in range(2)]
        v2 = [sb(f"v2{e}", [P, NT, 2 * VH], F32R) for e in range(2)]
        neg_max = sb("neg_max", [P, 2, NT])
        total = sb("total", [P, 2, NT])
        inv = sb("inv", [P, 2, NT])
        probs = [[sb(f"probs{c}{e}", [P, 4, (c + 1) * BANK]) for e in range(2)] for c in range(2)]
        pt_hi = sb("pt_hi", [P, 3, BANK], F32R)
        pt_lo = sb("pt_lo", [P, 3, BANK], F32R)
        o_part = sb("o_part", [P, BANK])
        carrier = sb("carrier", [P, 4])
        o_sum = sb("o_sum", [P, 2, BANK])
        s_ps = ps("s_ps", [P, 2, S])
        pt_ps = ps("pt_ps", [P, 3, BANK])
        o_ps = ps("o_ps", [P, BANK])
        loaded = [sem(f"loaded_{n}") for n in "qkv"]
        s_ready = sem("s_ready")
        s_free = sem("s_free")
        half_ready = sem("half_ready")
        t_high = sem("t_high")
        v_high, v_low = sem("v_high"), sem("v_low")
        exp_done, inv_done, p_ready = sem("exp_done"), sem("inv_done"), sem("p_ready")
        pt_ready, pt_high = sem("pt_ready"), sem("pt_high")
        pt_low = sem("pt_low")
        pv_done = sem("pv_done")
        o_copied = sem("o_copied")
        o_summed = sem("o_summed")
        gated = sem("gated")
        LAST = HEADS - 1

        def rows(e):
            return slice(e * VH, (e + 1) * VH)

        def is_head(h, n):
            return isinstance(h, int) and h == n

        def ring(h, p):
            if p >= 4 and not is_head(h, LAST):
                return 10 * h + 4 + p
            if is_head(h, 0):
                return 4 + p
            return 10 * h + ((2, 4, 6, 7)[p] if not is_head(h, LAST) else 2 + p)

        def slot(h, p):
            return p % 2 if p >= 4 or is_head(h, 0) or is_head(h, LAST) else (0, 0, 0, 1)[p]

        def alone(h, p):
            return p in (1, 2) and not is_head(h, 0) and not is_head(h, LAST)

        def scores(h, p, lo, hi):
            at = BANK if p == 1 and alone(h, p) else 0
            return s_ps[:, slot(h, p), at + lo:at + hi]

        def ring_q(h):
            return 2 * h if isinstance(h, int) and h < 2 else 10 * h - 7

        def ring_k(h):
            return 2 * h + 1 if isinstance(h, int) and h < 2 else 10 * h - 5

        def slot_q(h):
            return 0 if isinstance(h, int) and h < 2 else 1

        def walk(w, Fori):

            def scores_1(h, e, pair):
                g, o = h - 1, 1 - e
                products = not is_head(h, 0)
                w.tile(h, e, 4)
                if products:
                    w.split_v(h, e)
                    w.turn(g, o, 1, 2)
                    w.product(g, o, 1, 0)
                w.tile(h, e, 5)
                if products:
                    w.gating(g, o, 0, pair)
                    for j in range(1, 3):
                        w.turn(g, o, 1, j + 2)
                        w.product(g, o, 1, j)
                w.tile(h, e, 6)
                if products:
                    for j in range(3, 5):
                        w.turn(g, o, 1, j + 2)
                        w.product(g, o, 1, j)
                w.tile(h, e, 7)
                if products:
                    w.turn(g, o, 1, 7)
                    w.product(g, o, 1, 5)
                    w.product(g, o, 1, 6)
                w.turn(h, e, 0, 0)
                if products:
                    w.product(g, o, 1, 7)
                    w.output(g, o, 1)
                w.turn(h, e, 0, 1)

            def scores_0(h, e, pair, new_head=True):
                w.tile(h + 1, 1 - e, 0)
                w.turn(h, e, 0, 2)
                if new_head:
                    w.turn_q(h + 2, e)
                w.product(h, e, 0, 0)
                w.turn(h, e, 0, 3)
                w.product(h, e, 0, 1)
                w.tile(h + 1, 1 - e, 1)
                w.product(h, e, 0, 2)
                w.product(h, e, 0, 3)
                if new_head:
                    w.turn_k(h + 2, e)
                w.output(h, e, 0)
                w.tile(h + 1, 1 - e, 2)
                if not is_head(h, 0):
                    w.gating(h - 1, 1 - e, 1, pair)
                w.turn(h, e, 1, 0)
                w.turn(h, e, 1, 1)
                w.tile(h + 1, 1 - e, 3)

            for h in (0, 1):
                w.turn_q(h, h)
                w.turn_k(h, h)
            w.split_v(0, 0)
            for p in range(4):
                w.tile(0, 0, p)
            scores_1(0, 0, None)
            scores_0(0, 0, None)
            with Fori(0, PAIRS - 2) as i:
                scores_1(2 * i + 1, 1, i)
                scores_0(2 * i + 1, 1, i)
                scores_1(2 * i + 2, 0, i)
                scores_0(2 * i + 2, 0, i)
            for h in (LAST - 2, LAST - 1):
                scores_1(h, h % 2, (h - 1) // 2)
                scores_0(h, h % 2, (h - 1) // 2, new_head=h + 2 < HEADS)
            scores_1(LAST, 1, PAIRS - 1)
            w.finish_tiles()
            w.gating(LAST - 1, 0, 1, PAIRS - 1)
            for j in (2, 3):
                w.turn(LAST, 1, 0, j)
                w.product(LAST, 1, 0, j - 2)
            w.product(LAST, 1, 0, 2)
            w.product(LAST, 1, 0, 3)
            w.output(LAST, 1, 0)
            w.turn(LAST, 1, 1, 0)
            w.turn(LAST, 1, 1, 1)
            for j in range(8):
                if j + 2 < 8:
                    w.turn(LAST, 1, 1, j + 2)
                w.product(LAST, 1, 1, j)
            w.output(LAST, 1, 1)
            w.gating(LAST, 1, 0, PAIRS - 1)
            w.gating(LAST, 1, 1, PAIRS - 1)

        class Idle:

            def turn_q(self, h, e): pass
            def turn_k(self, h, e): pass
            def split_v(self, h, e): pass
            def tile(self, h, e, p): pass
            def finish_tiles(self): pass
            def turn(self, h, e, c, j): pass
            def product(self, h, e, c, j): pass
            def output(self, h, e, c): pass
            def gating(self, h, e, c, pair): pass

        def block_cols(c, j):
            return slice(max(0, j - 4 * c) * P, BANK)

        with nc.Block() as block:

            @block.sync
            def _(sp):
                parts = ((q_st, q_d, QKH), (k_st, k_d, QKH), (v_st, v_d, VH))

                def load(n, first):
                    dst, src, width = parts[n]
                    view = src.rearrange("(t p) c -> p t c", p=P)
                    sp.dma_start(dst[:], view[:, :, bass.ds(first, 2 * width)]).then_inc(loaded[n], 16)

                load(1, 0)
                sp.wait_ge(q_stored[0], 16)
                load(0, 0)
                load(2, 0)
                sp.wait_ge(q_stored[1], 16)
                for k in range(NK):
                    sp.dma_start(w_next[:, k, :], w_out[k * P:(k + 1) * P, :]).then_inc(w_next_in[k], 16)
                with sp.Fori(1, PAIRS) as pair:
                    first = [sp.snap(pair * 2 * width) for _, _, width in parts]
                    sp.wait_ge(s_ready, 20 * pair - 14)
                    load(0, first[0])
                    load(1, first[1])
                    sp.wait_ge(v_low, 2 * pair)
                    load(2, first[2])

            @block.gpsimd
            def _(pool):
                class Pool(Idle):
                    def normalise(self, h, e, p):
                        pool.wait_ge(inv_done, 8 * h + p + 1)
                        i = TILES[p]
                        row = probs[i // 4][e][:, i % 4, :(i + 1) * P]
                        nc.gpsimd.tensor_tensor(row, row, inv[:, e, i:i + 1].to_broadcast([P, (i + 1) * P]),
                                                ALU.mult).then_inc(p_ready, 1)

                    def tile(self, h, e, p):
                        if not is_head(h, 0):
                            pool.wait_ge(gated, 2 * h + (-1, -1, -1, 0, 0, 0, 1, 1)[p])
                        if p >= 2:
                            self.normalise(h, e, p - 2)
                        elif p == 0 and not is_head(h, 0):
                            self.normalise(h - 1, 1 - e, 6)
                            self.normalise(h - 1, 1 - e, 7)

                    def finish_tiles(self):
                        self.normalise(LAST, 1, 6)
                        self.normalise(LAST, 1, 7)

                    def split_v(self, h, e):
                        pool.wait_ge(v_high, h + 1)
                        hi, lo = e * VH, (1 - e) * VH
                        nc.gpsimd.tensor_tensor(v2[e][:, :, lo:lo + VH], v_st[:, :, rows(e)],
                                                f32(v2[e][:, :, hi:hi + VH]), ALU.subtract).then_inc(v_low, 1)

                    def gating(self, h, e, c, pair):
                        if is_head(h, LAST) or (is_head(h, LAST - 1) and c):
                            pool.wait_ge(p_ready, 8 * HEADS)
                        else:
                            pool.wait_ge(p_ready, 8 * h + (17 if c else 12))
                        pool.wait_ge(o_summed, 2 * h + c + 2)
                        whole = isinstance(pair, int)
                        g = gate[rows(e), pair if whole else bass.ds(pair, 1), c * BANK:(c + 1) * BANK]
                        o = o_sum[rows(e), c, :] if whole else o_sum[rows(e), c:c + 1, :]
                        nc.gpsimd.tensor_tensor(g, g, o, ALU.mult).then_inc(gated, 1)

                pool.sem_inc(gated, 2)
                walk(Pool(), pool.Fori)

            @block.scalar
            def _(act):
                class Act(Idle):
                    def turn_part(self, n, which, sl, at, e):
                        for c in range(2):
                            cols = slice(c * BANK, (c + 1) * BANK)
                            if c:
                                act.wait_ge(s_ready, at + 1)
                            else:
                                act.wait_ge(half_ready, n + 1)
                            nc.scalar.activation(t_hi[e][which][0:QKH, cols], s_ps[0:QKH, sl, cols], ACT.Copy,
                                                 scale=1.0 if which else gqk[0:QKH, 1:2]).then_inc(t_high, 1)

                    def turn_q(self, h, e):
                        self.turn_part(2 * h, 0, slot_q(h), ring_q(h), e)

                    def turn_k(self, h, e):
                        self.turn_part(2 * h + 1, 1, 1, ring_k(h), e)

                    def split_v(self, h, e):
                        act.wait_ge(loaded[2], a_pair(h, e) * 16)
                        if not (is_head(h, 0) or is_head(h, 1)):
                            act.wait_ge(pv_done, 12 * h - 12)
                        nc.scalar.activation(v2[e][:, :, rows(e)], v_st[:, :, rows(e)], ACT.Copy).then_inc(v_high, 1)

                    def exponentials(self, h, e, p):
                        act.wait_ge(s_free, ring(h, p) + 3)
                        i = TILES[p]
                        row = probs[i // 4][e][:, i % 4, :(i + 1) * P]
                        nc.scalar.activation(row, row, ACT.Exp, bias=neg_max[:, e, i:i + 1], scale=-1.0,
                                             accum_out=total[:, e, i:i + 1]).then_inc(exp_done, 1)

                    def tile(self, h, e, p):
                        if p:
                            self.exponentials(h, e, p - 1)
                        elif not is_head(h, 0):
                            self.exponentials(h - 1, 1 - e, 7)

                    def finish_tiles(self):
                        self.exponentials(LAST, 1, 7)

                    def turn(self, h, e, c, j):
                        n, cols = 4 * c + j, block_cols(c, j)
                        act.wait_ge(pt_ready, 12 * h + n + 1)
                        nc.scalar.activation(pt_hi[:, n % 3, cols], pt_ps[:, n % 3, cols],
                                             ACT.Copy).then_inc(pt_high, 1)

                    def output(self, h, e, c):
                        act.wait_ge(pv_done, 12 * h + 4 + 8 * c)
                        nc.scalar.activation(o_part[rows(e), :], o_ps[rows(1 - e), :],
                                             ACT.Copy).then_inc(o_copied, 1)

                walk(Act(), act.Fori)

            @block.vector
            def _(dve):
                class Dve(Idle):
                    def turn_q(self, h, e):
                        for c in range(2):
                            cols = slice(c * BANK, (c + 1) * BANK)
                            dve.wait_ge(t_high, 4 * h + c + 1)
                            ins = nc.vector.scalar_tensor_tensor(
                                t_lo[e][0][0:QKH, cols], s_ps[0:QKH, slot_q(h), cols], gqk[0:QKH, 1:2],
                                f32(t_hi[e][0][0:QKH, cols]), ALU.mult, ALU.subtract)
                        ins.then_inc(s_free, 1)

                    def turn_k(self, h, e):
                        for c in range(2):
                            cols = slice(c * BANK, (c + 1) * BANK)
                            dve.wait_ge(t_high, 4 * h + c + 3)
                            ins = nc.vector.tensor_tensor(t_lo[e][1][0:QKH, cols], s_ps[0:QKH, 1, cols],
                                                          f32(t_hi[e][1][0:QKH, cols]), ALU.subtract)
                        ins.then_inc(s_free, 1)

                    def inverse(self, h, e, p, at=None):
                        dve.wait_ge(exp_done, 8 * h + p + 1)
                        if at is not None:
                            dve.wait_ge(s_ready, at + 1)
                        i = TILES[p]
                        nc.vector.reciprocal(inv[:, e, i:i + 1], total[:, e, i:i + 1]).then_inc(inv_done, 1)

                    def tile(self, h, e, p):
                        at = ring(h, p)
                        if p >= 2:
                            self.inverse(h, e, p - 2, at)
                        elif p == 0 and not is_head(h, 0):
                            self.inverse(h - 1, 1 - e, 6, at)
                        else:
                            dve.wait_ge(s_ready, at + 1)
                            nc.vector.memset(carrier[:, 2 * e + p:2 * e + p + 1], 0.0)
                        i = TILES[p]
                        n = (i + 1) * P
                        nc.vector.tensor_tensor_reduce(probs[i // 4][e][:, i % 4, :n], scores(h, p, 0, n),
                                                       mask[:, S - n:], -SCALE, 3e38, ALU.add, ALU.min,
                                                       neg_max[:, e, i:i + 1]).then_inc(s_free, 1)
                        if p == 0 and not is_head(h, 0):
                            self.inverse(h - 1, 1 - e, 7)

                    def finish_tiles(self):
                        self.inverse(LAST, 1, 6)
                        self.inverse(LAST, 1, 7)

                    def turn(self, h, e, c, j):
                        n, cols = 4 * c + j, block_cols(c, j)
                        dve.wait_ge(pt_high, 12 * h + n + 1)
                        nc.vector.tensor_tensor(pt_lo[:, n % 3, cols], pt_ps[:, n % 3, cols],
                                                f32(pt_hi[:, n % 3, cols]), ALU.subtract).then_inc(pt_low, 1)

                    def output(self, h, e, c):
                        dve.wait_ge(o_copied, 2 * h + c + 1)
                        dve.wait_ge(gated, 2 * h + c + 1)
                        nc.vector.tensor_tensor(o_sum[rows(e), c, :], o_ps[rows(e), :], o_part[rows(e), :],
                                                ALU.add).then_inc(o_summed, 1)

                dve.sem_inc(s_free, 2)
                dve.sem_inc(pt_low, 3)
                dve.sem_inc(o_summed, 1)
                walk(Dve(), dve.Fori)

            @block.tensor
            def _(pe):
                class Pe(Idle):
                    def transposes(self, n, stage, at, sl, h, e):
                        pe.wait_ge(loaded[n], a_pair(h, e) * 16)
                        pe.wait_ge(s_free, at + 1)
                        for t in range(NT):
                            last = nc.tensor.transpose(s_ps[0:QKH, sl, t * P:(t + 1) * P],
                                                       stage[:, t, e * QKH:(e + 1) * QKH], ident[:])
                            if t == NT // 2 - 1:
                                last.then_inc(half_ready, 1)
                        last.then_inc(s_ready, 1)

                    def turn_q(self, h, e):
                        self.transposes(0, q_st, ring_q(h), slot_q(h), h, e)

                    def turn_k(self, h, e):
                        self.transposes(1, k_st, ring_k(h), 1, h, e)

                    def tile(self, h, e, p):
                        if p == 0:
                            pe.wait_ge(s_free, ring_k(h) + 3)
                        pe.wait_ge(s_free, ring(h, p) + (-1 if alone(h, p) else 1))
                        q_hi, q_lo = t_hi[e][0], t_lo[e][0]
                        k_hi, k_lo = t_hi[e][1], t_lo[e][1]
                        i = TILES[p]
                        qs = slice(i * P, (i + 1) * P)
                        for kc in range(i // 4 + 1):
                            ks = slice(kc * BANK, min((kc + 1) * BANK, (i + 1) * P))
                            last = three_passes(nc, scores(h, p, ks.start, ks.stop), q_hi[0:QKH, qs], q_lo[0:QKH, qs],
                                                k_hi[0:QKH, ks], k_lo[0:QKH, ks], True, True)
                        last.then_inc(s_ready, 1)

                    def turn(self, h, e, c, j):
                        n = 4 * c + j
                        pe.wait_ge(pt_low, 12 * h + n + 1)
                        for r in range(max(0, j - 4 * c), 4):
                            if j == 0:
                                pe.wait_ge(p_ready, 8 * h + (8 if c else r + 1))
                            last = nc.tensor.transpose(pt_ps[:, n % 3, r * P:(r + 1) * P],
                                                       probs[c][e][:, r, j * P:(j + 1) * P], ident[:])
                        last.then_inc(pt_ready, 1)

                    def product(self, h, e, c, j):
                        n, cols = 4 * c + j, block_cols(c, j)
                        pe.wait_ge(pt_low, 12 * h + n + 4)
                        if j == 0:
                            pe.wait_ge(v_low, h + 1)
                            pe.wait_ge(o_summed, 2 * h + c + 1)
                        nc.tensor.matmul(o_ps[:, cols], v2[e][:, j, :], pt_hi[:, n % 3, cols],
                                         start=(j == 0), stop=False)
                        nc.tensor.matmul(o_ps[:, cols], v2[e][:, j, :], pt_lo[:, n % 3, cols], start=False,
                                         stop=(j == 4 * c + 3)).then_inc(pv_done, 1)

                walk(Pe(), pe.Fori)


def a_pair(h, e):
    return (h - e + 2) // 2


def hybrid_trunk(nc, x, positions, norm_ab, w_in_ab, pool_w, pool_scale, conv_w, w_out_ab, norm_c, w_in_c,
                 q_lat_norm, w_uq, kv_lat_norm, w_ukv, q_head_norm, k_head_norm, w_out_c, out):
    x1_d = nc.dram_tensor("x1_scratch", [S, D], F32, kind="Internal").ap()
    q_d = nc.dram_tensor("q_scratch", [S, Q_COLS], F32, kind="Internal").ap()
    k_d = nc.dram_tensor("k_scratch", [S, Q_COLS], F32, kind="Internal").ap()
    v_d = nc.dram_tensor("v_scratch", [S, HEADS * VH], F32, kind="Internal").ap()
    with ExitStack() as keep:
        def sb(n, shape, dt=F32, ctx=keep):
            return ctx.enter_context(nc.sbuf_tensor(n, shape, dt))

        ident = sb("ident", [P, P])
        mask = sb("mask", [P, S])
        gqk = sb("gqk", [P, 2])
        rms_qkv = sb("rms_qkv", [P, 2, NT])
        k_rope_ss = sb("k_rope_ss", [P, NT])
        k_rope = sb("k_rope", [P, NT, ROPE])
        q_tab = sb("q_tab", [P, 4, NT, HALF])
        BIG = NK * S * 4
        base = -(-nc.sbuf_base // 32) * 32
        sb("arena01", [P, 2, NK, S])
        w_out0_in = [keep.enter_context(nc.semaphore(f"w_out0_in{k}")) for k in range(NK)]
        w_out1_in = [keep.enter_context(nc.semaphore(f"w_out1_in{k}")) for k in range(NK)]

        def big(n, name, dt=F32):
            return nc.alloc_sbuf_tensor_at(name, [P, NK, S], dt, offset=base + n * BIG)

        q_stored = [keep.enter_context(nc.semaphore(f"q_stored{n}")) for n in range(2)]
        w_kv_in = [keep.enter_context(nc.semaphore(f"w_kv_in{k}")) for k in range(KKV)]
        constants(nc, ident, mask)
        with ExitStack() as layers:
            sb("arena23", [P, 2, NK, S], F32, layers)
            w_out0, w_out0_lo = big(0, "w_out0"), big(0, "w_out0_lo", F32R)
            features, act1_lo = big(2, "features"), big(2, "act1_lo", F32R)
            act1_hi = big(3, "act1_hi", F32R)
            mixers(nc, x[0], norm_ab, w_in_ab[0], pool_w[0], pool_scale[0], conv_w[0], ident,
                   big(1, "act0_hi", F32R), big(3, "act0_lo", F32R), features, w_out_ab[0], w_out0, w_out0_in)
            lat_weights = Weights(nc, layers, "lat")
            output_projection(nc, "out0", features, x[0], x1_d, w_out0, big(1, "w_out0_hi", F32R), w_out0_lo,
                              w_out0_in, (norm_c, ident, act1_hi, act1_lo), (w_in_c[0], lat_weights))
            latent, gate = big(1, "latent"), big(0, "gate")
            w_kv_at = -(-nc.sbuf_base // 32) * 32
            sb("kv_place_early", [P, KKV, KV_COLS], F32, layers)
            w_kv = nc.alloc_sbuf_tensor_at("w_kv", [P, KKV, KV_COLS], F32, offset=w_kv_at)
            w_kv_lo = nc.alloc_sbuf_tensor_at("w_kv_lo", [P, KKV, KV_COLS], F32R, offset=w_kv_at)
            latent_projection(nc, w_in_c[0], positions[0], q_lat_norm[0], kv_lat_norm[0], q_head_norm,
                              k_head_norm, ident, act1_hi, act1_lo, latent, gate, rms_qkv, q_tab, k_rope,
                              k_rope_ss, lat_weights, w_ukv[0], w_kv, w_kv_in)
        head_projections(nc, w_kv, w_kv_lo, w_kv_at, w_kv_in, w_uq[0], latent, rms_qkv, q_tab, k_rope, k_rope_ss,
                         q_head_norm, k_head_norm, gqk, q_d, k_d, v_d, q_stored)
        w_out1 = big(1, "w_out1")
        attention(nc, q_d, k_d, v_d, q_stored, gqk, ident, mask, gate, w_out_c[0], w_out1, w_out1_in)
        with nc.sbuf_tensor("w_out1_hi", [P, NK, D], F32R) as w_hi:
            output_projection(nc, "out1", gate, x1_d, out[0], w_out1, w_hi, big(1, "w_out1_lo", F32R), w_out1_in)


INPUTS = ["x", "positions", "norm_ab", "w_in_ab", "pool_w", "pool_scale", "conv_w", "w_out_ab", "norm_c",
          "w_in_c", "q_lat_norm", "w_uq", "kv_lat_norm", "w_ukv", "q_head_norm", "k_head_norm", "w_out_c"]


def kernel(**inputs):
    import concourse.bacc as bacc
    from concourse.bass_utils import run_bass_kernel_spmd

    nc = bacc.Bacc("TRN2", target_bir_lowering=False, num_devices=1)
    arrays, args = {}, []
    for name in INPUTS:
        a = np.ascontiguousarray(inputs[name])
        arrays[f"in_{name}"] = a
        args.append(nc.dram_tensor(f"in_{name}", a.shape, mybir.dt.from_np(a.dtype), kind="ExternalInput").ap())
    out = nc.dram_tensor("out_x", (1, S, D), F32, kind="ExternalOutput").ap()
    hybrid_trunk(nc, *args, out)
    result = run_bass_kernel_spmd(nc, [arrays], core_ids=[0])
    return result.results[0]["out_x"]
```

```python
from contextlib import ExitStack

import concourse.bass as bass
import numpy as np
from concourse import mybir

F32 = mybir.dt.float32
F32R = mybir.dt.float32r
I32 = mybir.dt.int32
ACT = mybir.ActivationFunctionType
ALU = mybir.AluOpType
AX_X = mybir.AxisListType.X

P = 128
BANK = 512
S = 1024
D = 1024
NT = S // P
NK = D // P
WINDOWS = (2, 4, 8, 16)
GROUPS = len(WINDOWS)
MIX = 512
AB_IN = 6 * MIX
CONV_K = 3
HEADS, NOPE, ROPE, VH = 16, 64, 32, 64
QKH = NOPE + ROPE
HALF = ROPE // 2
Q_LORA, KV_LORA = 768, 256
KQ, KKV = Q_LORA // P, KV_LORA // P
Q_COLS = HEADS * QKH
KV_COLS = HEADS * (NOPE + VH)
Z_COL = Q_LORA + KV_LORA + ROPE
C_IN = Z_COL + HEADS * VH
THETA = 10000.0
EPS = 1e-6
SCALE = float(QKH) ** -0.5
MASKED = -1e30
PAIRS = HEADS // 2
TILES = (0, 1, 2, 3, 7, 6, 5, 4)


def f32(ap):
    return ap.bitcast(F32)


def by_tile(dram):
    return dram.rearrange("(t p) c -> p t c", p=P)


class Chain:

    def __init__(self, eng, sem, base=0):
        self.eng, self.sem, self.base, self.n = eng, sem, base, 0

    def __call__(self, ins):
        self.n += 1
        ins.then_inc(self.sem, 1)
        self.eng.wait_ge(self.sem, self.base + self.n)


RSQRT_STEPS = 10


def rsqrt(nc, link, y, t, x):
    link(nc.vector.tensor_scalar(y.bitcast(I32), x.bitcast(I32), -0.5, float(0x5F3759DF), ALU.mult, ALU.add))
    for _ in range(3):
        link(nc.vector.tensor_tensor(t, y, y, ALU.mult))
        link(nc.vector.scalar_tensor_tensor(t, t, -0.5, x, ALU.mult, ALU.mult))
        link(nc.vector.scalar_tensor_tensor(y, t, 1.5, y, ALU.add, ALU.mult))


def three_passes(nc, out, w_hi, w_lo, a_hi, a_lo, first, last):
    nc.tensor.matmul(out, w_hi, a_hi, start=first, stop=False)
    nc.tensor.matmul(out, w_hi, a_lo, start=False, stop=False)
    return nc.tensor.matmul(out, w_lo, a_hi, start=False, stop=last)


def phase(nc, name):
    ctx = ExitStack()

    def sb(n, shape, dt=F32):
        return ctx.enter_context(nc.sbuf_tensor(f"{name}_{n}", shape, dt))

    def ps(n, shape):
        return ctx.enter_context(nc.psum_tensor(f"{name}_{n}", shape, F32))

    def sem(n):
        return ctx.enter_context(nc.semaphore(f"{name}_{n}"))

    return ctx, sb, ps, sem


def mixers(nc, x, gamma, w_in, pool_w, pool_scale, conv_w, ident, mask, act_hi, act_lo, y, w_out, w_next, w_next_in):
    ctx, sb, ps, sem = phase(nc, "mix")
    with ctx:
        w = sb("w", [P, 2, NK, P])
        w_hi = sb("w_hi", [P, 2, NK, P], F32R)
        w_lo = sb("w_lo", [P, 2, NK, P], F32R)
        pw = sb("pw", [P, GROUPS, P])
        pw_hi = sb("pw_hi", [P, P], F32R)
        pw_lo = sb("pw_lo", [P, P], F32R)
        scl = sb("scl", [P, GROUPS])
        cw = sb("cw", [P, CONV_K, GROUPS])
        u = sb("u", [P, S])
        za = sb("za", [P, S])
        hb = sb("hb", [P, S])
        bb = sb("bb", [P, S])
        cb = sb("cb", [P, S])
        zb = sb("zb", [P, S])
        sums = sb("sums", [P, 2, S])
        d_hi = sb("d_hi", [P, S], F32R)
        d_lo = sb("d_lo", [P, S], F32R)
        count = sb("count", [P, max(WINDOWS)])
        inv = sb("inv", [P, max(WINDOWS)])
        head = sb("head", [P, max(WINDOWS)])
        ss = sb("ss", [P, NT])
        ms = sb("ms", [P, NT])
        rstd = sb("rstd", [P, NT])
        tmp = sb("tmp", [P, NT])
        x_sb, squares, gam, xn = y, hb, cb, sums
        proj = ps("proj", [P, 2, S])
        tp = ps("tp", [P, 2, NK, P])
        pooled = tp[:, 0].rearrange("p k t -> p (k t)")
        w_loaded = [sem("w_loaded0"), sem("w_loaded1")]
        filled, shaped, times_gamma = sem("filled"), sem("shaped"), sem("times_gamma")
        gamma_in = sem("gamma_in")
        x_in = [sem(f"x_in{t}") for t in range(NT)]
        squared, scalars, normed = sem("squared"), sem("scalars"), sem("normed")
        turned, act_high, act_done = sem("turned"), sem("act_high"), sem("act_done")
        small = [sem(f"small{n}") for n in range(3)]
        hi_done, lo_done, proj_ready, evacuated = sem("hi_done"), sem("lo_done"), sem("proj_ready"), sem("evacuated")
        counted, d_ready, pool_ready, mixed = sem("counted"), sem("d_ready"), sem("pool_ready"), sem("mixed")
        chain, pw_high, pw_done = sem("chain"), sem("pw_high"), sem("pw_done")
        N = 6 * GROUPS
        dest = [u, za, hb, bb, cb, zb]
        w_rows = w_in.rearrange("(k p) n -> p k n", p=P)
        with nc.Block() as block:

            @block.sync
            def _(sp):
                for t in range(NT):
                    sp.dma_start(x_sb[:, t, :], x[t * P:(t + 1) * P, :]).then_inc(x_in[t], 16)
                    if t == 1:
                        sp.dma_start(gam[:], gamma.to_broadcast([P, D])).then_inc(gamma_in, 16)
                    if t == NT // 2 - 1:
                        for j in range(2):
                            sp.dma_start(w[:, j], w_rows[:, :, j * MIX:j * MIX + P]).then_inc(w_loaded[j], 16)

                def load(m, j, col):
                    sp.wait_ge(lo_done, m + 1)
                    sp.dma_start(w[:, j % 2], w_rows[:, :, col]).then_inc(w_loaded[j % 2], 16)

                for j in range(2, 6):
                    load(j, j, slice(j * MIX, j * MIX + P))
                for k in range(NK):
                    sp.dma_start(w_next[:, k, :], w_out[k * P:(k + 1) * P, :]).then_inc(w_next_in, 16)
                with sp.Fori(1, GROUPS) as g:
                    for j in range(6):
                        load(6 * g + j, j, bass.ds(sp.snap(g * P + j * MIX), P))

            @block.gpsimd
            def _(pool):
                pool.wait_ge(filled, 2)
                nc.gpsimd.affine_select(out=ident[:], in_=ident[:], compare_op=ALU.not_equal, fill=1.0,
                                        base=0, pattern=[[-1, P]], channel_multiplier=1).then_inc(shaped, 1)
                tri = mask[:, S - P:S]
                nc.gpsimd.affine_select(out=tri, in_=tri, compare_op=ALU.is_ge, fill=MASKED,
                                        base=0, pattern=[[-1, P]], channel_multiplier=1)
                nc.gpsimd.iota(count[:], pattern=[[1, max(WINDOWS)]], base=1, channel_multiplier=0,
                               allow_small_or_imprecise_dtypes=True).then_inc(counted, 1)
                for m in range(2):
                    pool.wait_ge(hi_done, m + 1)
                    nc.gpsimd.tensor_tensor(w_lo[:, m], w[:, m], f32(w_hi[:, m]), ALU.subtract).then_inc(lo_done, 1)
                pool.wait_ge(gamma_in, 16)
                for t in range(NT // 2, NT):
                    pool.wait_ge(squared, t + 1)
                    nc.gpsimd.tensor_tensor(x_sb[:, t, :], x_sb[:, t, :], gam[:], ALU.mult).then_inc(times_gamma, 1)

            @block.scalar
            def _(act):
                def square(t):
                    act.wait_ge(x_in[t], 16)
                    if t:
                        act.wait_ge(squared, t)
                    nc.scalar.activation(squares[:], x_sb[:, t, :], ACT.Square,
                                         accum_out=ss[:, t:t + 1]).then_inc(squared, 1)

                def act_tile(t):
                    act.wait_ge(turned, t + 1)
                    nc.scalar.activation(act_hi[:, :, t * P:(t + 1) * P], tp[:, t % 2], ACT.Copy).then_inc(act_high, 1)

                for t in range(NT // 2):
                    square(t)
                act.dma_start(pw[:], pool_w.rearrange("g c d -> c g d")).then_inc(small[0], 16)
                with nc.allow_non_contiguous_dma(reason="a few scalars per channel"):
                    act.dma_start(scl[:], pool_scale.rearrange("(g p) -> p g", p=P)).then_inc(small[1], 16)
                    act.dma_start(cw[:], conv_w.rearrange("k (g p) -> p k g", p=P)).then_inc(small[2], 16)

                def high(m):
                    act.wait_ge(w_loaded[m % 2], 16 * (m // 2 + 1))
                    act.wait_ge(proj_ready, m + 1)
                    nc.scalar.activation(w_hi[:, m % 2], w[:, m % 2], ACT.Copy).then_inc(hi_done, 1)

                act.sem_inc(evacuated, 2)
                high(0)
                act_tile(0)
                high(1)
                for t in range(1, 4):
                    act_tile(t)
                    square(t + 3)
                square(7)
                for t in range(4, NT):
                    act_tile(t)
                act.wait_ge(small[0], 16)
                for m in range(N):
                    if 1 <= m < N - 1:
                        high(m + 1)
                    act.wait_ge(proj_ready, m + 3)
                    if m % 6 == 0:
                        act.wait_ge(mixed, m // 6 + 1)
                    nc.scalar.activation(dest[m % 6][:], proj[:, m % 2], ACT.Silu if m % 6 in (1, 5) else ACT.Copy
                                         ).then_inc(evacuated, 1)
                    if m % 6 == 0:
                        nc.scalar.activation(pw_hi[:], pw[:, m // 6], ACT.Copy).then_inc(pw_high, 1)

            @block.vector
            def _(dve):
                nc.vector.memset(ident[:], 0.0).then_inc(filled, 1)
                nc.vector.memset(mask[:], 0.0).then_inc(filled, 1)
                link = Chain(dve, chain)

                def low(m):
                    dve.wait_ge(hi_done, m + 1)
                    nc.vector.tensor_tensor(w_lo[:, m % 2], w[:, m % 2], f32(w_hi[:, m % 2]),
                                            ALU.subtract).then_inc(lo_done, 1)

                dve.sem_inc(lo_done, 2)
                dve.sem_inc(mixed, 1)
                dve.sem_inc(act_done, 2)

                def statistics(first, end):
                    ts = slice(first, end)
                    dve.wait_ge(squared, ts.stop)
                    link(nc.vector.tensor_scalar(ms[:, ts], ss[:, ts], 1.0 / D, EPS, ALU.mult, ALU.add))
                    rsqrt(nc, link, rstd[:, ts], tmp[:, ts], ms[:, ts])

                def norm(t):
                    if t >= NT // 2:
                        dve.wait_ge(times_gamma, t - NT // 2 + 1)
                        nc.vector.tensor_scalar(xn[:, t % 2], x_sb[:, t, :], rstd[:, t:t + 1], None,
                                                ALU.mult).then_inc(normed, 1)
                        return
                    nc.vector.scalar_tensor_tensor(xn[:, t % 2], x_sb[:, t, :], rstd[:, t:t + 1], gam[:],
                                                   ALU.mult, ALU.mult).then_inc(normed, 1)

                def act_low(t):
                    dve.wait_ge(act_high, t + 1)
                    cols = slice(t * P, (t + 1) * P)
                    nc.vector.tensor_tensor(act_lo[:, :, cols], tp[:, t % 2], f32(act_hi[:, :, cols]),
                                            ALU.subtract).then_inc(act_done, 1)

                statistics(0, 2)
                dve.wait_ge(gamma_in, 16)
                norm(0)
                norm(1)
                statistics(2, 4)
                for t in range(NT):
                    act_low(t)
                    if t == 3:
                        statistics(4, NT)
                        norm(4)
                    if t >= 3 or t < 2:
                        nxt = t + 2
                        if nxt < NT:
                            norm(nxt)
                dve.wait_ge(counted, 1)
                dve.wait_ge(small[1], 16)
                dve.wait_ge(small[2], 16)

                def pool_sums(g, m):
                    win = WINDOWS[g]
                    src, n = u, 0
                    step = 1
                    while step < win:
                        dst = sums[:, n % 2]
                        link(nc.vector.tensor_tensor(dst[:, step:], src[:, step:], src[:, :S - step], ALU.add))
                        link(nc.vector.tensor_copy(dst[:, :step], src[:, :step]))
                        src, n, step = dst, n + 1, 2 * step
                    low(m)
                    link(nc.vector.tensor_scalar(head[:, :win], count[:, :win], float(win), None, ALU.min))
                    link(nc.vector.reciprocal(inv[:, :win], head[:, :win]))
                    link(nc.vector.tensor_tensor(head[:, :win], src[:, :win], inv[:, :win], ALU.mult))
                    other = sums[:, n % 2]
                    link(nc.vector.scalar_tensor_tensor(other[:, win:], src[:, win:], 1.0 / win, u[:, win:],
                                                        ALU.mult, ALU.subtract))
                    link(nc.vector.tensor_tensor(other[:, :win], head[:, :win], u[:, :win], ALU.subtract))
                    link(nc.vector.tensor_copy(d_hi[:], other))
                    nc.vector.tensor_tensor(d_lo[:], other, f32(d_hi[:]), ALU.subtract).then_inc(d_ready, 1)

                def conv(g):
                    ch, acc = sums[:, 0], sums[:, 1]
                    dve.wait_ge(d_ready, g + 1)
                    link(nc.vector.tensor_tensor(ch, cb[:], hb[:], ALU.mult))
                    link(nc.vector.tensor_scalar(acc, ch, cw[:, 2, g:g + 1], None, ALU.mult))
                    for k in (1, 0):
                        lag = CONV_K - 1 - k
                        link(nc.vector.scalar_tensor_tensor(acc[:, lag:], ch[:, :S - lag], cw[:, k, g:g + 1],
                                                            acc[:, lag:], ALU.mult, ALU.add))
                    link(nc.vector.tensor_tensor(acc, acc, bb[:], ALU.mult))

                for m in range(N):
                    if 1 <= m < N - 1 and m % 6 != 2:
                        low(m + 1)
                    g = m // 6
                    dve.wait_ge(evacuated, m + 3)
                    if m % 6 == 1:
                        dve.wait_ge(pw_high, g + 1)
                        nc.vector.tensor_tensor(pw_lo[:], pw[:, g], f32(pw_hi[:]), ALU.subtract).then_inc(pw_done, 1)
                        pool_sums(g, m + 2)
                    if m % 6 == 4:
                        conv(g)
                        dve.wait_ge(pool_ready, g + 1)
                        nc.vector.scalar_tensor_tensor(y[:, g, :], pooled, scl[:, g:g + 1], za[:],
                                                       ALU.mult, ALU.mult)
                    if m % 6 == 5:
                        nc.vector.tensor_tensor(y[:, GROUPS + g, :], sums[:, 1], zb[:], ALU.mult).then_inc(mixed, 1)

            @block.tensor
            def _(pe):
                pe.sem_inc(proj_ready, 2)

                def transpose(t):
                    pe.wait_ge(normed, t + 1)
                    pe.wait_ge(act_done, t + 1)
                    for k in range(NK):
                        last = nc.tensor.transpose(tp[:, t % 2, k], xn[:, t % 2, k * P:(k + 1) * P], ident[:])
                    last.then_inc(turned, 1)

                def project(j, c, ks):
                    for k in ks:
                        cols = slice(c * BANK, (c + 1) * BANK)
                        last = three_passes(nc, proj[:, j % 2, cols], w_hi[:, j % 2, k], w_lo[:, j % 2, k],
                                            act_hi[:, k, cols], act_lo[:, k, cols], k == 0, k == NK - 1)
                    return last

                def project_group(g, j0):
                    for j in range(j0, 6):
                        m = 6 * g + j
                        pe.wait_ge(lo_done, m + 3)
                        pe.wait_ge(evacuated, m + 1)
                        for c in range(2):
                            last = project(j, c, range(NK))
                        last.then_inc(proj_ready, 1)
                        if j == 4:
                            pool_map(g)

                def pool_map(g):
                    pe.wait_ge(pw_done, g + 1)
                    pe.wait_ge(d_ready, g + 1)
                    pe.wait_ge(mixed, g + 1)
                    for c in range(2):
                        cols = slice(c * BANK, (c + 1) * BANK)
                        last = three_passes(nc, pooled[:, cols], pw_hi[:], pw_lo[:],
                                            d_hi[:, cols], d_lo[:, cols], True, True)
                    last.then_inc(pool_ready, 1)

                pe.wait_ge(shaped, 1)
                for t in range(NT // 2):
                    transpose(t)
                pe.wait_ge(act_done, NT // 2 + 2)
                for j in range(2):
                    pe.wait_ge(lo_done, j + 3)
                    for half in range(2):
                        project(j, 0, range(half * NK // 2, (half + 1) * NK // 2))
                        for t in ((4, 5), (6,), (7,), ())[2 * j + half]:
                            transpose(t)
                pe.wait_ge(act_done, NT + 2)
                for j in range(2):
                    project(j, 1, range(NK)).then_inc(proj_ready, 1)
                project_group(0, 2)
                with pe.Fori(1, GROUPS) as g:
                    project_group(g, 0)


class Weights:

    def __init__(self, nc, keep, name):
        self.nc = nc
        self.w = keep.enter_context(nc.sbuf_tensor(f"{name}_w", [P, 2, NK, P], F32))
        self.w_hi = keep.enter_context(nc.sbuf_tensor(f"{name}_w_hi", [P, 2, NK, P], F32R))
        self.w_lo = keep.enter_context(nc.sbuf_tensor(f"{name}_w_lo", [P, 2, NK, P], F32R))
        self.w_loaded = [keep.enter_context(nc.semaphore(f"{name}_w_loaded{n}")) for n in range(2)]
        self.hi_done = keep.enter_context(nc.semaphore(f"{name}_hi_done"))
        self.lo_done = keep.enter_context(nc.semaphore(f"{name}_lo_done"))

    def load(self, sp, w_in, m, slot, col):
        sp.wait_ge(self.lo_done, m + 1)
        sp.dma_start(self.w[:, slot], w_in.rearrange("(k p) n -> p k n", p=P)[:, :, col]).then_inc(
            self.w_loaded[slot], 16)

    def high(self, act, m, proj_ready=None):
        act.wait_ge(self.w_loaded[m % 2], 16 * (m // 2 + 1))
        if proj_ready is not None:
            act.wait_ge(proj_ready, m + 1)
        self.nc.scalar.activation(self.w_hi[:, m % 2], self.w[:, m % 2], ACT.Copy).then_inc(self.hi_done, 1)

    def low(self, dve, m):
        dve.wait_ge(self.hi_done, m + 1)
        self.nc.vector.tensor_tensor(self.w_lo[:, m % 2], self.w[:, m % 2], f32(self.w_hi[:, m % 2]),
                                     ALU.subtract).then_inc(self.lo_done, 1)


def output_projection(nc, name, features, res_dram, dest, w, w_hi, w_lo, w_in, norm=None, following=None):
    ctx, sb, ps, sem = phase(nc, name)
    with ctx:
        a_hi = sb("a_hi", [P, 2, NK, P], F32R)
        a_lo = sb("a_lo", [P, 2, NK, P], F32R)
        SLOTS = 3
        res = sb("res", [P, SLOTS, D])
        out = following[2] if following else ps("out", [P, 2, D])
        res_in = [sem(f"res_in{n}") for n in range(SLOTS)]
        w_high, w_done, a_high, a_done = sem("w_high"), sem("w_done"), sem("a_high"), sem("a_done")
        projected, added = sem("projected"), sem("added")
        stored = [sem(f"stored{n}") for n in range(SLOTS)]
        if norm:
            gamma, ident, act_hi, act_lo = norm
            gam = sb("gamma", [P, D])
            squares = sb("squares", [P, D])
            xn = sb("xn", [P, D])
            ss = sb("ss", [P, NT])
            ms = sb("ms", [P, NT])
            rstd = sb("rstd", [P, NT])
            tmp = sb("tmp", [P, NT])
            tp = ps("tp", [P, NK, P])
            gamma_in = sem("gamma_in")
            squared, scalars, normed = sem("squared"), sem("scalars"), sem("normed")
            turned, act_high, act_done = sem("turned"), sem("act_high"), sem("act_done")
        with nc.Block() as block:

            @block.sync
            def _(sp):
                def load(t):
                    n = t % SLOTS
                    sp.dma_start(res[:, n, :], res_dram[t * P:(t + 1) * P, :]).then_inc(res_in[n], 16)

                for t in range(SLOTS):
                    load(t)
                if following:
                    for m in range(2):
                        following[1].load(sp, following[0], m, m, slice(m * P, (m + 1) * P))
                for t in range(NT):
                    n = t % SLOTS
                    sp.wait_ge(added, t + 3)
                    sp.dma_start(dest[t * P:(t + 1) * P, :], res[:, n, :]).then_inc(stored[n], 16)
                    if t and t - 1 + SLOTS < NT:
                        before = t - 1
                        sp.wait_ge(stored[before % SLOTS], 16 * (before // SLOTS + 1))
                        if norm:
                            sp.wait_ge(normed, before + 1)
                        load(before + SLOTS)
                for n in range(SLOTS):
                    sp.wait_ge(stored[n], 16 * len(range(n, NT, SLOTS)))

            @block.scalar
            def _(act):
                if norm:
                    act.dma_start(gam[:], gamma.to_broadcast([P, D])).then_inc(gamma_in, 16)

                def split_features(t, ks=slice(0, NK)):
                    if t >= 2:
                        act.wait_ge(projected, t - 1)
                    nc.scalar.activation(a_hi[:, t % 2, ks], features[:, ks, t * P:(t + 1) * P],
                                         ACT.Copy).then_inc(a_high, 1)

                split_features(0, slice(0, NK // 2))
                for k in range(NK):
                    if k == 1:
                        split_features(0, slice(NK // 2, NK))
                    act.wait_ge(w_in, 16 * NK)
                    nc.scalar.activation(w_hi[:, k, :], w[:, k, :], ACT.Copy).then_inc(w_high, 1)
                split_features(1)
                for t in range(NT):
                    if norm:
                        act.wait_ge(added, t + 3)
                        if t:
                            act.wait_ge(squared, t)
                        nc.scalar.activation(squares[:], res[:, t % SLOTS, :], ACT.Square,
                                             accum_out=ss[:, t:t + 1]).then_inc(squared, 1)
                    if t + 2 < NT:
                        split_features(t + 2)
                    if norm:
                        act.wait_ge(turned, t + 1)
                        nc.scalar.activation(act_hi[:, :, t * P:(t + 1) * P], tp[:], ACT.Copy).then_inc(act_high, 1)
                    if following and t in (2, 3):
                        following[1].high(act, t - 2)

            @block.vector
            def _(dve):
                dve.sem_inc(added, 2)
                if following:
                    dve.sem_inc(following[1].lo_done, 2)

                def low_features(t, half=1):
                    ks = slice(0, NK) if t else slice(half * NK // 2, (half + 1) * NK // 2)
                    dve.wait_ge(a_high, t + half + 1)
                    nc.vector.tensor_tensor(a_lo[:, t % 2, ks], features[:, ks, t * P:(t + 1) * P],
                                            f32(a_hi[:, t % 2, ks]), ALU.subtract).then_inc(a_done, 1)

                low_features(0, 0)
                for k in range(NK):
                    if k == 1:
                        low_features(0, 1)
                    dve.wait_ge(w_high, k + 1)
                    nc.vector.tensor_tensor(w_lo[:, k, :], w[:, k, :], f32(w_hi[:, k, :]),
                                            ALU.subtract).then_inc(w_done, 1)
                low_features(1)
                if norm:
                    link = Chain(dve, scalars)
                    dve.wait_ge(gamma_in, 16)
                for t in range(NT):
                    n = t % SLOTS
                    dve.wait_ge(res_in[n], 16 * (t // SLOTS + 1))
                    dve.wait_ge(projected, t + 1)
                    nc.vector.tensor_tensor(res[:, n, :], out[:, t % 2, :], res[:, n, :], ALU.add).then_inc(added, 1)
                    if norm:
                        one = slice(t, t + 1)
                        dve.wait_ge(squared, t + 1)
                        link(nc.vector.tensor_scalar(ms[:, one], ss[:, one], 1.0 / D, EPS, ALU.mult, ALU.add))
                        rsqrt(nc, link, rstd[:, one], tmp[:, one], ms[:, one])
                        nc.vector.scalar_tensor_tensor(xn[:], res[:, n, :], rstd[:, one], gam[:],
                                                       ALU.mult, ALU.mult).then_inc(normed, 1)
                    if t + 2 < NT:
                        low_features(t + 2)
                    if norm:
                        dve.wait_ge(act_high, t + 1)
                        cols = slice(t * P, (t + 1) * P)
                        nc.vector.tensor_tensor(act_lo[:, :, cols], tp[:], f32(act_hi[:, :, cols]),
                                                ALU.subtract).then_inc(act_done, 1)
                    if following and t in (2, 3):
                        following[1].low(dve, t - 2)

            @block.tensor
            def _(pe):
                def transpose(t):
                    pe.wait_ge(normed, t + 1)
                    if t:
                        pe.wait_ge(act_done, t)
                    for k in range(NK):
                        last = nc.tensor.transpose(tp[:, k], xn[:, k * P:(k + 1) * P], ident[:])
                    last.then_inc(turned, 1)

                for t in range(NT):
                    pe.wait_ge(a_done, t + 2 if t else 1)
                    pe.wait_ge(added, t + 1)
                    for k in range(NK):
                        if t == 0 and k == NK // 2:
                            pe.wait_ge(a_done, 2)
                        if t == 0:
                            pe.wait_ge(w_done, k + 1)
                        if norm and t and k == NK - 2:
                            transpose(t - 1)
                        for c in range(2):
                            cols = slice(c * BANK, (c + 1) * BANK)
                            last = three_passes(nc, out[:, t % 2, cols], a_hi[:, t % 2, k], a_lo[:, t % 2, k],
                                                w_hi[:, k, cols], w_lo[:, k, cols], k == 0, k == NK - 1)
                    last.then_inc(projected, 1)
                if following:
                    early, ps_next = following[1], following[2]
                    pe.wait_ge(act_done, NT // 2)
                    for m in range(2):
                        pe.wait_ge(early.lo_done, m + 3)
                        pe.wait_ge(added, NT + 1 + m)
                        for k in range(NK):
                            if m and k == 3:
                                transpose(NT - 1)
                            three_passes(nc, ps_next[:, m, :BANK], early.w_hi[:, m, k], early.w_lo[:, m, k],
                                         act_hi[:, k, :BANK], act_lo[:, k, :BANK], k == 0, k == NK - 1)


def latent_projection(nc, w_in, positions, q_lat_g, kv_lat_g, q_head_g, k_head_g, ident, act_hi, act_lo,
                      latent, gate, rms_qkv, q_tab, k_rope, k_rope_ss, weights, proj, w_ukv, w_next, w_next_in):
    ctx, sb, ps, sem = phase(nc, "lat")
    with ctx:
        w_hi, w_lo, lo_done = weights.w_hi, weights.w_lo, weights.lo_done
        gam = sb("gam", [P, KQ + KKV])
        squares = sb("squares", [P, S])
        sq = sb("sq", [P, 2, S])
        krt = sb("krt", [P, S])
        ones = sb("ones", [P, 2])
        ms = sb("ms", [P, 2, NT])
        tmp = sb("tmp", [P, 2, NT])
        pos_i = sb("pos_i", [P, NT], I32)
        pos = sb("pos", [P, NT])
        freq = sb("freq", [P, HALF])
        head_g = sb("head_g", [P, 2, ROPE])
        ang = sb("ang", [P, NT, HALF])
        turns = sb("turns", [P, NT, HALF])
        red = sb("red", [P, 2, NT, HALF])
        trig = sb("trig", [P, 2, NT, HALF])
        kr = sb("kr", [P, NT, ROPE])
        ktab = sb("ktab", [P, 4, NT, HALF])
        prod = sb("prod", [P, 4, NT, HALF])
        kr2 = sb("kr2", [P, NT, ROPE])
        small_ps = ps("small", [P, BANK])
        turned_ps = ps("turned", [P, NT, ROPE])
        gam_in = [sem("gam_in0"), sem("gam_in1")]
        small_in = [sem(f"small_in{n}") for n in range(3)]
        proj_ready, evacuated = sem("proj_ready"), sem("evacuated")
        chain, freq_set, reduced, trig_done = sem("chain"), sem("freq_set"), sem("reduced"), sem("trig_done")
        squared, summed, ones_set, small_ready, kr_out = (
            sem("squared"), sem("summed"), sem("ones_set"), sem("small_ready"), sem("kr_out"))
        LAT = KQ + KKV
        N = LAT + 1 + NK

        with nc.Block() as block:

            @block.sync
            def _(sp):
                with sp.Fori(1, LAT // 2) as i:
                    for e in range(2):
                        weights.load(sp, w_in, 2 * i + e, e, bass.ds(sp.snap(i * 2 * P + e * P), P))
                for k in range(KKV):
                    sp.dma_start(w_next[:, k, :], w_ukv[k * P:(k + 1) * P, :]).then_inc(w_next_in, 16)
                weights.load(sp, w_in, LAT, 0, slice(LAT * P, LAT * P + P))
                with sp.Fori(0, NK // 2) as i:
                    for e in range(2):
                        weights.load(sp, w_in, 2 * i + LAT + 1 + e, 1 - e, bass.ds(sp.snap(i * 2 * P + Z_COL + e * P), P))

            @block.gpsimd
            def _(pool):
                for j in range(HALF):
                    f = float(np.float32(THETA ** (-2.0 * j / ROPE)))
                    nc.gpsimd.memset(freq[:, j:j + 1], f).then_inc(freq_set, 1)
                nc.gpsimd.memset(ones[:], 1.0).then_inc(ones_set, 1)
                for n, m in enumerate([1, 2, 3, 4, 5, 7]):
                    if n:
                        pool.wait_ge(summed, n)
                    pool.wait_ge(squared, m + 1)
                    total = sq[:, 0 if m < KQ else 1, :]
                    nc.gpsimd.tensor_tensor(total, total, squares[:], ALU.add).then_inc(summed, 1)

            @block.scalar
            def _(act):
                act.sem_inc(evacuated, 2)
                with nc.allow_non_contiguous_dma(reason="a few scalars per channel or token"):
                    act.dma_start(gam[:, :KQ], q_lat_g.rearrange("(k p) -> p k", p=P)).then_inc(gam_in[0], 16)
                    act.dma_start(gam[:, KQ:], kv_lat_g.rearrange("(k p) -> p k", p=P)).then_inc(gam_in[1], 16)
                    act.dma_start(pos_i[:], positions.rearrange("(t p) -> p t", p=P)).then_inc(small_in[0], 16)
                act.dma_start(head_g[:, 0], q_head_g[:, NOPE:].to_broadcast([P, ROPE])).then_inc(small_in[1], 16)
                act.dma_start(head_g[:, 1], k_head_g[:, NOPE:].to_broadcast([P, ROPE])).then_inc(small_in[2], 16)
                act.wait_ge(gam_in[0], 16)
                act.wait_ge(gam_in[1], 16)
                for m in range(N):
                    if 1 <= m < N - 1:
                        weights.high(act, m + 1, proj_ready)
                    act.wait_ge(proj_ready, m + 3)
                    src = proj[:, m % 2]
                    if m < LAT:
                        nc.scalar.activation(latent[:, m, :], src, ACT.Copy, scale=gam[:, m:m + 1])
                        if m in (0, KQ):
                            sq_dst = sq[:, 0 if m == 0 else 1, :]
                        else:
                            sq_dst = squares[:]
                            before = m - 1 if m < KQ else m - 2
                            if before:
                                act.wait_ge(summed, before)
                        nc.scalar.activation(sq_dst, src, ACT.Square).then_inc(squared, 1)
                        act.wait_ge(squared, m + 1)
                        act.sem_inc(evacuated, 1)
                        if m == 2:
                            act.wait_ge(reduced, 2)
                            nc.scalar.activation(trig[:], red[:], ACT.Sin).then_inc(trig_done, 1)
                    elif m == LAT:
                        nc.scalar.activation(krt[0:ROPE, :], src[0:ROPE, :], ACT.Copy).then_inc(evacuated, 1)
                    else:
                        nc.scalar.activation(gate[:, m - LAT - 1, :], src, ACT.Silu).then_inc(evacuated, 1)

            @block.vector
            def _(dve):
                link = Chain(dve, chain)

                def by_token(ap):
                    return ap.unsqueeze(1).to_broadcast([P, NT, HALF])

                dve.wait_ge(small_in[0], 16)
                dve.wait_ge(freq_set, HALF)
                link(nc.vector.tensor_copy(pos[:], pos_i[:]))
                link(nc.vector.tensor_tensor(ang[:], pos[:].unsqueeze(2).to_broadcast([P, NT, HALF]),
                                             by_token(freq[:]), ALU.mult))
                for which, quarter in ((0, 0.0), (1, 0.25)):
                    r = red[:, which]
                    link(nc.vector.tensor_scalar(turns[:], ang[:], TURN, quarter, ALU.mult, ALU.add))
                    link(nc.vector.tensor_scalar(turns[:], turns[:], ROUND, ROUND, ALU.add, ALU.subtract))
                    link(nc.vector.scalar_tensor_tensor(r, turns[:], -TWO_PI[0], ang[:], ALU.mult, ALU.add))
                    for part in TWO_PI[1:]:
                        link(nc.vector.scalar_tensor_tensor(r, turns[:], -part, r, ALU.mult, ALU.add))
                    if which:
                        link(nc.vector.tensor_scalar(r, r, float(np.float32(np.pi / 2)), None, ALU.add))
                    link(nc.vector.tensor_scalar(r, r, PI, -PI, ALU.min, ALU.max))
                    dve.sem_inc(reduced, 1)
                    weights.low(dve, 2 + which)
                dve.wait_ge(trig_done, 1)
                dve.wait_ge(small_in[1], 16)
                dve.wait_ge(small_in[2], 16)
                sin, cos = trig[:, 0], trig[:, 1]
                for which, tab in ((0, q_tab), (1, ktab)):
                    g1, g2 = head_g[:, which, :HALF], head_g[:, which, HALF:]
                    for n, (g, f) in enumerate(((g1, cos), (g2, sin), (g1, sin), (g2, cos))):
                        link(nc.vector.tensor_tensor(tab[:, n], f, by_token(g), ALU.mult))
                for m in range(4, LAT + 6):
                    weights.low(dve, m)
                dve.wait_ge(small_ready, 1)
                for n, width in ((0, Q_LORA), (1, KV_LORA)):
                    link(nc.vector.tensor_scalar(ms[:, n], small_ps[:, n * NT:(n + 1) * NT], 1.0 / width, EPS,
                                                 ALU.mult, ALU.add))
                rsqrt(nc, link, rms_qkv[:], tmp[:], ms[:])
                link(nc.vector.tensor_copy(kr[:], turned_ps[:]))
                link(nc.vector.tensor_tensor(kr2[:], kr[:], kr[:], ALU.mult))
                link(nc.vector.tensor_reduce(k_rope_ss[:], kr2[:], AX_X, ALU.add))
                link(nc.vector.tensor_scalar(k_rope_ss[:], k_rope_ss[:], QKH * EPS, None, ALU.add))
                x1, x2 = kr[:, :, :HALF], kr[:, :, HALF:]
                for n, x in enumerate((x1, x2, x1, x2)):
                    link(nc.vector.tensor_tensor(prod[:, n], x, ktab[:, n], ALU.mult))
                link(nc.vector.tensor_tensor(k_rope[:, :, :HALF], prod[:, 0], prod[:, 1], ALU.subtract))
                link(nc.vector.tensor_tensor(k_rope[:, :, HALF:], prod[:, 2], prod[:, 3], ALU.add))
                for m in range(LAT + 6, N):
                    weights.low(dve, m)

            @block.tensor
            def _(pe):
                def tile(m, slot, chunks=range(2)):
                    pe.wait_ge(lo_done, m + 3)
                    pe.wait_ge(evacuated, m + 1)
                    for c in chunks:
                        for k in range(NK):
                            cols = slice(c * BANK, (c + 1) * BANK)
                            last = three_passes(nc, proj[:, slot, cols], w_hi[:, slot, k], w_lo[:, slot, k],
                                                act_hi[:, k, cols], act_lo[:, k, cols], k == 0, k == NK - 1)
                    last.then_inc(proj_ready, 1)

                pe.sem_inc(proj_ready, 2)
                for m in range(2):
                    tile(m, m, (1,))
                with pe.Fori(1, LAT // 2) as i:
                    for e in range(2):
                        tile(2 * i + e, e)
                for j in range(3):
                    tile(LAT + j, j % 2)
                pe.wait_ge(ones_set, 1)
                pe.wait_ge(summed, LAT - 2)
                for n in range(2):
                    for t in range(NT):
                        col = n * NT + t
                        nc.tensor.matmul(small_ps[:, col:col + 1], sq[:, n, t * P:(t + 1) * P], ones[:, 0:1],
                                         start=True, stop=True)
                for t in range(NT):
                    last = nc.tensor.transpose(turned_ps[:, t], krt[0:ROPE, t * P:(t + 1) * P],
                                               ident[0:ROPE, 0:ROPE])
                last.then_inc(small_ready, 1)
                with pe.Fori(1, NK // 2) as i:
                    for e in range(2):
                        tile(2 * i + LAT + 1 + e, 1 - e)


TURN = float(np.float32(1.0 / (2.0 * np.pi)))
ROUND = float(1.5 * 2 ** 23)
PI = float(np.nextafter(np.float32(np.pi), np.float32(0)))


def _two_pi_parts():
    parts, rest = [], 2.0 * np.pi
    for bits in (8, 11):
        unit = 2.0 ** (np.floor(np.log2(rest)) - bits + 1)
        parts.append(float(np.floor(rest / unit) * unit))
        rest -= parts[-1]
    return parts + [float(np.float32(rest))]


TWO_PI = _two_pi_parts()


def head_projections(nc, w_kv, w_kv_lo, w_kv_at, w_kv_in, w_uq, latent, rms_qkv, q_tab, k_rope, k_rope_ss,
                     q_head_g, k_head_g, gqk, q_d, k_d, v_d, q_stored, stages, loaded):
    ctx, sb, ps, sem = phase(nc, "heads")
    with ctx:
        EARLY = KQ - 2
        STEPS = 2 * NT

        def shared(name, like, blocks, dt):
            return nc.alloc_sbuf_tensor_at(name, [P, blocks, Q_COLS], dt, offset=like)

        at = -(-nc.sbuf_base // 32) * 32
        sb("uq_place", [P, EARLY, Q_COLS])
        uq = nc.alloc_sbuf_tensor_at("uq", [P, EARLY, Q_COLS], F32, offset=at)
        uq_lo = nc.alloc_sbuf_tensor_at("uq_lo", [P, EARLY, Q_COLS], F32R, offset=at)
        uq_hi = sb("uq_hi", [P, EARLY, Q_COLS], F32R)
        a_hi = sb("a_hi", [P, 2, KQ, P], F32R)
        a_lo = sb("a_lo", [P, 2, KQ, P], F32R)
        RING = 4
        x = sb("x", [P, RING, HEADS, QKH])
        assert nc.sbuf_base <= w_kv_at, (nc.sbuf_base, w_kv_at)
        if w_kv_at > nc.sbuf_base:
            sb("gap", [P, (w_kv_at - nc.sbuf_base) // 4])
        sb("kv_place", [P, KKV, KV_COLS])
        kv_hi_at = -(-nc.sbuf_base // 32) * 32
        sb("kv_hi_place", [P, KKV, KV_COLS])
        w_kv_hi = nc.alloc_sbuf_tensor_at("w_kv_hi", [P, KKV, KV_COLS], F32R, offset=kv_hi_at)
        late = shared("uq_late", w_kv_at, KQ - EARLY, F32)
        late_lo = shared("uq_late_lo", w_kv_at, KQ - EARLY, F32R)
        late_hi = shared("uq_late_hi", kv_hi_at, KQ - EARLY, F32R)
        v = sb("v", [P, 2, HEADS, VH])
        sq = sb("sq", [P, HEADS * QKH])
        ss = sb("ss", [P, HEADS])
        rs = sb("rs", [P, 2, HEADS])
        tmp = sb("tmp", [P, HEADS])
        prod = v[:, 0].rearrange("p h d -> p (h d)").rearrange("p (n h d) -> p n h d", n=4, h=HEADS)
        out = ps("out", [P, 2, 4, BANK])
        uq_in = [sem(f"uq_in{k}") for k in range(KQ)]
        kv_high, kv_done = sem("kv_high"), sem("kv_done")
        uq_high, uq_done, late_done = sem("uq_high"), sem("uq_done"), sem("late_done")
        a_high, a_done = sem("a_high"), sem("a_done")
        projected, squared, v_done = sem("projected"), sem("squared"), sem("v_done")
        k_done = sem("k_done")
        chain, reduced = sem("chain"), sem("reduced")
        scaled, q_scaled = sem("scaled"), sem("q_scaled")
        turned, multiplied, half_read = sem("turned"), sem("multiplied"), sem("half_read")
        q_first, q_copied = sem("q_first"), sem("q_copied")
        x_stored = [sem(f"x_stored{e}") for e in range(RING)]
        g_in, g_made = [sem("g_in0"), sem("g_in1")], sem("g_made")
        v_stored = [sem(f"v_stored{e}") for e in range(2)]
        half = KV_COLS // 2

        def features(n):
            t = n % NT
            lo, hi = (KQ, KQ + KKV) if n < NT else (0, KQ)
            return latent[:, lo:hi, t * P:(t + 1) * P], slice(0, hi - lo)

        def head_part(n):
            if n < NT:
                return out[:, n % 2].rearrange("p b c -> p (b c)").rearrange("p (h d) -> p h d", h=HEADS)[:, :, :NOPE]
            return out[:, n % 2, :3].rearrange("p b c -> p (b c)").rearrange("p (h d) -> p h d", h=HEADS)

        def squares(n):
            w = NOPE if n < NT else QKH
            return sq[:, :HEADS * w].rearrange("p (h d) -> p h d", h=HEADS)

        def products(eng, link, n, js):
            for j in js:
                ins = eng.tensor_tensor(prod[:, j], x[:, n % RING, :, NOPE + j % 2 * HALF:NOPE + (j % 2 + 1) * HALF],
                                        q_tab[:, j, n - NT, :].unsqueeze(1).to_broadcast([P, HEADS, HALF]), ALU.mult)
            link(ins)

        def sums(eng, link, n, halves):
            for j in halves:
                ins = eng.tensor_tensor(x[:, n % RING, :, NOPE + j * HALF:NOPE + (j + 1) * HALF], prod[:, 2 * j],
                                        prod[:, 2 * j + 1], ALU.add if j else ALU.subtract)
            link(ins)

        def rms(n):
            return rms_qkv[:, 1 if n < NT else 0, n % NT:n % NT + 1]

        with nc.Block() as block:

            @block.sync
            def _(sp):
                for k in range(EARLY):
                    sp.dma_start(uq[:, k, :], w_uq[k * P:(k + 1) * P, :]).then_inc(uq_in[k], 16)
                with nc.allow_non_contiguous_dma(reason="a few scalars per channel"):
                    sp.dma_start(gqk[0:QKH, 0:1], q_head_g.rearrange("a d -> d a")).then_inc(g_in[0], 16)
                    sp.dma_start(gqk[0:QKH, 1:2], k_head_g.rearrange("a d -> d a")).then_inc(g_in[1], 16)
                for n in range(STEPS):
                    t, e = n % NT, n % 2
                    if n == STEPS - 1:
                        for slot in range(RING):
                            sp.wait_ge(x_stored[slot], 16 * len(range(slot, STEPS - 1, RING)))
                        for slot in range(2):
                            sp.wait_ge(v_stored[slot], 16 * (NT // 2))
                        sp.wait_ge(projected, STEPS + 2)
                        k_st, q_st, v_st = (stages[name] for name in "kqv")
                        sp.dma_start(k_st[:], by_tile(k_d)[:, :, :2 * QKH]).then_inc(loaded["k"], 16)
                        sp.dma_start(q_st[:, :NT - 1], by_tile(q_d)[:, :NT - 1, :2 * QKH]).then_inc(q_first, 16)
                        sp.dma_start(v_st[:], by_tile(v_d)[:, :, :2 * VH]).then_inc(loaded["v"], 16)
                    sp.wait_ge(turned, n + 1 + (n == STEPS - 1))
                    dest, flat = k_d if n < NT else q_d, x[:, n % RING].rearrange("p h d -> p (h d)")
                    if n == STEPS - 1:
                        sp.dma_start(dest[t * P:(t + 1) * P, :], flat).then_inc(q_stored, 16)
                        continue
                    sp.dma_start(dest[t * P:(t + 1) * P, :], flat).then_inc(x_stored[n % RING], 16)
                    if n < NT:
                        sp.dma_start(v_d[t * P:(t + 1) * P, :],
                                     v[:, e].rearrange("p h d -> p (h d)")).then_inc(v_stored[e], 16)
                sp.wait_ge(q_first, 16)
                sp.sem_inc(loaded["q"], 16)

            @block.scalar
            def _(act):
                def split_features(n):
                    if n >= 2:
                        act.wait_ge(projected, n + 1)
                    src, ks = features(n)
                    nc.scalar.activation(a_hi[:, n % 2, ks], src, ACT.Copy).then_inc(a_high, 1)

                act.sem_inc(k_done, 2)
                split_features(0)
                for k in range(KKV):
                    act.wait_ge(w_kv_in, 16 * KKV)
                    for c in range(2):
                        cols = slice(c * half, (c + 1) * half)
                        nc.scalar.activation(w_kv_hi[:, k, cols], w_kv[:, k, cols], ACT.Copy).then_inc(kv_high, 1)
                split_features(1)
                for n in range(STEPS):
                    if n == NT:
                        for k in range(EARLY, KQ):
                            act.wait_ge(uq_in[k], 16)
                            nc.scalar.activation(late_hi[:, k - EARLY, :], late[:, k - EARLY, :],
                                                 ACT.Copy).then_inc(uq_high, 1)
                    act.wait_ge(projected, n + 3)
                    if n == NT - 1:
                        for k in range(EARLY, KQ):
                            act.dma_start(late[:, k - EARLY, :], w_uq[k * P:(k + 1) * P, :]).then_inc(uq_in[k], 16)
                    if n + 2 < STEPS:
                        split_features(n + 2)
                    if n:
                        act.wait_ge(reduced, n)
                    nc.scalar.activation(squares(n), head_part(n), ACT.Square, scale=rms(n)).then_inc(squared, 1)
                    if n < NT:
                        if n >= 2:
                            act.wait_ge(v_stored[n % 2], 16 * (n // 2))
                        kv = out[:, n % 2].rearrange("p b c -> p (b c)").rearrange("p (h d) -> p h d", h=HEADS)
                        nc.scalar.activation(v[:, n % 2], kv[:, :, NOPE:], ACT.Copy, scale=rms(n)).then_inc(v_done, 1)
                        if n >= RING:
                            act.wait_ge(x_stored[n % RING], 16 * (n // RING))
                        nc.scalar.activation(x[:, n % RING, :, :NOPE], kv[:, :, :NOPE], ACT.Copy,
                                             scale=rms(n)).then_inc(k_done, 1)
                    if 1 <= n <= EARLY:
                        act.wait_ge(uq_in[n - 1], 16)
                        nc.scalar.activation(uq_hi[:, n - 1, :], uq[:, n - 1, :], ACT.Copy).then_inc(uq_high, 1)
                act.wait_ge(turned, STEPS + 1)
                nc.scalar.activation(stages["q"][:, NT - 1], x[:, (STEPS - 1) % RING, :2].rearrange("p h d -> p (h d)"),
                                     ACT.Copy).then_inc(q_copied, 1)
                act.wait_ge(q_copied, 1)

            @block.vector
            def _(dve):
                link = Chain(dve, chain)
                dve.sem_inc(q_scaled, 2)

                def low_features(n):
                    dve.wait_ge(a_high, n + 1)
                    src, ks = features(n)
                    nc.vector.tensor_tensor(a_lo[:, n % 2, ks], src, f32(a_hi[:, n % 2, ks]),
                                            ALU.subtract).then_inc(a_done, 1)

                low_features(0)
                for k in range(KKV):
                    for c in range(2):
                        cols = slice(c * half, (c + 1) * half)
                        dve.wait_ge(kv_high, 2 * k + c + 1)
                        nc.vector.tensor_tensor(w_kv_lo[:, k, cols], w_kv[:, k, cols], f32(w_kv_hi[:, k, cols]),
                                                ALU.subtract).then_inc(kv_done, 1)
                low_features(1)
                for n in range(STEPS):
                    if n == NT:
                        for k in range(EARLY, KQ):
                            dve.wait_ge(uq_high, k + 1)
                            nc.vector.tensor_tensor(late_lo[:, k - EARLY, :], late[:, k - EARLY, :],
                                                    f32(late_hi[:, k - EARLY, :]), ALU.subtract).then_inc(late_done, 1)
                    dve.wait_ge(squared, n + 1)
                    nc.vector.tensor_reduce(ss[:], squares(n), AX_X, ALU.add).then_inc(reduced, 1)
                    if n + 2 < STEPS:
                        low_features(n + 2)
                    dve.wait_ge(reduced, n + 1)
                    if n < NT:
                        link(nc.vector.tensor_scalar(ss[:], ss[:], k_rope_ss[:, n:n + 1], 1.0 / QKH,
                                                     ALU.add, ALU.mult))
                    else:
                        link(nc.vector.tensor_scalar(ss[:], ss[:], 1.0 / QKH, EPS, ALU.mult, ALU.add))
                    e = n % 2
                    if n >= 2:
                        dve.wait_ge(turned, n - 1)
                    rsqrt(nc, link, rs[:, e], tmp[:], ss[:])
                    at = rs[:, e].unsqueeze(2)
                    if n < NT:
                        dve.wait_ge(k_done, n + 3)
                        k = x[:, n % RING, :, :NOPE]
                        nc.vector.tensor_tensor(k, k, at.to_broadcast([P, HEADS, NOPE]), ALU.mult).then_inc(scaled, 1)
                    else:
                        dve.wait_ge(x_stored[n % RING], 16 * (n // RING))
                        nc.vector.scalar_tensor_tensor(x[:, n % RING], head_part(n), rms(n),
                                                       at.to_broadcast([P, HEADS, QKH]),
                                                       ALU.mult, ALU.mult).then_inc(q_scaled, 1)
                    if n == 2:
                        dve.wait_ge(g_in[0], 16)
                        dve.wait_ge(g_in[1], 16)
                        nc.vector.tensor_tensor(gqk[0:NOPE, 1:2], gqk[0:NOPE, 0:1], gqk[0:NOPE, 1:2], ALU.mult)
                        nc.vector.memset(gqk[NOPE:QKH, 1:2], 1.0)
                dve.wait_ge(q_scaled, NT + 2)
                dve.wait_ge(turned, STEPS - 1)
                products(nc.vector, link, STEPS - 1, (2, 3))
                dve.sem_inc(half_read, 1)
                dve.wait_ge(half_read, 2)
                sums(nc.vector, link, STEPS - 1, (1,))
                dve.sem_inc(turned, 1)

            @block.gpsimd
            def _(pool):
                link = Chain(pool, multiplied)
                for n in range(NT):
                    pool.wait_ge(scaled, n + 1)
                    e = n % 2
                    nc.gpsimd.tensor_tensor(
                        x[:, n % RING, :, NOPE:], k_rope[:, n, :].unsqueeze(1).to_broadcast([P, HEADS, ROPE]),
                        rs[:, e].unsqueeze(2).to_broadcast([P, HEADS, ROPE]), ALU.mult).then_inc(turned, 1)
                    if 1 <= n <= EARLY:
                        pool.wait_ge(uq_high, n)
                        nc.gpsimd.tensor_tensor(uq_lo[:, n - 1, :], uq[:, n - 1, :], f32(uq_hi[:, n - 1, :]),
                                                ALU.subtract).then_inc(uq_done, 1)
                pool.wait_ge(v_stored[0], 16 * (NT // 2))
                for n in range(NT, STEPS):
                    pool.wait_ge(q_scaled, n - NT + 3)
                    if n == STEPS - 1:
                        products(nc.gpsimd, link, n, (0, 1))
                        pool.sem_inc(half_read, 1)
                        pool.wait_ge(half_read, 2)
                        sums(nc.gpsimd, link, n, (0,))
                        pool.sem_inc(turned, 1)
                        continue
                    products(nc.gpsimd, link, n, range(4))
                    sums(nc.gpsimd, link, n, range(2))
                    pool.sem_inc(turned, 1)

            @block.tensor
            def _(pe):
                pe.sem_inc(projected, 2)

                def step(n, e, nk, banks, ready, w_hi, w_lo):
                    pe.wait_ge(a_done, n + 1)
                    for k in range(nk):
                        for c in range(banks):
                            cc = slice(c * BANK, (c + 1) * BANK)
                            ready(k, c)
                            last = three_passes(nc, out[:, e, c], a_hi[:, e, k], a_lo[:, e, k],
                                                w_hi(k, cc), w_lo(k, cc), k == 0, k == nk - 1)
                    last.then_inc(projected, 1)

                def kv_ready(k, c):
                    if c % 2 == 0:
                        pe.wait_ge(kv_done, 2 * k + c // 2 + 1)

                def uq_ready(k, c):
                    if c == 0 and k < EARLY:
                        pe.wait_ge(uq_done, k + 1)
                    elif c == 0:
                        pe.wait_ge(late_done, k - EARLY + 1)

                with pe.Fori(0, NT // 2) as i:
                    for e in range(2):
                        pe.wait_ge(k_done, 2 * i + e + 1)
                        step(2 * i + e, e, KKV, 4, kv_ready,
                             lambda k, cc: w_kv_hi[:, k, cc], lambda k, cc: w_kv_lo[:, k, cc])
                with pe.Fori(NT // 2, NT) as i:
                    for e in range(2):
                        pe.wait_ge(k_done, NT + 1 + e)
                        pe.wait_ge(q_scaled, 2 * i + e - NT + 1)
                        step(2 * i + e, e, KQ, 3, uq_ready,
                             lambda k, cc: uq_hi[:, k, cc] if k < EARLY else late_hi[:, k - EARLY, cc],
                             lambda k, cc: uq_lo[:, k, cc] if k < EARLY else late_lo[:, k - EARLY, cc])


def attention(nc, q_d, k_d, v_d, q_stored, gqk, stages, loaded, ident, mask, gate, w_out, w_next, w_next_in):
    ctx, sb, ps, sem = phase(nc, "att")
    with ctx:
        sb("stages_place", [P, NT, 2 * (QKH + QKH + VH)])
        q_st, k_st, v_st = (stages[name] for name in "qkv")
        t_hi = [[sb(f"{n}t_hi{e}", [P, S], F32R) for n in "qk"] for e in range(2)]
        t_lo = [[sb(f"{n}t_lo{e}", [P, S], F32R) for n in "qk"] for e in range(2)]
        v2 = [sb(f"v2{e}", [P, NT, 2 * VH], F32R) for e in range(2)]
        neg_max = sb("neg_max", [P, 2, NT])
        total = sb("total", [P, 2, NT])
        inv = sb("inv", [P, 2, NT])
        probs = [[sb(f"probs{c}{e}", [P, 4, (c + 1) * BANK]) for e in range(2)] for c in range(2)]
        pt_hi = sb("pt_hi", [P, 3, BANK], F32R)
        pt_lo = sb("pt_lo", [P, 3, BANK], F32R)
        o_part = sb("o_part", [P, BANK])
        carrier = sb("carrier", [P, 4])
        o_sum = sb("o_sum", [P, 2, BANK])
        s_ps = ps("s_ps", [P, 2, S])
        pt_ps = ps("pt_ps", [P, 3, BANK])
        o_ps = ps("o_ps", [P, BANK])
        s_ready = sem("s_ready")
        s_free = sem("s_free")
        half_ready = sem("half_ready")
        half_free = sem("half_free")
        t_high = sem("t_high")
        v_high, v_low = sem("v_high"), sem("v_low")
        exp_done, inv_done, p_ready = sem("exp_done"), sem("inv_done"), sem("p_ready")
        pt_ready, pt_high = sem("pt_ready"), sem("pt_high")
        pt_low = sem("pt_low")
        pv_done = sem("pv_done")
        o_copied = sem("o_copied")
        o_summed = sem("o_summed")
        gated = sem("gated")
        LAST = HEADS - 1

        def rows(e):
            return slice(e * VH, (e + 1) * VH)

        def is_head(h, n):
            return isinstance(h, int) and h == n

        def ring(h, p):
            if p >= 4 and not is_head(h, LAST):
                return 10 * h + 4 + p
            if is_head(h, 0):
                return 4 + p
            return 10 * h + ((2, 4, 6, 7)[p] if not is_head(h, LAST) else 2 + p)

        def slot(h, p):
            return p % 2 if p >= 4 or is_head(h, 0) or is_head(h, LAST) else (0, 0, 0, 1)[p]

        def alone(h, p):
            return p in (1, 2) and not is_head(h, 0) and not is_head(h, LAST)

        def scores(h, p, lo, hi):
            at = BANK if p == 1 and alone(h, p) else 0
            return s_ps[:, slot(h, p), at + lo:at + hi]

        def ring_q(h):
            return 2 * h if isinstance(h, int) and h < 2 else 10 * h - 7

        def ring_k(h):
            return 2 * h + 1 if isinstance(h, int) and h < 2 else 10 * h - 5

        def slot_q(h):
            return 0 if isinstance(h, int) and h < 2 else 1

        def walk(w, Fori):

            def scores_1(h, e, pair):
                g, o = h - 1, 1 - e
                products = not is_head(h, 0)
                w.tile(h, e, 4)
                if products:
                    w.split_v(h, e)
                    w.turn(g, o, 1, 2)
                    w.product(g, o, 1, 0)
                w.tile(h, e, 5)
                if products:
                    w.gating(g, o, 0, pair)
                    for j in range(1, 3):
                        w.turn(g, o, 1, j + 2)
                        w.product(g, o, 1, j)
                w.tile(h, e, 6)
                if products:
                    for j in range(3, 5):
                        w.turn(g, o, 1, j + 2)
                        w.product(g, o, 1, j)
                w.tile(h, e, 7)
                if products:
                    w.turn(g, o, 1, 7)
                    w.product(g, o, 1, 5)
                    w.product(g, o, 1, 6)
                w.turn(h, e, 0, 0)
                if products:
                    w.product(g, o, 1, 7)
                    w.output(g, o, 1)
                w.turn(h, e, 0, 1)

            def scores_0(h, e, pair, new_head=True):
                w.tile(h + 1, 1 - e, 0)
                w.turn(h, e, 0, 2)
                if new_head:
                    w.turn_q(h + 2, e)
                w.close(h, e)
                w.product(h, e, 0, 0)
                w.turn(h, e, 0, 3)
                w.product(h, e, 0, 1)
                w.tile(h + 1, 1 - e, 1)
                w.product(h, e, 0, 2)
                if new_head:
                    w.turn_k(h + 2, e)
                w.product(h, e, 0, 3)
                w.tile(h + 1, 1 - e, 2)
                w.output(h, e, 0)
                if not is_head(h, 0):
                    w.gating(h - 1, 1 - e, 1, pair)
                w.turn(h, e, 1, 0)
                w.turn(h, e, 1, 1)
                w.tile(h + 1, 1 - e, 3)

            for h in (0, 1):
                w.turn_q(h, h)
                w.turn_k(h, h)
            w.split_v(0, 0)
            for p in range(4):
                w.tile(0, 0, p)
            scores_1(0, 0, None)
            scores_0(0, 0, None)
            with Fori(0, PAIRS - 2) as i:
                scores_1(2 * i + 1, 1, i)
                scores_0(2 * i + 1, 1, i)
                scores_1(2 * i + 2, 0, i)
                scores_0(2 * i + 2, 0, i)
            for h in (LAST - 2, LAST - 1):
                scores_1(h, h % 2, (h - 1) // 2)
                scores_0(h, h % 2, (h - 1) // 2, new_head=h + 2 < HEADS)
            scores_1(LAST, 1, PAIRS - 1)
            w.finish_tiles()
            w.gating(LAST - 1, 0, 1, PAIRS - 1)
            for j in (2, 3):
                w.turn(LAST, 1, 0, j)
                w.product(LAST, 1, 0, j - 2)
            w.product(LAST, 1, 0, 2)
            w.product(LAST, 1, 0, 3)
            w.output(LAST, 1, 0)
            w.turn(LAST, 1, 1, 0)
            w.turn(LAST, 1, 1, 1)
            for j in range(8):
                if j + 2 < 8:
                    w.turn(LAST, 1, 1, j + 2)
                w.product(LAST, 1, 1, j)
            w.output(LAST, 1, 1)
            w.gating(LAST, 1, 0, PAIRS - 1)
            w.gating(LAST, 1, 1, PAIRS - 1)

        class Idle:

            def turn_q(self, h, e): pass
            def turn_k(self, h, e): pass
            def split_v(self, h, e): pass
            def tile(self, h, e, p): pass
            def close(self, h, e): pass
            def finish_tiles(self): pass
            def turn(self, h, e, c, j): pass
            def product(self, h, e, c, j): pass
            def output(self, h, e, c): pass
            def gating(self, h, e, c, pair): pass

        def block_cols(c, j):
            return slice(max(0, j - 4 * c) * P, BANK)

        with nc.Block() as block:

            @block.sync
            def _(sp):
                parts = ((q_st, q_d, QKH), (k_st, k_d, QKH), (v_st, v_d, VH))

                def load(n, first):
                    dst, src, width = parts[n]
                    view = by_tile(src)
                    sp.dma_start(dst[:], view[:, :, bass.ds(first, 2 * width)]).then_inc(loaded["qkv"[n]], 16)

                sp.wait_ge(q_stored, 16)
                for k in range(NK):
                    sp.dma_start(w_next[:, k, :], w_out[k * P:(k + 1) * P, :]).then_inc(w_next_in, 16)
                with sp.Fori(1, PAIRS) as pair:
                    first = [sp.snap(pair * 2 * width) for _, _, width in parts]
                    sp.wait_ge(s_ready, 20 * pair - 14)
                    load(0, first[0])
                    load(1, first[1])
                    sp.wait_ge(v_low, 2 * pair)
                    load(2, first[2])

            @block.gpsimd
            def _(pool):
                class Pool(Idle):
                    def normalise(self, h, e, p):
                        pool.wait_ge(inv_done, 8 * h + p + 1)
                        i = TILES[p]
                        row = probs[i // 4][e][:, i % 4, :(i + 1) * P]
                        nc.gpsimd.tensor_tensor(row, row, inv[:, e, i:i + 1].to_broadcast([P, (i + 1) * P]),
                                                ALU.mult).then_inc(p_ready, 1)

                    def tile(self, h, e, p):
                        if not is_head(h, 0):
                            pool.wait_ge(gated, 2 * h + (-1, -1, -1, 0, 0, 0, 1, 1)[p])
                        if p >= 2:
                            self.normalise(h, e, p - 2)
                        elif p == 0 and not is_head(h, 0):
                            self.normalise(h - 1, 1 - e, 6)

                    def close(self, h, e):
                        self.normalise(h, e, 7)

                    def finish_tiles(self):
                        self.normalise(LAST, 1, 6)
                        self.normalise(LAST, 1, 7)

                    def split_v(self, h, e):
                        pool.wait_ge(v_high, h + 1)
                        hi, lo = e * VH, (1 - e) * VH
                        nc.gpsimd.tensor_tensor(v2[e][:, :, lo:lo + VH], v_st[:, :, rows(e)],
                                                f32(v2[e][:, :, hi:hi + VH]), ALU.subtract).then_inc(v_low, 1)

                    def gating(self, h, e, c, pair):
                        if is_head(h, LAST) or (is_head(h, LAST - 1) and c):
                            pool.wait_ge(p_ready, 8 * HEADS)
                        else:
                            pool.wait_ge(p_ready, 8 * h + (17 if c else 12))
                        pool.wait_ge(o_summed, 2 * h + c + 2)
                        whole = isinstance(pair, int)
                        g = gate[rows(e), pair if whole else bass.ds(pair, 1), c * BANK:(c + 1) * BANK]
                        o = o_sum[rows(e), c, :] if whole else o_sum[rows(e), c:c + 1, :]
                        nc.gpsimd.tensor_tensor(g, g, o, ALU.mult).then_inc(gated, 1)

                pool.sem_inc(gated, 2)
                walk(Pool(), pool.Fori)

            @block.scalar
            def _(act):
                class Act(Idle):
                    def turn_part(self, n, which, sl, at, e):
                        for c in range(2):
                            cols = slice(c * BANK, (c + 1) * BANK)
                            if c:
                                act.wait_ge(s_ready, at + 1)
                            else:
                                act.wait_ge(half_ready, n + 1)
                            nc.scalar.activation(t_hi[e][which][0:QKH, cols], s_ps[0:QKH, sl, cols], ACT.Copy,
                                                 scale=1.0 if which else gqk[0:QKH, 1:2]).then_inc(t_high, 1)

                    def turn_q(self, h, e):
                        self.turn_part(2 * h, 0, slot_q(h), ring_q(h), e)

                    def turn_k(self, h, e):
                        self.turn_part(2 * h + 1, 1, 1, ring_k(h), e)

                    def split_v(self, h, e):
                        act.wait_ge(loaded["v"], a_pair(h, e) * 16)
                        if not (is_head(h, 0) or is_head(h, 1)):
                            act.wait_ge(pv_done, 12 * h - 12)
                        nc.scalar.activation(v2[e][:, :, rows(e)], v_st[:, :, rows(e)], ACT.Copy).then_inc(v_high, 1)

                    def exponentials(self, h, e, p):
                        act.wait_ge(s_free, ring(h, p) + 3)
                        i = TILES[p]
                        row = probs[i // 4][e][:, i % 4, :(i + 1) * P]
                        nc.scalar.activation(row, row, ACT.Exp, bias=neg_max[:, e, i:i + 1], scale=-1.0,
                                             accum_out=total[:, e, i:i + 1]).then_inc(exp_done, 1)

                    def tile(self, h, e, p):
                        if p:
                            self.exponentials(h, e, p - 1)

                    def close(self, h, e):
                        self.exponentials(h, e, 7)

                    def finish_tiles(self):
                        self.exponentials(LAST, 1, 7)

                    def turn(self, h, e, c, j):
                        n, cols = 4 * c + j, block_cols(c, j)
                        act.wait_ge(pt_ready, 12 * h + n + 1)
                        nc.scalar.activation(pt_hi[:, n % 3, cols], pt_ps[:, n % 3, cols],
                                             ACT.Copy).then_inc(pt_high, 1)

                    def output(self, h, e, c):
                        act.wait_ge(pv_done, 12 * h + 4 + 8 * c)
                        nc.scalar.activation(o_part[rows(e), :], o_ps[rows(1 - e), :],
                                             ACT.Copy).then_inc(o_copied, 1)

                walk(Act(), act.Fori)

            @block.vector
            def _(dve):
                class Dve(Idle):
                    def turn_q(self, h, e):
                        for c in range(2):
                            cols = slice(c * BANK, (c + 1) * BANK)
                            dve.wait_ge(t_high, 4 * h + c + 1)
                            ins = nc.vector.scalar_tensor_tensor(
                                t_lo[e][0][0:QKH, cols], s_ps[0:QKH, slot_q(h), cols], gqk[0:QKH, 1:2],
                                f32(t_hi[e][0][0:QKH, cols]), ALU.mult, ALU.subtract)
                            if c == 0:
                                ins.then_inc(half_free, 1)
                        ins.then_inc(s_free, 1)

                    def turn_k(self, h, e):
                        for c in range(2):
                            cols = slice(c * BANK, (c + 1) * BANK)
                            dve.wait_ge(t_high, 4 * h + c + 3)
                            ins = nc.vector.tensor_tensor(t_lo[e][1][0:QKH, cols], s_ps[0:QKH, 1, cols],
                                                          f32(t_hi[e][1][0:QKH, cols]), ALU.subtract)
                            if c == 0:
                                ins.then_inc(half_free, 1)
                        ins.then_inc(s_free, 1)

                    def inverse(self, h, e, p, at=None):
                        dve.wait_ge(exp_done, 8 * h + p + 1)
                        if at is not None:
                            dve.wait_ge(s_ready, at + 1)
                        i = TILES[p]
                        nc.vector.reciprocal(inv[:, e, i:i + 1], total[:, e, i:i + 1]).then_inc(inv_done, 1)

                    def tile(self, h, e, p):
                        at = ring(h, p)
                        if is_head(h, 0) and p == 4:
                            dve.wait_ge(q_stored, 16)
                        if p >= 2:
                            self.inverse(h, e, p - 2, at)
                        elif p == 0 and not is_head(h, 0):
                            self.inverse(h - 1, 1 - e, 6, at)
                        else:
                            dve.wait_ge(s_ready, at + 1)
                            nc.vector.memset(carrier[:, 2 * e + p:2 * e + p + 1], 0.0)
                        i = TILES[p]
                        n = (i + 1) * P
                        nc.vector.tensor_tensor_reduce(probs[i // 4][e][:, i % 4, :n], scores(h, p, 0, n),
                                                       mask[:, S - n:], -SCALE, 3e38, ALU.add, ALU.min,
                                                       neg_max[:, e, i:i + 1]).then_inc(s_free, 1)

                    def close(self, h, e):
                        self.inverse(h, e, 7)

                    def finish_tiles(self):
                        self.inverse(LAST, 1, 6)
                        self.inverse(LAST, 1, 7)

                    def turn(self, h, e, c, j):
                        n, cols = 4 * c + j, block_cols(c, j)
                        dve.wait_ge(pt_high, 12 * h + n + 1)
                        nc.vector.tensor_tensor(pt_lo[:, n % 3, cols], pt_ps[:, n % 3, cols],
                                                f32(pt_hi[:, n % 3, cols]), ALU.subtract).then_inc(pt_low, 1)

                    def output(self, h, e, c):
                        dve.wait_ge(o_copied, 2 * h + c + 1)
                        dve.wait_ge(gated, 2 * h + c + 1)
                        nc.vector.tensor_tensor(o_sum[rows(e), c, :], o_ps[rows(e), :], o_part[rows(e), :],
                                                ALU.add).then_inc(o_summed, 1)

                dve.sem_inc(s_free, 2)
                dve.sem_inc(pt_low, 3)
                dve.sem_inc(o_summed, 1)
                walk(Dve(), dve.Fori)

            @block.tensor
            def _(pe):
                class Pe(Idle):
                    def transposes(self, n, stage, at, sl, h, e):
                        pe.wait_ge(loaded["qk"[n]], a_pair(h, e) * 16)
                        follows_q = n == 1 and not (is_head(h, 0) or is_head(h, 1))
                        if follows_q:
                            pe.wait_ge(half_free, 2 * h + 1)
                        else:
                            pe.wait_ge(s_free, at + 1)
                        for t in range(NT):
                            if follows_q and t == NT // 2:
                                pe.wait_ge(s_free, at + 1)
                            last = nc.tensor.transpose(s_ps[0:QKH, sl, t * P:(t + 1) * P],
                                                       stage[:, t, e * QKH:(e + 1) * QKH], ident[:])
                            if t == NT // 2 - 1:
                                last.then_inc(half_ready, 1)
                        last.then_inc(s_ready, 1)

                    def turn_q(self, h, e):
                        self.transposes(0, q_st, ring_q(h), slot_q(h), h, e)

                    def turn_k(self, h, e):
                        self.transposes(1, k_st, ring_k(h), 1, h, e)

                    def tile(self, h, e, p):
                        if p == 0:
                            pe.wait_ge(s_free, ring_k(h) + 3)
                        if p == 3 and not is_head(h, 0) and not is_head(h, LAST):
                            pe.wait_ge(half_free, 2 * h + 4)
                        else:
                            pe.wait_ge(s_free, ring(h, p) + (-1 if alone(h, p) else 1))
                        q_hi, q_lo = t_hi[e][0], t_lo[e][0]
                        k_hi, k_lo = t_hi[e][1], t_lo[e][1]
                        i = TILES[p]
                        qs = slice(i * P, (i + 1) * P)
                        for kc in range(i // 4 + 1):
                            ks = slice(kc * BANK, min((kc + 1) * BANK, (i + 1) * P))
                            last = three_passes(nc, scores(h, p, ks.start, ks.stop), q_hi[0:QKH, qs], q_lo[0:QKH, qs],
                                                k_hi[0:QKH, ks], k_lo[0:QKH, ks], True, True)
                        last.then_inc(s_ready, 1)

                    def turn(self, h, e, c, j):
                        n = 4 * c + j
                        pe.wait_ge(pt_low, 12 * h + n + 1)
                        for r in range(max(0, j - 4 * c), 4):
                            if j == 0:
                                pe.wait_ge(p_ready, 8 * h + (8 if c else r + 1))
                            last = nc.tensor.transpose(pt_ps[:, n % 3, r * P:(r + 1) * P],
                                                       probs[c][e][:, r, j * P:(j + 1) * P], ident[:])
                        last.then_inc(pt_ready, 1)

                    def product(self, h, e, c, j):
                        n, cols = 4 * c + j, block_cols(c, j)
                        pe.wait_ge(pt_low, 12 * h + n + 4)
                        if j == 0:
                            pe.wait_ge(v_low, h + 1)
                            pe.wait_ge(o_summed, 2 * h + c + 1)
                        nc.tensor.matmul(o_ps[:, cols], v2[e][:, j, :], pt_hi[:, n % 3, cols],
                                         start=(j == 0), stop=False)
                        nc.tensor.matmul(o_ps[:, cols], v2[e][:, j, :], pt_lo[:, n % 3, cols], start=False,
                                         stop=(j == 4 * c + 3)).then_inc(pv_done, 1)

                walk(Pe(), pe.Fori)


def a_pair(h, e):
    return (h - e + 2) // 2


def hybrid_trunk(nc, x, positions, norm_ab, w_in_ab, pool_w, pool_scale, conv_w, w_out_ab, norm_c, w_in_c,
                 q_lat_norm, w_uq, kv_lat_norm, w_ukv, q_head_norm, k_head_norm, w_out_c, out):
    x1_d = nc.dram_tensor("x1_scratch", [S, D], F32, kind="Internal").ap()
    q_d = nc.dram_tensor("q_scratch", [S, Q_COLS], F32, kind="Internal").ap()
    k_d = nc.dram_tensor("k_scratch", [S, Q_COLS], F32, kind="Internal").ap()
    v_d = nc.dram_tensor("v_scratch", [S, HEADS * VH], F32, kind="Internal").ap()
    with ExitStack() as keep:
        def sb(n, shape, dt=F32, ctx=keep):
            return ctx.enter_context(nc.sbuf_tensor(n, shape, dt))

        ident = sb("ident", [P, P])
        mask = sb("mask", [P, S])
        gqk = sb("gqk", [P, 2])
        rms_qkv = sb("rms_qkv", [P, 2, NT])
        k_rope_ss = sb("k_rope_ss", [P, NT])
        k_rope = sb("k_rope", [P, NT, ROPE])
        q_tab = sb("q_tab", [P, 4, NT, HALF])
        BIG = NK * S * 4
        base = -(-nc.sbuf_base // 32) * 32
        sb("arena01", [P, 2, NK, S])
        w_out0_in = keep.enter_context(nc.semaphore("w_out0_in"))
        w_out1_in = keep.enter_context(nc.semaphore("w_out1_in"))

        def big(n, name, dt=F32):
            return nc.alloc_sbuf_tensor_at(name, [P, NK, S], dt, offset=base + n * BIG)

        q_stored = keep.enter_context(nc.semaphore("q_stored"))
        loaded = {name: keep.enter_context(nc.semaphore(f"loaded_{name}")) for name in "qkv"}
        w_kv_in = keep.enter_context(nc.semaphore("w_kv_in"))
        with ExitStack() as layers:
            sb("arena23", [P, 2, NK, S], F32, layers)
            w_out0, w_out0_lo = big(0, "w_out0"), big(0, "w_out0_lo", F32R)
            features, act1_lo = big(2, "features"), big(2, "act1_lo", F32R)
            act1_hi = big(3, "act1_hi", F32R)
            mixers(nc, x[0], norm_ab, w_in_ab[0], pool_w[0], pool_scale[0], conv_w[0], ident, mask,
                   big(1, "act0_hi", F32R), big(3, "act0_lo", F32R), features, w_out_ab[0], w_out0, w_out0_in)
            lat_weights = Weights(nc, layers, "lat")
            lat_ps = layers.enter_context(nc.psum_tensor("lat_proj", [P, 2, S], F32))
            output_projection(nc, "out0", features, x[0], x1_d, w_out0, big(1, "w_out0_hi", F32R), w_out0_lo,
                              w_out0_in, (norm_c, ident, act1_hi, act1_lo), (w_in_c[0], lat_weights, lat_ps))
            latent, gate = big(1, "latent"), big(0, "gate")
            w_kv_at = -(-nc.sbuf_base // 32) * 32
            sb("kv_place_early", [P, KKV, KV_COLS], F32, layers)
            w_kv = nc.alloc_sbuf_tensor_at("w_kv", [P, KKV, KV_COLS], F32, offset=w_kv_at)
            w_kv_lo = nc.alloc_sbuf_tensor_at("w_kv_lo", [P, KKV, KV_COLS], F32R, offset=w_kv_at)
            latent_projection(nc, w_in_c[0], positions[0], q_lat_norm[0], kv_lat_norm[0], q_head_norm,
                              k_head_norm, ident, act1_hi, act1_lo, latent, gate, rms_qkv, q_tab, k_rope,
                              k_rope_ss, lat_weights, lat_ps, w_ukv[0], w_kv, w_kv_in)
        st_at = -(-nc.sbuf_base // 32) * 32
        stages = {name: nc.alloc_sbuf_tensor_at(f"{name}_st", [P, NT, 2 * w], F32, offset=st_at + n * NT * 2 * QKH * 4)
                  for n, (name, w) in enumerate((("q", QKH), ("k", QKH), ("v", VH)))}
        head_projections(nc, w_kv, w_kv_lo, w_kv_at, w_kv_in, w_uq[0], latent, rms_qkv, q_tab, k_rope, k_rope_ss,
                         q_head_norm, k_head_norm, gqk, q_d, k_d, v_d, q_stored, stages, loaded)
        w_out1 = big(1, "w_out1")
        attention(nc, q_d, k_d, v_d, q_stored, gqk, stages, loaded, ident, mask, gate, w_out_c[0], w_out1, w_out1_in)
        with nc.sbuf_tensor("w_out1_hi", [P, NK, D], F32R) as w_hi:
            output_projection(nc, "out1", gate, x1_d, out[0], w_out1, w_hi, big(1, "w_out1_lo", F32R), w_out1_in)


INPUTS = ["x", "positions", "norm_ab", "w_in_ab", "pool_w", "pool_scale", "conv_w", "w_out_ab", "norm_c",
          "w_in_c", "q_lat_norm", "w_uq", "kv_lat_norm", "w_ukv", "q_head_norm", "k_head_norm", "w_out_c"]


def kernel(**inputs):
    import concourse.bacc as bacc
    from concourse.bass_utils import run_bass_kernel_spmd

    nc = bacc.Bacc("TRN2", target_bir_lowering=False, num_devices=1)
    arrays, args = {}, []
    for name in INPUTS:
        a = np.ascontiguousarray(inputs[name])
        arrays[f"in_{name}"] = a
        args.append(nc.dram_tensor(f"in_{name}", a.shape, mybir.dt.from_np(a.dtype), kind="ExternalInput").ap())
    out = nc.dram_tensor("out_x", (1, S, D), F32, kind="ExternalOutput").ap()
    hybrid_trunk(nc, *args, out)
    result = run_bass_kernel_spmd(nc, [arrays], core_ids=[0])
    return result.results[0]["out_x"]
```
